# Optimizing a Trainium2 kernel written in Bass

```python
import jax, jax.numpy as jnp
from jax import lax
import numpy as np
import jax
import jax.numpy as jnp

D_MODEL = 1024
BATCH = 1
SEQ = 256
DEPTH = 2

N_HEADS = 16
HEAD_DIM = D_MODEL // N_HEADS
N_MIXERS = 2
GRID_W = 64
NA_ROWS = 8
NA_COLS = 16
DIL_GROUPS = ((128, 1), (512, 4), (2048, 16))
N_GROUPS = len(DIL_GROUPS)
BAND_BLOCK = 128
D_FF = -(-8 * D_MODEL // (3 * 256)) * 256
RMS_EPS = 1e-6
NEG_INF = -1e30
N_A_LAYERS = (DEPTH + 1) // 2
N_B_LAYERS = DEPTH // 2


def rms_norm(x, g):
    xf = x.astype(jnp.float32)
    y = xf * lax.rsqrt(jnp.mean(xf * xf, axis=-1, keepdims=True) + RMS_EPS)
    return (y * g.astype(jnp.float32)).astype(x.dtype)

def alibi_slopes(n):
    return 2.0 ** (-8.0 * jnp.arange(1, n + 1, dtype=jnp.float32) / n)

def swiglu(x, w_gate, w_up, w_down):
    return (jax.nn.silu(x @ w_gate) * (x @ w_up)) @ w_down

def neighbourhood_attention(x, w_qkv, w_o, rpb):
    b, s, _ = x.shape
    rows = s // GRID_W
    kh = min(NA_ROWS, rows)
    qkv = (x @ w_qkv).reshape(b, rows, GRID_W, 3, N_HEADS, HEAD_DIM)
    q, k, v = (jnp.transpose(qkv[:, :, :, i], (0, 3, 1, 2, 4)) for i in range(3))
    q = q * HEAD_DIM ** -0.5
    col = jnp.arange(GRID_W)
    col_start = jnp.clip(col - NA_COLS // 2, 0, GRID_W - NA_COLS)
    col_mask = (col[None, :] >= col_start[:, None]) & (col[None, :] < col_start[:, None] + NA_COLS)
    col_idx = jnp.clip(col[None, :] - col[:, None] + NA_COLS - 1, 0, 2 * NA_COLS - 2)
    rpb_cols = rpb.astype(jnp.float32)[:, :, col_idx]

    def row_block(i):
        rs = jnp.clip(i - kh // 2, 0, rows - kh)
        qi = lax.dynamic_index_in_dim(q, i, axis=2, keepdims=False)
        kr = lax.dynamic_slice_in_dim(k, rs, kh, axis=2)
        vr = lax.dynamic_slice_in_dim(v, rs, kh, axis=2)
        bias = lax.dynamic_slice_in_dim(rpb_cols, rs - i + NA_ROWS - 1, kh, axis=1)
        sc = jnp.einsum('bhqd,bhrkd->bhqrk', qi, kr).astype(jnp.float32)
        sc = sc + jnp.transpose(bias, (0, 2, 1, 3))[None]
        sc = jnp.where(col_mask[:, None, :], sc, NEG_INF)
        p = jax.nn.softmax(sc.reshape(b, N_HEADS, GRID_W, kh * GRID_W), axis=-1).reshape(sc.shape)
        return jnp.einsum('bhqrk,bhrkd->bhqd', p.astype(vr.dtype), vr)

    o = lax.map(row_block, jnp.arange(rows))
    o = jnp.transpose(o, (1, 0, 3, 2, 4)).reshape(b, s, D_MODEL)
    return o @ w_o

def banded_attention(q, k, v, radius, slope_dist):
    n, h, l, dh = q.shape
    nb = -(-l // BAND_BLOCK)
    lp = nb * BAND_BLOCK
    qb = jnp.pad(q, ((0, 0), (0, 0), (0, lp - l), (0, 0))).reshape(n, h, nb, BAND_BLOCK, dh)

    def key_blocks(t):
        tp = jnp.pad(t, ((0, 0), (0, 0), (radius, lp - l + BAND_BLOCK - radius), (0, 0)))
        tp = tp.reshape(n, h, nb + 1, BAND_BLOCK, dh)
        return jnp.concatenate([tp[:, :, :-1], tp[:, :, 1:]], axis=3)

    kb, vb = key_blocks(k), key_blocks(v)
    qi = jnp.arange(lp).reshape(nb, BAND_BLOCK)
    kj = jnp.arange(nb)[:, None] * BAND_BLOCK - radius + jnp.arange(2 * BAND_BLOCK)[None, :]
    dist = jnp.abs(qi[:, :, None] - kj[:, None, :])
    valid = (dist <= radius) & (kj[:, None, :] >= 0) & (kj[:, None, :] < l)
    sc = jnp.einsum('nhbqd,nhbkd->nhbqk', qb, kb).astype(jnp.float32)
    sc = sc - slope_dist[None, :, None, None, None] * dist.astype(jnp.float32)
    sc = jnp.where(valid, sc, NEG_INF)
    lse = jax.nn.logsumexp(sc, axis=-1)
    p = jnp.exp(sc - lse[..., None])
    o = jnp.einsum('nhbqk,nhbkd->nhbqd', p.astype(vb.dtype), vb)
    return o.reshape(n, h, lp, dh)[:, :, :l], lse.reshape(n, h, lp)[:, :, :l]

def dilated_attention(x, w_qkv, w_o):
    b, s, _ = x.shape
    qkv = (x @ w_qkv).reshape(b, s, N_GROUPS, 3, N_HEADS, HEAD_DIM)
    slopes = alibi_slopes(N_HEADS)
    outs, lses = [], []
    for g, (window, dil) in enumerate(DIL_GROUPS):
        radius = window // (2 * dil)
        l = s // dil

        def to_sub(t):
            t = jnp.transpose(t.reshape(b, l, dil, N_HEADS, HEAD_DIM), (0, 2, 3, 1, 4))
            return t.reshape(b * dil, N_HEADS, l, HEAD_DIM)

        q, k, v = (to_sub(qkv[:, :, g, i]) for i in range(3))
        o, lse = banded_attention(q * HEAD_DIM ** -0.5, k, v, radius, slopes * dil)
        o = jnp.transpose(o.reshape(b, dil, N_HEADS, l, HEAD_DIM), (0, 3, 1, 2, 4)).reshape(b, s, N_HEADS, HEAD_DIM)
        lse = jnp.transpose(lse.reshape(b, dil, N_HEADS, l), (0, 3, 1, 2)).reshape(b, s, N_HEADS)
        outs.append(o)
        lses.append(lse)
    alpha = jax.nn.softmax(jnp.stack(lses, axis=0), axis=0)
    o = jnp.einsum('gbsh,gbshd->bshd', alpha, jnp.stack(outs, axis=0).astype(jnp.float32)).astype(x.dtype)
    return o.reshape(b, s, D_MODEL) @ w_o

def first_inputs(seed: int = 0) -> dict:
    key = jax.random.key(seed)
    ks = jax.random.split(key, 14)
    d = D_MODEL

    def w(k, shape, fan_in):
        return jax.random.normal(k, shape, jnp.float32) * fan_in ** -0.5

    def gain(k):
        return 1.0 + 0.02 * jax.random.normal(k, (DEPTH, d), jnp.float32)

    return {
        "x": jax.random.normal(ks[0], (BATCH, SEQ, d), jnp.float32),
        "norm_mix_pre": gain(ks[1]),
        "norm_mix_post": gain(ks[2]),
        "norm_ffn_pre": gain(ks[3]),
        "norm_ffn_post": gain(ks[4]),
        "na_w_qkv": w(ks[5], (N_A_LAYERS, d, 3 * d), d),
        "na_w_o": w(ks[6], (N_A_LAYERS, d, d), d),
        "na_rpb": 0.5 * jax.random.normal(ks[7], (N_A_LAYERS, N_HEADS, 2 * NA_ROWS - 1, 2 * NA_COLS - 1), jnp.float32),
        "dil_w_qkv": w(ks[8], (N_B_LAYERS, d, N_GROUPS * 3 * d), d),
        "dil_w_o": w(ks[9], (N_B_LAYERS, d, d), d),
        "ffn_w_gate": w(ks[10], (DEPTH, d, D_FF), d),
        "ffn_w_up": w(ks[11], (DEPTH, d, D_FF), d),
        "ffn_w_down": w(ks[12], (DEPTH, D_FF, d), D_FF),
    }

def first_block(x, norm_mix_pre, norm_mix_post, norm_ffn_pre, norm_ffn_post, na_w_qkv, na_w_o, na_rpb,
              dil_w_qkv, dil_w_o, ffn_w_gate, ffn_w_up, ffn_w_down):
    for layer in range(DEPTH):
        j = layer // N_MIXERS
        h = rms_norm(x, norm_mix_pre[layer])
        if layer % N_MIXERS == 0:
            h = neighbourhood_attention(h, na_w_qkv[j], na_w_o[j], na_rpb[j])
        else:
            h = dilated_attention(h, dil_w_qkv[j], dil_w_o[j])
        x = x + rms_norm(h, norm_mix_post[layer])
        h = rms_norm(x, norm_ffn_pre[layer])
        x = x + rms_norm(swiglu(h, ffn_w_gate[layer], ffn_w_up[layer], ffn_w_down[layer]), norm_ffn_post[layer])
    return x


DEPTH_2 = 1

CTX_LEN = 256
N_MOD = 6
ADA_SCALE = 0.5
LN_EPS = 1e-5
DN_ALPHA = (2 * DEPTH_2) ** 0.25
DN_BETA = (8 * DEPTH_2) ** -0.25

SSD_HEADS = 8
SSD_HEAD_DIM = 64
SSD_INNER = SSD_HEADS * SSD_HEAD_DIM
SSD_GROUPS = 2
SSD_STATE = 128
SSD_CONV = 3
SSD_CHUNK = 128
SSD_XBC = SSD_INNER + 2 * SSD_GROUPS * SSD_STATE

RWKV_HEADS = 4
RWKV_HEAD_DIM = 64
RWKV_WIDTH = RWKV_HEADS * RWKV_HEAD_DIM
RWKV_DECAY_LORA = 64
RWKV_ICLR_LORA = 64
RWKV_GATE_LORA = 128
RWKV_COLS = 3 * RWKV_WIDTH + 2 * RWKV_DECAY_LORA + 2 * RWKV_ICLR_LORA + RWKV_GATE_LORA
RWKV_LNX_EPS = 64e-5

GLA_HEADS = 4
GLA_KEY_DIM = 32
GLA_VAL_DIM = 64
GLA_K_WIDTH = GLA_HEADS * GLA_KEY_DIM
GLA_V_WIDTH = GLA_HEADS * GLA_VAL_DIM
GLA_GATE_LORA = 16
GLA_GATE_NORMALIZER = 16.0
GLA_CHUNK = 16

MIX_WIDTH = SSD_INNER + RWKV_WIDTH + GLA_V_WIDTH
IN_WIDTHS = (SSD_INNER, SSD_XBC, 2 * SSD_HEADS, RWKV_COLS, GLA_K_WIDTH, GLA_K_WIDTH, GLA_V_WIDTH, 2 * GLA_GATE_LORA, GLA_V_WIDTH)
N_IN = SSD_INNER + SSD_XBC + 2 * SSD_HEADS + RWKV_COLS + 2 * GLA_K_WIDTH + 2 * GLA_V_WIDTH + 2 * GLA_GATE_LORA

N_EXPERTS = 64
TOP_K = 8
N_GROUPS_2 = 8
TOPK_GROUPS = 4
EXPERT_DIM = 256
SHARED_DIM = 256
ROUTED_SCALE = 2.5
MOE_BLOCK = 128


def _split(z, widths):
    return jnp.split(z, [int(i) for i in np.cumsum(widths)[:-1]], axis=-1)

def _layernorm(x, w=None, b=None, eps=LN_EPS):
    xf = x.astype(jnp.float32)
    mu = jnp.mean(xf, -1, keepdims=True)
    var = jnp.mean(jnp.square(xf - mu), -1, keepdims=True)
    y = (xf - mu) * lax.rsqrt(var + eps)
    if w is not None:
        y = y * w.astype(jnp.float32) + b.astype(jnp.float32)
    return y.astype(x.dtype)

def _rmsnorm_groups(x, w, group, eps=1e-5):
    xf = x.astype(jnp.float32)
    shp = xf.shape
    g = xf.reshape(shp[:-1] + (shp[-1] // group, group))
    g = g * lax.rsqrt(jnp.mean(g * g, -1, keepdims=True) + eps)
    return (g.reshape(shp) * w.astype(jnp.float32)).astype(x.dtype)

def _seg_flip(z, n_ctx):
    return jnp.concatenate([jnp.flip(z[:, :n_ctx], 1), jnp.flip(z[:, n_ctx:], 1)], axis=1)

def _dwconv_centred(z, w, b):
    ch = z.shape[-1]
    pad = (SSD_CONV - 1) // 2
    y = lax.conv_general_dilated(z, w[:, None, :].astype(z.dtype), window_strides=(1,), padding=[(pad, pad)],
                                 dimension_numbers=('NWC', 'WIO', 'NWC'), feature_group_count=ch)
    return y + b

def _seq_shift_mix(z, mu_prev, mu_next):
    prev = jnp.pad(z, ((0, 0), (1, 0), (0, 0)))[:, :-1]
    nxt = jnp.pad(z, ((0, 0), (0, 1), (0, 0)))[:, 1:]
    return z + mu_prev * (prev - z) + mu_next * (nxt - z)

def _grid_shift_mix(z, mu):
    b, s, ch = z.shape
    rows = s // GRID_W
    g = z.reshape(b, rows, GRID_W, ch)
    left = jnp.pad(g, ((0, 0), (0, 0), (1, 0), (0, 0)))[:, :, :-1]
    right = jnp.pad(g, ((0, 0), (0, 0), (0, 1), (0, 0)))[:, :, 1:]
    up = jnp.pad(g, ((0, 0), (1, 0), (0, 0), (0, 0)))[:, :-1]
    down = jnp.pad(g, ((0, 0), (0, 1), (0, 0), (0, 0)))[:, 1:]
    out = g + mu[0] * (left - g) + mu[1] * (right - g) + mu[2] * (up - g) + mu[3] * (down - g)
    return out.reshape(b, s, ch)

def _ssd_chunked(x, dt, log_a, bm, cm):
    n, t, h, p = x.shape
    g, ds = bm.shape[2], bm.shape[3]
    q = SSD_CHUNK
    nc = t // q
    rep = h // g
    b_h = jnp.repeat(bm, rep, axis=2).reshape(n, nc, q, h, ds)
    c_h = jnp.repeat(cm, rep, axis=2).reshape(n, nc, q, h, ds)
    xdt = (x * dt[..., None]).reshape(n, nc, q, h, p)
    acs = jnp.cumsum(log_a.reshape(n, nc, q, h), axis=2)
    acs_h = jnp.moveaxis(acs, 3, 1)
    tril = jnp.tril(jnp.ones((q, q), dtype=bool))
    seg = acs_h[..., :, None] - acs_h[..., None, :]
    lmat = jnp.exp(jnp.where(tril, seg, -jnp.inf))
    scores = jnp.einsum('nclhd,ncshd->nhcls', c_h, b_h) * lmat
    y_diag = jnp.einsum('nhcls,ncshp->nclhp', scores, xdt)
    decay_end = jnp.exp(acs[:, :, -1:, :] - acs)
    states = jnp.einsum('nclhd,nclh,nclhp->nchpd', b_h, decay_end, xdt)
    chunk_decay = jnp.exp(acs[:, :, -1, :])

    def step(hprev, inp):
        st, dec = inp
        return hprev * dec[..., None, None] + st, hprev

    h0 = jnp.zeros((n, h, p, ds), x.dtype)
    _, h_in = lax.scan(step, h0, (jnp.moveaxis(states, 1, 0), jnp.moveaxis(chunk_decay, 1, 0)))
    h_in = jnp.moveaxis(h_in, 0, 1)
    y_off = jnp.einsum('nclhd,nchpd,nclh->nclhp', c_h, h_in, jnp.exp(acs))
    return (y_diag + y_off).reshape(n, t, h, p)

def _rwkv7_scan(r, w, k, v, kk, a):
    n, t, h, dk = r.shape

    def step(S, inp):
        r_t, w_t, k_t, v_t, kk_t, a_t = inp
        sa = -jnp.einsum('nhvk,nhk->nhv', S, kk_t)
        S = S * w_t[:, :, None, :] + sa[..., None] * (kk_t * a_t)[:, :, None, :] + v_t[..., None] * k_t[:, :, None, :]
        return S, jnp.einsum('nhvk,nhk->nhv', S, r_t)

    S0 = jnp.zeros((n, h, dk, dk), r.dtype)
    xs = (jnp.moveaxis(r, 1, 0), jnp.moveaxis(w, 1, 0), jnp.moveaxis(k, 1, 0),
          jnp.moveaxis(v, 1, 0), jnp.moveaxis(kk, 1, 0), jnp.moveaxis(a, 1, 0))
    _, y = lax.scan(step, S0, xs)
    return jnp.moveaxis(y, 0, 1)

def _gla_chunked(q, k, v, log_a):
    n, t, h, dk = q.shape
    dv = v.shape[-1]
    c = GLA_CHUNK
    nc = t // c
    q = q.reshape(n, nc, c, h, dk)
    k = k.reshape(n, nc, c, h, dk)
    v = v.reshape(n, nc, c, h, dv)
    acs = jnp.cumsum(log_a.reshape(n, nc, c, h, dk), axis=2)
    tril = jnp.tril(jnp.ones((c, c), dtype=bool))[:, :, None, None]
    seg = acs[:, :, :, None] - acs[:, :, None, :]
    decay = jnp.exp(jnp.where(tril, seg, -jnp.inf))
    scores = jnp.einsum('ncihd,ncjhd,ncijhd->nchij', q, k, decay)
    o_intra = jnp.einsum('nchij,ncjhv->ncihv', scores, v)
    q_dec = q * jnp.exp(acs)
    k_dec = k * jnp.exp(acs[:, :, -1:] - acs)
    states = jnp.einsum('ncjhd,ncjhv->nchdv', k_dec, v)
    chunk_decay = jnp.exp(acs[:, :, -1])

    def step(S, inp):
        st, dec = inp
        return S * dec[..., None] + st, S

    S0 = jnp.zeros((n, h, dk, dv), q.dtype)
    _, s_in = lax.scan(step, S0, (jnp.moveaxis(states, 1, 0), jnp.moveaxis(chunk_decay, 1, 0)))
    s_in = jnp.moveaxis(s_in, 0, 1)
    o_inter = jnp.einsum('ncihd,nchdv->ncihv', q_dec, s_in)
    return (o_intra + o_inter).reshape(n, t, h, dv)

def _token_mixer(u, n_ctx, w_in, ssd_conv_w, ssd_conv_b, ssd_dt_bias, ssd_a_log, ssd_d, ssd_norm_w,
                 rwkv_mu, rwkv_w0, rwkv_w2, rwkv_a0, rwkv_a2, rwkv_g2, rwkv_kk, rwkv_ka, rwkv_rk,
                 rwkv_lnx_w, rwkv_lnx_b, gla_gu, gla_gb, gla_norm_w, w_out):
    f32 = jnp.float32
    bsz, t, _ = u.shape
    flip = lambda zz: _seg_flip(zz, n_ctx)

    def both(fwd, bwd):
        s = jnp.stack([fwd, flip(bwd)])
        return s.reshape((2 * bsz,) + s.shape[2:])

    def unboth(y):
        y = y.reshape((2, bsz) + y.shape[1:])
        return y[0] + flip(y[1])

    z, xbc, dt, rw, gq, gk, gv, gd, og = _split(u @ w_in, IN_WIDTHS)

    xbc = jax.nn.silu(jnp.concatenate([_dwconv_centred(xbc[:, :n_ctx], ssd_conv_w, ssd_conv_b),
                                       _dwconv_centred(xbc[:, n_ctx:], ssd_conv_w, ssd_conv_b)], axis=1))
    xs, bm, cm = _split(xbc.astype(f32), (SSD_INNER, SSD_GROUPS * SSD_STATE, SSD_GROUPS * SSD_STATE))
    xs = xs.reshape(bsz, t, SSD_HEADS, SSD_HEAD_DIM)
    bm = bm.reshape(bsz, t, SSD_GROUPS, SSD_STATE)
    cm = cm.reshape(bsz, t, SSD_GROUPS, SSD_STATE)
    dt = jax.nn.softplus(dt.astype(f32).reshape(bsz, t, 2, SSD_HEADS) + ssd_dt_bias.astype(f32))
    neg_a = -jnp.exp(ssd_a_log.astype(f32))
    dt_f, dt_b = dt[:, :, 0], dt[:, :, 1]
    y = unboth(_ssd_chunked(both(xs, xs), both(dt_f, dt_b), both(dt_f * neg_a[0], dt_b * neg_a[1]),
                            both(bm, bm), both(cm, cm)))
    y = y + ssd_d.astype(f32)[:, None] * xs
    y_ssd = _rmsnorm_groups(y.reshape(bsz, t, SSD_INNER) * jax.nn.silu(z.astype(f32)), ssd_norm_w,
                            SSD_INNER // SSD_GROUPS)

    rw = jnp.concatenate([_seq_shift_mix(rw[:, :n_ctx], rwkv_mu[0], rwkv_mu[1]),
                          _grid_shift_mix(rw[:, n_ctx:], rwkv_mu)], axis=1)
    r, k, v, wd_f, wd_b, ad_f, ad_b, gd_r = _split(
        rw.astype(f32), (RWKV_WIDTH,) * 3 + (RWKV_DECAY_LORA,) * 2 + (RWKV_ICLR_LORA,) * 2 + (RWKV_GATE_LORA,))
    hd = lambda zz: zz.reshape(bsz, t, RWKV_HEADS, RWKV_HEAD_DIM)
    decay = lambda wd, i: jnp.exp(-jnp.exp(-jax.nn.softplus(-(rwkv_w0[i] + jnp.tanh(wd) @ rwkv_w2[i])) - 0.5))
    iclr = lambda ad, i: jax.nn.sigmoid(rwkv_a0[i] + ad @ rwkv_a2[i])
    w_f, w_b = hd(decay(wd_f, 0)), hd(decay(wd_b, 1))
    a_f, a_b = hd(iclr(ad_f, 0)), hd(iclr(ad_b, 1))
    r, k, v = hd(r), hd(k), hd(v)
    kk = k * rwkv_kk.reshape(RWKV_HEADS, RWKV_HEAD_DIM)
    kk = kk / jnp.maximum(jnp.sqrt(jnp.sum(kk * kk, -1, keepdims=True)), 1e-12)
    ka = rwkv_ka.reshape(RWKV_HEADS, RWKV_HEAD_DIM)
    k_f = k * (1.0 + (a_f - 1.0) * ka)
    k_b = k * (1.0 + (a_b - 1.0) * ka)
    y = unboth(_rwkv7_scan(both(r, r), both(w_f, w_b), both(k_f, k_b), both(v, v), both(kk, kk), both(a_f, a_b)))
    mu = jnp.mean(y, -1, keepdims=True)
    var = jnp.mean(jnp.square(y - mu), -1, keepdims=True)
    y = ((y - mu) * lax.rsqrt(var + RWKV_LNX_EPS)).reshape(bsz, t, RWKV_WIDTH) * rwkv_lnx_w + rwkv_lnx_b
    bonus = (jnp.sum(r * (k_f + k_b) * rwkv_rk, -1, keepdims=True) * v).reshape(bsz, t, RWKV_WIDTH)
    y_rwkv = (y + bonus) * (jax.nn.sigmoid(gd_r) @ rwkv_g2)

    gh = lambda zz, d: zz.reshape(bsz, t, GLA_HEADS, d)
    q = gh(gq.astype(f32), GLA_KEY_DIM) * GLA_KEY_DIM ** -0.5
    kg = gh(gk.astype(f32), GLA_KEY_DIM)
    vg = gh(gv.astype(f32), GLA_VAL_DIM)
    gd_f, gd_b = _split(gd.astype(f32), (GLA_GATE_LORA, GLA_GATE_LORA))
    la = lambda gg, i: gh(jax.nn.log_sigmoid(gg @ gla_gu[i] + gla_gb[i]) / GLA_GATE_NORMALIZER, GLA_KEY_DIM)
    o = unboth(_gla_chunked(both(q, q), both(kg, kg), both(vg, vg), both(la(gd_f, 0), la(gd_b, 1))))
    y_gla = _rmsnorm_groups(o.reshape(bsz, t, GLA_V_WIDTH), gla_norm_w, GLA_VAL_DIM) * jax.nn.silu(og.astype(f32))

    y_mix = jnp.concatenate([y_ssd, y_rwkv, y_gla], axis=-1).astype(u.dtype)
    return y_mix @ w_out

def _moe_ffn(h, router_w, router_b, w1, w3, w2, sw1, sw3, sw2):
    f32 = jnp.float32
    t = h.shape[0]
    per_group = N_EXPERTS // N_GROUPS_2
    scores = jax.nn.sigmoid((h @ router_w).astype(f32))
    sel = scores + router_b.astype(f32)
    grp_score = lax.top_k(sel.reshape(t, N_GROUPS_2, per_group), 2)[0].sum(-1)
    _, top_g = lax.top_k(grp_score, TOPK_GROUPS)
    gmask = jax.nn.one_hot(top_g, N_GROUPS_2, dtype=f32).sum(1) > 0
    sel = jnp.where(jnp.repeat(gmask, per_group, axis=1), sel, -jnp.inf)
    _, idx = lax.top_k(sel, TOP_K)
    wts = jnp.take_along_axis(scores, idx, axis=1)
    wts = wts / jnp.sum(wts, -1, keepdims=True) * ROUTED_SCALE

    n_assign = t * TOP_K
    flat_e = idx.reshape(-1)
    order = jnp.argsort(flat_e)
    sorted_e = flat_e[order]
    counts = jnp.bincount(flat_e, length=N_EXPERTS)
    padded = (counts + MOE_BLOCK - 1) // MOE_BLOCK * MOE_BLOCK
    pend = jnp.cumsum(padded)
    pstart = pend - padded
    sstart = jnp.cumsum(counts) - counts
    dest = pstart[sorted_e] + jnp.arange(n_assign, dtype=jnp.int32) - sstart[sorted_e]
    n_rows = -(-n_assign // MOE_BLOCK) * MOE_BLOCK + N_EXPERTS * MOE_BLOCK
    n_blocks = n_rows // MOE_BLOCK
    row_tok = jnp.zeros((n_rows,), jnp.int32).at[dest].set((order // TOP_K).astype(jnp.int32))
    row_w = jnp.zeros((n_rows,), f32).at[dest].set(wts.reshape(-1)[order])
    block_e = jnp.minimum(jnp.searchsorted(pend, jnp.arange(n_blocks, dtype=jnp.int32) * MOE_BLOCK, side='right'),
                          N_EXPERTS - 1)

    def body(acc, blk):
        tok, wt, e = blk
        xb = h[tok]
        hid = jax.nn.silu(xb @ w1[e]) * (xb @ w3[e])
        return acc.at[tok].add(wt[:, None] * (hid @ w2[e]).astype(f32)), None

    routed, _ = lax.scan(body, jnp.zeros(h.shape, f32),
                         (row_tok.reshape(n_blocks, MOE_BLOCK), row_w.reshape(n_blocks, MOE_BLOCK), block_e))
    shared = (jax.nn.silu(h @ sw1) * (h @ sw3)) @ sw2
    return routed.astype(h.dtype) + shared

def second_inputs(seed: int = 0) -> dict:
    key = jax.random.key(seed)
    ks = jax.random.split(key, 40)
    L, D, E, F, Fs = DEPTH_2, D_MODEL, N_EXPERTS, EXPERT_DIM, SHARED_DIM
    nrm = lambda k, shape, s: jax.random.normal(k, shape, jnp.float32) * s
    one = lambda k, shape: 1.0 + 0.1 * jax.random.normal(k, shape, jnp.float32)
    dt0 = jnp.exp(jax.random.uniform(ks[9], (L, 2, SSD_HEADS), jnp.float32, np.log(1e-3), np.log(1e-1)))
    return {
        'x': nrm(ks[0], (BATCH, SEQ, D), 1.0),
        'c': nrm(ks[1], (BATCH, D), 1.0),
        'ctx': nrm(ks[2], (BATCH, CTX_LEN, D), 1.0),
        'c_ctx': nrm(ks[3], (D,), 1.0),
        'ada_w': nrm(ks[4], (L, D, N_MOD * D), D ** -0.5 * ADA_SCALE),
        'ada_b': nrm(ks[5], (L, N_MOD * D), 0.02),
        'w_in': nrm(ks[6], (L, D, N_IN), D ** -0.5),
        'ssd_conv_w': nrm(ks[7], (L, SSD_CONV, SSD_XBC), SSD_CONV ** -0.5),
        'ssd_conv_b': nrm(ks[8], (L, SSD_XBC), 0.02),
        'ssd_dt_bias': dt0 + jnp.log(-jnp.expm1(-dt0)),
        'ssd_a_log': jnp.log(jax.random.uniform(ks[10], (L, 2, SSD_HEADS), jnp.float32, 1.0, 16.0)),
        'ssd_d': one(ks[11], (L, SSD_HEADS)),
        'ssd_norm_w': one(ks[12], (L, SSD_INNER)),
        'rwkv_mu': jax.random.uniform(ks[13], (L, 4, RWKV_COLS), jnp.float32, 0.0, 0.5),
        'rwkv_w0': jax.random.uniform(ks[14], (L, 2, RWKV_WIDTH), jnp.float32, -6.0, 1.0),
        'rwkv_w2': nrm(ks[15], (L, 2, RWKV_DECAY_LORA, RWKV_WIDTH), 0.1),
        'rwkv_a0': nrm(ks[16], (L, 2, RWKV_WIDTH), 0.1),
        'rwkv_a2': nrm(ks[17], (L, 2, RWKV_ICLR_LORA, RWKV_WIDTH), 0.1),
        'rwkv_g2': nrm(ks[18], (L, RWKV_GATE_LORA, RWKV_WIDTH), RWKV_GATE_LORA ** -0.5),
        'rwkv_kk': one(ks[19], (L, RWKV_WIDTH)),
        'rwkv_ka': one(ks[20], (L, RWKV_WIDTH)),
        'rwkv_rk': nrm(ks[21], (L, RWKV_HEADS, RWKV_HEAD_DIM), 0.1),
        'rwkv_lnx_w': one(ks[22], (L, RWKV_WIDTH)),
        'rwkv_lnx_b': nrm(ks[23], (L, RWKV_WIDTH), 0.02),
        'gla_gu': nrm(ks[24], (L, 2, GLA_GATE_LORA, GLA_K_WIDTH), GLA_GATE_LORA ** -0.5),
        'gla_gb': nrm(ks[25], (L, 2, GLA_K_WIDTH), 0.5),
        'gla_norm_w': one(ks[26], (L, GLA_V_WIDTH)),
        'w_out': nrm(ks[27], (L, MIX_WIDTH, D), MIX_WIDTH ** -0.5 * DN_BETA),
        'ln1_w': one(ks[28], (L, D)),
        'ln1_b': nrm(ks[29], (L, D), 0.02),
        'ln2_w': one(ks[30], (L, D)),
        'ln2_b': nrm(ks[31], (L, D), 0.02),
        'router_w': nrm(ks[32], (L, D, E), D ** -0.5),
        'router_b': nrm(ks[33], (L, E), 0.01),
        'exp_w1': nrm(ks[34], (L, E, D, F), D ** -0.5),
        'exp_w3': nrm(ks[35], (L, E, D, F), D ** -0.5),
        'exp_w2': nrm(ks[36], (L, E, F, D), F ** -0.5 * DN_BETA),
        'sh_w1': nrm(ks[37], (L, D, Fs), D ** -0.5),
        'sh_w3': nrm(ks[38], (L, D, Fs), D ** -0.5),
        'sh_w2': nrm(ks[39], (L, Fs, D), Fs ** -0.5 * DN_BETA),
    }

def second_block(x, c, ctx, c_ctx, ada_w, ada_b, w_in, ssd_conv_w, ssd_conv_b, ssd_dt_bias, ssd_a_log, ssd_d,
              ssd_norm_w, rwkv_mu, rwkv_w0, rwkv_w2, rwkv_a0, rwkv_a2, rwkv_g2, rwkv_kk, rwkv_ka, rwkv_rk,
              rwkv_lnx_w, rwkv_lnx_b, gla_gu, gla_gb, gla_norm_w, w_out, ln1_w, ln1_b, ln2_w, ln2_b,
              router_w, router_b, exp_w1, exp_w3, exp_w2, sh_w1, sh_w3, sh_w2):
    n_ctx = ctx.shape[1]
    xc = ctx
    for l in range(DEPTH_2):
        mod = jnp.split(jax.nn.silu(c) @ ada_w[l] + ada_b[l], N_MOD, axis=-1)
        modc = jnp.split(jax.nn.silu(c_ctx) @ ada_w[l] + ada_b[l], N_MOD, axis=-1)
        sh1, sc1, g1, sh2, sc2, g2 = [m[:, None, :] for m in mod]
        sh1c, sc1c, g1c, sh2c, sc2c, g2c = modc

        u = jnp.concatenate([_layernorm(xc) * (1.0 + sc1c) + sh1c,
                             _layernorm(x) * (1.0 + sc1) + sh1], axis=1)
        mix = _token_mixer(u, n_ctx, w_in[l], ssd_conv_w[l], ssd_conv_b[l], ssd_dt_bias[l], ssd_a_log[l], ssd_d[l],
                           ssd_norm_w[l], rwkv_mu[l], rwkv_w0[l], rwkv_w2[l], rwkv_a0[l], rwkv_a2[l], rwkv_g2[l],
                           rwkv_kk[l], rwkv_ka[l], rwkv_rk[l], rwkv_lnx_w[l], rwkv_lnx_b[l], gla_gu[l], gla_gb[l],
                           gla_norm_w[l], w_out[l])
        x = _layernorm(DN_ALPHA * x + g1 * mix[:, n_ctx:], ln1_w[l], ln1_b[l])
        xc = _layernorm(DN_ALPHA * xc + g1c * mix[:, :n_ctx], ln1_w[l], ln1_b[l])

        h = _layernorm(x) * (1.0 + sc2) + sh2
        moe_w = (router_w[l], router_b[l], exp_w1[l], exp_w3[l], exp_w2[l], sh_w1[l], sh_w3[l], sh_w2[l])
        if l < DEPTH_2 - 1:
            hc = _layernorm(xc) * (1.0 + sc2c) + sh2c
            tok = jnp.concatenate([hc, h], axis=1)
            f = _moe_ffn(tok.reshape(-1, D_MODEL), *moe_w).reshape(tok.shape)
            xc = _layernorm(DN_ALPHA * xc + g2c * f[:, :n_ctx], ln2_w[l], ln2_b[l])
            f = f[:, n_ctx:]
        else:
            f = _moe_ffn(h.reshape(-1, D_MODEL), *moe_w).reshape(h.shape)
        x = _layernorm(DN_ALPHA * x + g2 * f, ln2_w[l], ln2_b[l])
    return x


def setup_inputs(seed=0):
    out = dict(first_inputs(seed))
    for name, value in second_inputs(seed + 1).items():
        if name != "x":
            out[name + "_2"] = value
    return out


def reference(
    x, norm_mix_pre, norm_mix_post, norm_ffn_pre, norm_ffn_post, na_w_qkv, na_w_o, na_rpb,
    dil_w_qkv, dil_w_o, ffn_w_gate, ffn_w_up, ffn_w_down, c_2, ctx_2, c_ctx_2, ada_w_2, ada_b_2,
    w_in_2, ssd_conv_w_2, ssd_conv_b_2, ssd_dt_bias_2, ssd_a_log_2, ssd_d_2, ssd_norm_w_2,
    rwkv_mu_2, rwkv_w0_2, rwkv_w2_2, rwkv_a0_2, rwkv_a2_2, rwkv_g2_2, rwkv_kk_2, rwkv_ka_2,
    rwkv_rk_2, rwkv_lnx_w_2, rwkv_lnx_b_2, gla_gu_2, gla_gb_2, gla_norm_w_2, w_out_2, ln1_w_2,
    ln1_b_2, ln2_w_2, ln2_b_2, router_w_2, router_b_2, exp_w1_2, exp_w3_2, exp_w2_2, sh_w1_2,
    sh_w3_2, sh_w2_2,
):
    x = first_block(
        x, norm_mix_pre, norm_mix_post, norm_ffn_pre, norm_ffn_post, na_w_qkv, na_w_o, na_rpb,
        dil_w_qkv, dil_w_o, ffn_w_gate, ffn_w_up, ffn_w_down,
    )
    return second_block(
        x, c_2, ctx_2, c_ctx_2, ada_w_2, ada_b_2, w_in_2, ssd_conv_w_2, ssd_conv_b_2,
        ssd_dt_bias_2, ssd_a_log_2, ssd_d_2, ssd_norm_w_2, rwkv_mu_2, rwkv_w0_2, rwkv_w2_2,
        rwkv_a0_2, rwkv_a2_2, rwkv_g2_2, rwkv_kk_2, rwkv_ka_2, rwkv_rk_2, rwkv_lnx_w_2,
        rwkv_lnx_b_2, gla_gu_2, gla_gb_2, gla_norm_w_2, w_out_2, ln1_w_2, ln1_b_2, ln2_w_2,
        ln2_b_2, router_w_2, router_b_2, exp_w1_2, exp_w3_2, exp_w2_2, sh_w1_2, sh_w3_2,
        sh_w2_2,
    )


_drawn_inputs = setup_inputs


def setup_inputs(seed=0):
    import zlib

    import numpy as np

    out = dict(_drawn_inputs(seed))
    spreads = {}
    factors = {'ctx_2': 16.051,
     'c_ctx_2': 5.481,
     'ada_b_2': 2.754,
     'ssd_conv_b_2': 56.67,
     'ssd_dt_bias_2': 37.24,
     'ssd_a_log_2': 30.752,
     'ssd_d_2': 170.854,
     'ssd_norm_w_2': 45.488,
     'rwkv_mu_2': 3.347,
     'rwkv_w0_2': 11.426,
     'rwkv_w2_2': 58.982,
     'rwkv_a0_2': 8.0,
     'rwkv_a2_2': 7.732,
     'rwkv_kk_2': 200.0,
     'rwkv_ka_2': 6.956,
     'rwkv_rk_2': 5.953,
     'rwkv_lnx_w_2': 200.0,
     'rwkv_lnx_b_2': 200.0,
     'gla_gu_2': 17.46,
     'gla_gb_2': 24.003,
     'gla_norm_w_2': 200.0,
     'ln2_b_2': 2.804}
    for name, (base, spread) in spreads.items():
        noise = np.random.default_rng([zlib.crc32(name.encode()), seed]).standard_normal(out[name].shape)
        drawn = base * np.exp(spread * noise) if base else spread * noise
        out[name] = jnp.asarray(drawn.astype(out[name].dtype))
    for name, factor in factors.items():
        out[name] = (out[name] * factor).astype(out[name].dtype)
    return out
```

```python
from contextlib import ExitStack

import numpy as np

import concourse.bass as bass
from concourse import mybir

F32 = mybir.dt.float32
I32 = mybir.dt.int32
ALU = mybir.AluOpType
ACT = mybir.ActivationFunctionType
X = mybir.AxisListType.X

P = 128
D = 1024
KC = D // P
SEQ = 256
CTX = 256
NT = SEQ // P
ALL = CTX + SEQ
DEPTH = 2
HEADS = 16
HD = 64
GRID_W = 64
GRID_H = SEQ // GRID_W
NA_COLS = 16
RPB_R, RPB_C = 15, 31
GROUPS = 3
DFF = 2816
FF_TILE = 256
N_FF = DFF // FF_TILE
RMS_EPS = 1e-6
LN_EPS = 1e-5
RWKV_LNX_EPS = 64e-5
SLOTS = 6
SLOT = 2048
NEG_FILL = -1e33

EXPERTS = 64
TOP_K = 8
EGROUPS = 8
TOP_GROUPS = 4
ROUTED_SCALE = 2.5
DN_ALPHA = 2.0 ** 0.25


def slope(h):
    return float(np.float32(2.0) ** np.float32(-8.0 * (h + 1) / HEADS))


def offsets(widths):
    table, off = {}, 0
    for k, w in widths:
        table[k] = (off, w)
        off += w
    return table, off


VCOL, VCOL_N = offsets([("conv_w", 24), ("conv_b", 8), ("mu", 36), ("rwkv_a0", 4), ("rwkv_kk", 2), ("rwkv_ka", 2),
                        ("rwkv_rk", 2), ("one_less_ka", 2)])
VROW, VROW_N = offsets([("rwkv_w0", 512), ("dt_bias", 16), ("a_log", 16), ("ssd_d", 8), ("ssd_norm_w", 512),
                        ("lnx_w", 256), ("lnx_b", 256), ("gla_gb", 256), ("gla_norm_w", 256), ("router_b", 64)])

FENCES = ["na_attn", "na_out", "ffn0_out", "dil_attn", "dil_out", "ffn1_out", "mod", "mix_in", "mix_conv", "gla_done",
          "ssd_done", "rwkv_once", "rwkv_fwd", "rwkv_bwd", "mix_out", "moe_out"]


def constants():
    p = np.arange(P)[:, None]
    i = np.arange(P)[None, :]
    f = {}
    f["ident"] = (p == i)
    f["ones"] = np.ones((P, P))
    f["mirror"] = (p // 64 == i // 64) & (p % 64 == 63 - i % 64)
    f["head_sum"] = (p // HD == i // HD)
    f["below8"] = np.broadcast_to((np.arange(64) % 8 < np.arange(64) // 8)[None, :], (P, 64))
    f["head_cols"] = (p // HD == np.arange(2)[None, :])
    f["gla_diag"] = (p // 32 == np.arange(256)[None, :] // 64)
    same = p // 64 == i // 64
    col = np.arange(2)[None, :]
    for d in range(2):
        inc = (p <= i) if d == 0 else (p >= i)
        f[f"cum{d}"] = inc
        f[f"rest{d}"] = ~inc
        mid = (p % 64 <= 31) if d == 0 else (p % 64 >= 32)
        exc = (p < i) if d == 0 else (p > i)
        f[f"rk_inc{d}"] = (same & inc).astype(int) - (same & mid)
        f[f"rk_exc{d}"] = (same & exc).astype(int) - (same & mid)
        f[f"rk_tail{d}"] = (p // 64 == col) & ~mid
        f[f"rk_ref{d}"] = (p // 64 == col) & mid
        for n in range(7):
            s = 1 << n
            blk, u = i // (2 * s), i % (2 * s)
            m = blk * 2 * s + s - 1
            if d == 0:
                a = np.where(u >= s, (p > m) & (p <= i), (p > i) & (p <= m))
            else:
                a = np.where(u < s, (p >= i) & (p <= m), (p > m) & (p < i))
            f[f"lev{d}_{n}"] = a
    names, parts, off = {}, [], 0
    for k, v in f.items():
        names[k] = (off, v.shape[1])
        parts.append(v.astype(np.float32))
        off += v.shape[1]
    masks = []
    for d in range(2):
        for n in range(7):
            s = 1 << n
            same_blk = p // (2 * s) == i // (2 * s)
            first, second = p % (2 * s) < s, i % (2 * s) >= s
            masks.append(same_blk & (first & second if d == 0 else ~first & ~second))
    masks.append(p == i)
    masks = np.concatenate([m.astype(np.int32) for m in masks], 1)
    fm = []
    for d in range(2):
        inc = (p <= i) if d == 0 else (p >= i)
        fm += [inc, same & inc, same & inc & (p != i)]
        fm += [masks[:, (7 * d + n) * P:(7 * d + n + 1) * P] for n in range(6)]
    fm = np.concatenate([m.astype(np.float32) for m in fm], 1)
    tok = np.arange(SEQ)
    nd = np.zeros((P, NT, GROUPS, SEQ), np.float32)
    for t in range(NT):
        dist = np.abs(tok[None, :] - (t * P + np.arange(P))[:, None])
        for g, ok in enumerate((dist <= 64, dist % 4 == 0, dist % 16 == 0)):
            nd[:, t, g] = np.where(ok, -dist.astype(np.float32), NEG_FILL)
    c = 63 - np.arange(P)[:, None] % 64
    start = np.clip(c - NA_COLS // 2, 0, GRID_W - NA_COLS)
    k = np.arange(GRID_W)[None, :]
    win = np.where((k >= start) & (k < start + NA_COLS), 0.0, -1e30).astype(np.float32)
    return names, {"cst": np.concatenate(parts, 1), "lev_masks": masks, "tri_masks": fm,
                   "neg_dist": nd.reshape(P, -1), "na_window": win}


def program(nc, d, out, names):
    ctx = ExitStack()
    sems = {}

    def S(name):
        if name not in sems:
            sems[name] = ctx.enter_context(nc.semaphore(name))
        return sems[name]

    MEM = 52900
    mem = ctx.enter_context(nc.sbuf_tensor("mem", [P, MEM], F32))
    psum = ctx.enter_context(nc.psum_tensor("psum", [P, 8, 512], F32))
    top = [0]
    high = [0]

    def alloc(*shape, dt=F32):
        n = int(np.prod(shape))
        a = mem[:, top[0]:top[0] + n]
        top[0] += n
        high[0] = max(high[0], top[0])
        assert top[0] <= MEM, (top[0], shape)
        if dt is not F32:
            a = a.bitcast(dt)
        names_ = "abcd"[:len(shape)]
        if len(shape) > 1:
            a = a.rearrange(f"p ({' '.join(names_)}) -> p {' '.join(names_)}",
                            **{k: v for k, v in zip(names_[1:], shape[1:])})
        return a

    def bc(ap, axis, n):
        a = ap.unsqueeze(axis)
        shape = list(a.shape)
        shape[axis] = n
        return a.to_broadcast(shape)

    def bank(b, n=512, off=0):
        return psum[:, b, off:off + n]

    def banks(b, n):
        return psum[:, b:b + n, :].rearrange("p b n -> p (b n)")

    ring = alloc(SLOTS, SLOT)
    cst = alloc(sum(n for _, n in names.values()))
    x_tok = alloc(NT, D)

    def C(name):
        o, n = names[name]
        return cst[:, o:o + n]

    ident = C("ident")
    aT = alloc(KC, SEQ)
    xn = alloc(NT, D)
    stat = alloc(4, 64)
    gains = alloc(8, KC)
    gain_b = alloc(D)
    rms_eps = alloc(1)
    ln_eps = alloc(1)
    lnx_eps = alloc(1)
    hid = alloc(2, 2 * SEQ)
    gate_act = alloc(2 * SEQ)
    base_top = top[0]

    def cols(w, n0, n=256):
        return w.rearrange("(p c) n -> p c n", p=P)[:, :, n0:n0 + n]

    def slot(n, c, w):
        return ring[:, n % SLOTS, 0:c * w].rearrange("p (c w) -> p c w", c=c)

    sp_items, pe_items = [0], [0]

    def load(sp, src, c, w):
        n = sp_items[0]
        sp_items[0] += 1
        if n >= SLOTS:
            sp.wait_ge(S("item_used"), n - SLOTS + 1)
        sp.dma_start(slot(n, c, w), src).then_inc(S(f"slot_loaded{n % SLOTS}"), 16)

    def take(pe, c, w):
        n = pe_items[0]
        pe_items[0] += 1
        pe.wait_ge(S(f"slot_loaded{n % SLOTS}"), 16 * (n // SLOTS + 1))
        return slot(n, c, w)

    fences = {}

    def fence(eng, name):
        fences[name] = 1
        eng.drain().then_inc(S("fence"), 1)
        eng.wait_ge(S("fence"), 4 * fence_no[name])

    fence_no = {n: k + 1 for k, n in enumerate(FENCES)}

    links = {}

    def link(eng, key, ins):
        links[key] = links.get(key, 0) + 1
        ins.then_inc(S(f"{key}_chain"), 1)
        eng.wait_ge(S(f"{key}_chain"), links[key])

    norm_n = {"act": 0, "dve": 0, "pe": 0}

    def norm_act(act, src, tiles, kind, dst, scale, shift):
        k = norm_n["act"]
        norm_n["act"] += 1
        if kind == "rms":
            for t in range(tiles):
                link(act, "act", nc.scalar.activation(xn[:, t % NT, :], src[:, t, :], ACT.Square,
                                                      accum_out=stat[:, 0, t:t + 1]))
            act.activation(stat[:, 1, 0:tiles], stat[:, 0, 0:tiles], ACT.Sqrt, bias=rms_eps,
                           scale=1.0 / D).then_inc(S("norm_root"), 1)
        else:
            act.wait_ge(S("norm_var"), norm_count["ln", k] + 1)
            act.activation(stat[:, 1, 0:tiles], stat[:, 0, 0:2 * tiles].rearrange("p (t s) -> p t s", s=2)[:, :, 1],
                           ACT.Sqrt, bias=ln_eps, scale=1.0).then_inc(S("norm_root"), 1)
        for q in range(4):
            act.wait_ge(S("norm_turned"), 4 * k + q + 1)
            for c in (2 * q, 2 * q + 1):
                w = tiles * P
                o = dst[:, c, 0:w]
                i = bank(q, 2 * SEQ)[:, (c % 2) * w:(c % 2 + 1) * w]
                if shift is None:
                    ins = act.activation(o, i, ACT.Identity, scale=scale[:, c:c + 1])
                else:
                    ins = act.activation(o, i, ACT.Identity, scale=scale[:, c:c + 1], bias=shift[:, c:c + 1])
                ins.then_inc(S("norm_T"), 1)

    norm_count = {}
    norm_kinds = ["rms", "rms", "rms", "rms", "ln", "ln", "ln"]
    seen = 0
    for k, kind in enumerate(norm_kinds):
        norm_count["ln", k] = seen
        seen += kind == "ln"

    def norm_dve(dve, src, tiles, kind):
        k = norm_n["dve"]
        norm_n["dve"] += 1
        if kind == "ln":
            for t in range(tiles):
                for h in range(2):
                    link(dve, "dve", dve.bn_stats(stat[:, 2, 12 * t + 6 * h:12 * t + 6 * h + 6],
                                                  src[:, t, 512 * h:512 * h + 512]))
            for t in range(tiles):
                ins = dve.bn_aggr(stat[:, 0, 2 * t:2 * t + 2], stat[:, 2, 12 * t:12 * t + 12])
                if t < tiles - 1:
                    link(dve, "dve", ins)
            ins.then_inc(S("norm_var"), 1)
        dve.wait_ge(S("norm_root"), k + 1)
        link(dve, "dve", dve.reciprocal(stat[:, 3, 0:tiles], stat[:, 1, 0:tiles]))
        if k:
            dve.wait_ge(S("norm_turned"), 4 * k)
        for t in range(tiles):
            if kind == "rms":
                ins = dve.tensor_scalar(xn[:, t, :], src[:, t, :], stat[:, 3, t:t + 1], None, ALU.mult)
            else:
                ins = dve.tensor_scalar(xn[:, t, :], src[:, t, :], stat[:, 0, 2 * t:2 * t + 1],
                                        stat[:, 3, t:t + 1], ALU.subtract, ALU.mult)
            ins.then_inc(S("norm_rows"), 1)

    def norm_pe(pe, tiles):
        k = norm_n["pe"]
        norm_n["pe"] += 1
        pe.wait_ge(S("norm_rows"), NT * (k + 1))
        if k:
            pe.wait_ge(S("norm_T"), KC * k)
        turn_pe(pe, xn, "norm_turned")

    def turn_pe(pe, rows, done):
        for q in range(4):
            for c in (2 * q, 2 * q + 1):
                for t in range(NT):
                    ins = pe.transpose(bank(q, P, (c % 2) * SEQ + t * P),
                                       rows[:, t, :].rearrange("p (i c) -> p c i", c=KC)[:, c, :], ident)
            ins.then_inc(S(done), 1)

    def rows_product(pe, lhs, lhs_ready, out_bank0, n_items, done):
        for i in range(n_items):
            w = take(pe, KC, 256)
            for t in range(NT):
                o = banks(out_bank0 + 2 * t, 2)[:, 256 * i:256 * i + 256]
                for c in range(KC):
                    ins = pe.matmul(o, lhs[:, c, t * P:(t + 1) * P], w[:, c, :], start=c == 0, stop=c == KC - 1)
            ins.then_inc(S("item_used"), 1)

    res_n = {"act": 0, "dve": 0}

    def residual_act(act, item_count):
        k = res_n["act"]
        res_n["act"] += 1
        act.wait_ge(S("item_used"), item_count)
        for t in range(NT):
            link(act, "act", act.activation(xn[:, t, :], banks(4 + 2 * t, 2), ACT.Square,
                                            accum_out=stat[:, 0, t:t + 1]))
        act.activation(stat[:, 1, 0:NT], stat[:, 0, 0:NT], ACT.Sqrt, bias=rms_eps,
                       scale=1.0 / D).then_inc(S("post_root"), 1)

    def residual_dve(dve):
        k = res_n["dve"]
        res_n["dve"] += 1
        dve.wait_ge(S("post_root"), k + 1)
        dve.wait_ge(S("gain_b"), 16 * (k + 1))
        link(dve, "dve", dve.reciprocal(stat[:, 3, 0:NT], stat[:, 1, 0:NT]))
        for t in range(NT):
            link(dve, "dve", dve.scalar_tensor_tensor(xn[:, t, :], banks(4 + 2 * t, 2), stat[:, 3, t:t + 1], gain_b,
                                                      ALU.mult, ALU.mult))
            link(dve, "dve", dve.tensor_tensor(x_tok[:, t, :], x_tok[:, t, :], xn[:, t, :], ALU.add))

    def experts_sp(sp, n, up, down):
        for w in up(0):
            load(sp, w, KC, 256)
        n0 = sp_items[0]
        for e in range(2):
            for w in up(e + 1):
                load(sp, w, KC, 256)
            load(sp, down(e), 2, D)
        with sp.Fori(1, (n - 1) // 2) as i:
            for j in range(2):
                srcs = list(up(2 * i + 1 + j)) + [down(2 * i + j)]
                for m, w in enumerate(srcs):
                    q = n0 + 3 * j + m
                    sp.wait_ge(S("item_used"), 6 * i + (q - SLOTS + 1))
                    c, wd = (KC, 256) if m < 2 else (2, D)
                    sp.dma_start(slot(q, c, wd), w).then_inc(S(f"slot_loaded{q % SLOTS}"), 16)
        sp_items[0] = n0 + 6 * ((n - 1) // 2)
        load(sp, down(n - 1), 2, D)

    def experts_pe(pe, tag, n, gated):
        def up(get, e, static):
            for m, (b, free) in enumerate(((0, f"{tag}_silu"), (1, f"{tag}_hid"))):
                w = get()
                if not static:
                    pe.wait_ge(S(free), e)
                for f in range(2):
                    for c in range(KC):
                        ins = pe.matmul(bank(b, SEQ, f * SEQ), w[:, c, f::2], aT[:, c, :],
                                        start=c == 0, stop=c == KC - 1)
                ins.then_inc(S("item_used"), 1)
            if gated:
                if not static:
                    pe.wait_ge(S("gate_diag"), e)
                    pe.matmul(bank(2, SEQ), C("ones"), gate_diag, start=True, stop=True
                              ).then_inc(S("gate_spread"), 1)

        def down(get, e, parity, first, last):
            w = get()
            pe.wait_ge(S(f"{tag}_hid"), e + 1)
            for f in range(2):
                for t in range(NT):
                    for h in range(2):
                        ins = pe.matmul(bank(4 + 2 * t + h), hid[:, parity, f * SEQ + t * P:f * SEQ + (t + 1) * P],
                                        w[:, f, 512 * h:512 * h + 512], start=first and f == 0,
                                        stop=last and f == 1, skip_group_check=True)
            ins.then_inc(S("item_used"), 1)

        up(lambda: take(pe, KC, 256), 0, True)
        n0 = pe_items[0]
        up(lambda: take(pe, KC, 256), 1, False)
        down(lambda: take(pe, 2, D), 0, 0, True, False)
        up(lambda: take(pe, KC, 256), 2, False)
        down(lambda: take(pe, 2, D), 1, 1, False, False)
        with pe.Fori(1, (n - 1) // 2) as i:
            for j in range(2):
                def get(m, c, w):
                    q = n0 + 3 * j + m
                    pe.wait_ge(S(f"slot_loaded{q % SLOTS}"), 16 * i + 16 * (q // SLOTS + 1))
                    return slot(q, c, w)
                order = iter(range(2))
                up(lambda: get(next(order), KC, 256), 2 * i + 1 + j, False)
                down(lambda: get(2, 2, D), 2 * i + j, j, False, False)
        pe_items[0] = n0 + 6 * ((n - 1) // 2)
        down(lambda: take(pe, 2, D), n - 1, 0, False, True)

    def experts_act(act, tag, n, base):
        def silu(e, used, first):
            act.wait_ge(S("item_used"), used)
            if not first:
                act.wait_ge(S(f"{tag}_hid"), e)
            act.activation(gate_act, bank(0), ACT.Silu).then_inc(S(f"{tag}_silu"), 1)

        silu(0, base + 1, True)
        with act.Fori(1, n) as e:
            silu(e, 3 * e + base, False)

    def experts_dve(dve, tag, n, base, gated):
        def one(e, used, parity, first):
            dve.wait_ge(S(f"{tag}_silu"), e + 1)
            if gated and not first:
                dve.wait_ge(S("gate_spread"), e)
                dve.tensor_tensor(gate_act.rearrange("p (f t) -> p f t", f=2), gate_act.rearrange("p (f t) -> p f t", f=2),
                                  bc(bank(2, SEQ), 1, 2), ALU.mult).then_inc(S(f"{tag}_gated"), 1)
                dve.wait_ge(S(f"{tag}_gated"), e)
            dve.wait_ge(S("item_used"), used)
            dve.tensor_tensor(hid[:, parity, :], gate_act, bank(1), ALU.mult).then_inc(S(f"{tag}_hid"), 1)
            if gated:
                diag(e, first)

        def diag(e, first):
            if not first:
                dve.wait_ge(S("gate_spread"), e)
            for t in range(NT):
                g = gate[:, t, 0:1] if first else gate[:, t, bass.ds(e, 1)]
                ins = dve.tensor_scalar(gate_diag[:, t * P:(t + 1) * P], ident, g, None, ALU.mult)
            ins.then_inc(S("gate_diag"), 1)

        one(0, base + 2, 0, True)
        with dve.Fori(0, (n - 1) // 2) as i:
            for j in range(2):
                one(2 * i + 1 + j, 6 * i + (base + 3 * (1 + j) + 1), (1 + j) % 2, False)

    qT, kT, v_tok = [], [], []
    for g in range(GROUPS):
        if g == GROUPS - 1:
            na_bias = mem[:, top[0]:top[0] + HEADS * 6 * GRID_W].rearrange("p (a b c) -> p a b c", a=HEADS, b=6)
        qT.append(alloc(KC, SEQ))
        kT.append(alloc(KC, SEQ))
        v_tok.append(alloc(NT, D))
    s_buf = alloc(2, GROUPS * SEQ)
    p_buf = alloc(2, GROUPS * SEQ)
    pT_buf = alloc(2, GROUPS * SEQ)
    neg_max = alloc(2 * HEADS)
    row_sum = alloc(NT, HEADS)
    inv_sum = alloc(NT, HEADS)
    o_tok = xn
    na_window = alloc(GRID_W)
    neg_dist = alloc(NT, GROUPS * SEQ)
    attn_top = top[0]

    NA_QKV = 0
    NA_WO = 12
    FF0 = 16
    DIL_QKV = FF0 + 3 * N_FF
    DIL_WO = DIL_QKV + 12 * GROUPS
    FF1 = DIL_WO + 4
    MOD = FF1 + 3 * N_FF

    def qkv_pe(pe, g, n0):
        for i in range(12):
            m = n0 + i
            w = take(pe, KC, 256)
            if m >= 4:
                pe.wait_ge(S(f"qkv_moved{m % 2}"), (m - 4) // 2 + 1)
            for half in range(2):
                o = bank(4 + m % 4, SEQ, half * SEQ)
                for c in range(KC):
                    if i < 8:
                        ins = pe.matmul(o, w[:, c, half * P:(half + 1) * P], aT[:, c, :], start=c == 0,
                                        stop=c == KC - 1)
                    else:
                        ins = pe.matmul(o, aT[:, c, half * P:(half + 1) * P], w[:, c, :], start=c == 0,
                                        stop=c == KC - 1)
            ins.then_inc(S("item_used"), 1)

    def qkv_place(g, i):
        if i < 8:
            return (qT if i < 4 else kT)[g][:, 2 * (i % 4):2 * (i % 4) + 2, :]
        return v_tok[g][:, :, 256 * (i - 8):256 * (i - 8) + 256]

    def qkv_move(eng, g, n0, item0, parity):
        for i in range(12):
            m = n0 + i
            if m % 2 != parity:
                continue
            eng.wait_ge(S("item_used"), item0 + i + 1)
            src = bank(4 + m % 4).rearrange("p (a b) -> p a b", a=2)
            f = HD ** -0.5 if i < 4 else 1.0
            if parity == 0:
                ins = nc.scalar.activation(qkv_place(g, i), src, ACT.Copy, scale=f)
            else:
                ins = nc.vector.tensor_scalar(qkv_place(g, i), src, f, None, ALU.mult)
            ins.then_inc(S(f"qkv_moved{parity}"), 1)

    def na_attn_pe(pe):
        pe.wait_ge(S("qkv_moved0"), 6)
        pe.wait_ge(S("qkv_moved1"), 6)
        pe.wait_ge(S("na_bias_ready"), 1)
        for h in range(HEADS + 2):
            if h < HEADS:
                if h >= 2:
                    pe.wait_ge(S("na_exp"), 2 * (h - 1))
                r = slice(HD * (h % 2), HD * (h % 2) + HD)
                for t in range(NT):
                    o = bank(h % 2, SEQ, t * SEQ)
                    pe.matmul(o, qT[0][r, h // 2, t * P:(t + 1) * P], kT[0][r, h // 2, :], start=True, stop=False)
                    ins = pe.matmul(o, C("mirror"), na_bias[:, h, 2 - 2 * t:6 - 2 * t, :].rearrange("p a b -> p (a b)"),
                                    start=False, stop=True)
                ins.then_inc(S("na_scores"), 1)
            if 1 <= h <= HEADS:
                g = h - 1
                pe.wait_ge(S("na_exp"), 2 * g + 2)
                if g >= 2:
                    pe.wait_ge(S("na_pT"), g - 1)
                for kc in range(2):
                    for t in range(NT):
                        ins = pe.transpose(bank(2 + g % 2, P, (2 * kc + t) * P), p_buf[:, g % 2, t * SEQ + kc * P:
                                           t * SEQ + kc * P + P], ident)
                ins.then_inc(S("na_turned"), 1)
            if h >= 2:
                g = h - 2
                pe.wait_ge(S("na_pT"), g + 1)
                if g % 4 == 0 and g >= 8:
                    pe.wait_ge(S("na_o"), g // 4 - 1)
                for t in range(NT):
                    for kc in range(2):
                        ins = pe.matmul(bank(4 + (g // 4) % 2, HD, t * SEQ + (g % 4) * HD),
                                        pT_buf[:, g % 2, (2 * kc + t) * P:(2 * kc + t + 1) * P],
                                        v_tok[0][:, kc, g * HD:(g + 1) * HD], start=kc == 0, stop=kc == 1)
                ins.then_inc(S("na_pv"), 1)

    def na_attn_act(act):
        for h in range(HEADS):
            act.wait_ge(S("na_max"), h + 1)
            if h >= 2:
                act.wait_ge(S("na_turned"), h - 1)
            for t in range(NT):
                act.activation(p_buf[:, h % 2, t * SEQ:(t + 1) * SEQ], bank(h % 2, SEQ, t * SEQ), ACT.Exp,
                               bias=neg_max[:, 2 * h + t:2 * h + t + 1], accum_out=row_sum[:, t, h:h + 1]
                               ).then_inc(S("na_exp"), 1)

    def na_attn_dve(dve):
        def rows(gq):
            dve.wait_ge(S("na_pv"), 4 * gq + 4)
            hs = slice(4 * gq, 4 * gq + 4)
            link(dve, "dve", dve.reciprocal(inv_sum[:, :, hs], row_sum[:, :, hs]))
            for t in range(NT):
                ins = dve.tensor_tensor(o_tok[:, t, 256 * gq:256 * gq + 256].rearrange("p (h e) -> p h e", h=4),
                                        bank(4 + gq % 2, SEQ, t * SEQ).rearrange("p (h e) -> p h e", h=4),
                                        bc(inv_sum[:, t, hs], 2, HD), ALU.mult)
            ins.then_inc(S("na_o"), 1)

        for h in range(HEADS + 1):
            if h < HEADS:
                dve.wait_ge(S("na_scores"), h + 1)
                dve.tensor_reduce(neg_max[:, 2 * h:2 * h + 2], bank(h % 2).rearrange("p (t k) -> p t k", t=2), X,
                                  ALU.max, negate=True).then_inc(S("na_max"), 1)
            if h >= 1:
                g = h - 1
                dve.wait_ge(S("na_turned"), g + 1)
                if g >= 2:
                    dve.wait_ge(S("na_pv"), g - 1)
                dve.tensor_copy(pT_buf[:, g % 2, 0:512], bank(2 + g % 2)).then_inc(S("na_pT"), 1)
                if g % 4 == 1 and g >= 5:
                    rows(g // 4 - 1)
        rows(3)

    def dil_attn_pe(pe):
        pe.wait_ge(S("qkv_moved0"), 6 + 18)
        pe.wait_ge(S("qkv_moved1"), 6 + 18)
        U = HEADS * NT
        for u in range(U + 2):
            if u < U:
                h, t = divmod(u, NT)
                r = slice(HD * (h % 2), HD * (h % 2) + HD)
                if u >= 2:
                    pe.wait_ge(S("dil_biased"), u - 1)
                for g in range(GROUPS):
                    ins = pe.matmul(banks(2 * (u % 2), 2)[:, g * SEQ:(g + 1) * SEQ],
                                    qT[g][r, h // 2, t * P:(t + 1) * P], kT[g][r, h // 2, :], start=True, stop=True)
                ins.then_inc(S("dil_scores"), 1)
            if 1 <= u <= U:
                w = u - 1
                pe.wait_ge(S("dil_exp"), w + 1)
                if w >= 1:
                    pe.wait_ge(S("dil_pT"), w)
                for k in range(2 * GROUPS):
                    ins = pe.transpose(banks(4, 2)[:, k * P:(k + 1) * P], p_buf[:, w % 2, k * P:(k + 1) * P], ident)
                ins.then_inc(S("dil_turned"), 1)
            if u >= 2:
                w = u - 2
                h, t = divmod(w, NT)
                pe.wait_ge(S("dil_pT"), w + 1)
                if w % 8 == 0 and w >= 16:
                    pe.wait_ge(S("dil_o"), w // 8 - 1)
                for k in range(2 * GROUPS):
                    ins = pe.matmul(bank(6 + (h // 4) % 2, HD, t * SEQ + (h % 4) * HD),
                                    pT_buf[:, w % 2, k * P:(k + 1) * P],
                                    v_tok[k // 2][:, k % 2, h * HD:(h + 1) * HD], start=k == 0,
                                    stop=k == 2 * GROUPS - 1)
                ins.then_inc(S("dil_pv"), 1)

    def dil_attn_act(act):
        for u in range(HEADS * NT + 1):
            if u < HEADS * NT:
                h, t = divmod(u, NT)
                act.wait_ge(S("dil_max"), u + 1)
                if u >= 2:
                    act.wait_ge(S("dil_turned"), u - 1)
                act.activation(p_buf[:, u % 2, :], s_buf[:, u % 2, :], ACT.Exp, bias=neg_max[:, u:u + 1],
                               accum_out=row_sum[:, t, h:h + 1]).then_inc(S("dil_exp"), 1)
            if u >= 1:
                w = u - 1
                act.wait_ge(S("dil_turned"), w + 1)
                if w >= 2:
                    act.wait_ge(S("dil_pv"), w - 1)
                act.activation(pT_buf[:, w % 2, :], banks(4, 2)[:, 0:GROUPS * SEQ], ACT.Copy
                               ).then_inc(S("dil_pT"), 1)

    def dil_attn_dve(dve):
        def rows(gq):
            dve.wait_ge(S("dil_pv"), 8 * gq + 8)
            hs = slice(4 * gq, 4 * gq + 4)
            link(dve, "dve", dve.reciprocal(inv_sum[:, :, hs], row_sum[:, :, hs]))
            for t in range(NT):
                ins = dve.tensor_tensor(o_tok[:, t, 256 * gq:256 * gq + 256].rearrange("p (h e) -> p h e", h=4),
                                        bank(6 + gq % 2, SEQ, t * SEQ).rearrange("p (h e) -> p h e", h=4),
                                        bc(inv_sum[:, t, hs], 2, HD), ALU.mult)
            ins.then_inc(S("dil_o"), 1)

        dve.wait_ge(S("stage_in"), 16)
        for u in range(HEADS * NT):
            h, t = divmod(u, NT)
            dve.wait_ge(S("dil_scores"), u + 1)
            if u >= 2:
                dve.wait_ge(S("dil_exp"), u - 1)
            dve.scalar_tensor_tensor(s_buf[:, u % 2, :], neg_dist[:, t, :], slope(h),
                                     banks(2 * (u % 2), 2)[:, 0:GROUPS * SEQ], ALU.mult, ALU.add
                                     ).then_inc(S("dil_biased"), 1)
            dve.wait_ge(S("dil_biased"), u + 1)
            dve.tensor_reduce(neg_max[:, u:u + 1], s_buf[:, u % 2, :], X, ALU.max, negate=True
                              ).then_inc(S("dil_max"), 1)
            if u % 8 == 4 and u >= 12:
                rows(u // 8 - 1)
        rows(3)

    def wo_pe(pe, k):
        turn_pe(pe, o_tok, "o_turned")
        pe.wait_ge(S("o_T"), KC * (k + 1))
        rows_product(pe, aT, None, 4, 4, None)

    def wo_act(act, k):
        for q in range(4):
            act.wait_ge(S("o_turned"), 4 * k + q + 1)
            for c in (2 * q, 2 * q + 1):
                act.activation(aT[:, c, :], bank(q, SEQ, (c % 2) * SEQ), ACT.Copy).then_inc(S("o_T"), 1)

    def gain_load(act, src, k):
        act.dma_start(gain_b, src.to_broadcast([P, D])).then_inc(S("gain_b"), 16)

    def g_row(name, layer):
        return d[name][layer:layer + 1, :]

    def block1_sp(sp):
        W = d["na_w_qkv"][0]
        for i in range(12):
            load(sp, cols(W, 256 * i), KC, 256)
        for i in range(4):
            load(sp, cols(d["na_w_o"][0], 256 * i), KC, 256)
        ffn_sp(sp, 0)
        W = d["dil_w_qkv"][0]
        for i in range(12 * GROUPS):
            load(sp, cols(W, 256 * i), KC, 256)
        for i in range(4):
            load(sp, cols(d["dil_w_o"][0], 256 * i), KC, 256)
        ffn_sp(sp, 1)

    def ffn_sp(sp, layer):
        def up(e):
            return [d[n][layer].rearrange("(p c) n -> p c n", p=P)[:, :, bass.ds(e * FF_TILE, FF_TILE)]
                    for n in ("ffn_w_gate", "ffn_w_up")]

        def down(e):
            return d["ffn_w_down"][layer].rearrange("(e p c) n -> e p c n", p=P, c=2)[bass.ds(e, 1)].rearrange(
                "e p c n -> (e p) c n")

        experts_sp(sp, N_FF, up, down)

    def block1_pe(pe):
        pe.wait_ge(S("consts"), 16 * 5)
        norm_pe(pe, NT)
        pe.wait_ge(S("norm_T"), KC * 1)
        qkv_pe(pe, 0, 0)
        na_attn_pe(pe)
        fence(pe, "na_attn")
        wo_pe(pe, 0)
        fence(pe, "na_out")
        norm_pe(pe, NT)
        pe.wait_ge(S("norm_T"), KC * 2)
        experts_pe(pe, "ff0", N_FF, False)
        fence(pe, "ffn0_out")
        norm_pe(pe, NT)
        pe.wait_ge(S("norm_T"), KC * 3)
        for g in range(GROUPS):
            qkv_pe(pe, g, 12 + 12 * g)
        dil_attn_pe(pe)
        fence(pe, "dil_attn")
        wo_pe(pe, 1)
        fence(pe, "dil_out")
        norm_pe(pe, NT)
        pe.wait_ge(S("norm_T"), KC * 4)
        experts_pe(pe, "ff1", N_FF, False)
        fence(pe, "ffn1_out")

    def block1_act(act):
        act.dma_start(x_tok, d["x"][0].rearrange("(t p) c -> p t c", p=P)).then_inc(S("consts"), 16)
        for k, n in enumerate(("norm_mix_pre", "norm_ffn_pre")):
            act.dma_start(gains[:, 2 * k:2 * k + 2, :], d[n].rearrange("l (p c) -> p l c", p=P)).then_inc(S("consts"), 16)
        act.dma_start(cst, d["cst"]).then_inc(S("consts"), 16)
        act.dma_start(na_window, d["na_window"]).then_inc(S("consts"), 16)
        rpb = d["na_rpb"]
        for half in range(2):
            for j in range(6):
                src = bass.AP(tensor=rpb.tensor, offset=(5 - half + j) * RPB_C + NA_COLS - 1 - (GRID_W - 1),
                              ap=[[1, GRID_W], [RPB_R * RPB_C, HEADS], [1, GRID_W]])
                act.dma_start(na_bias[half * 64:half * 64 + 64, :, j, :], src).then_inc(S("na_bias_in"), 16)
        gain_load(act, g_row("norm_mix_post", 0), 0)
        act.wait_ge(S("consts"), 16 * 5)
        act.wait_ge(S("eps_set"), 3)
        norm_act(act, x_tok, NT, "rms", aT, gains[:, 0, :], None)
        qkv_move(act, 0, 0, NA_QKV, 0)
        na_attn_act(act)
        fence(act, "na_attn")
        wo_act(act, 0)
        residual_act(act, NA_WO + 4)
        fence(act, "na_out")
        gain_load(act, g_row("norm_ffn_post", 0), 1)
        act.dma_start(neg_dist.rearrange("p t n -> p (t n)"), d["neg_dist"]).then_inc(S("stage_in"), 16)
        norm_act(act, x_tok, NT, "rms", aT, gains[:, 2, :], None)
        experts_act(act, "ff0", N_FF, FF0)
        residual_act(act, DIL_QKV)
        fence(act, "ffn0_out")
        gain_load(act, g_row("norm_mix_post", 1), 2)
        norm_act(act, x_tok, NT, "rms", aT, gains[:, 1, :], None)
        for g in range(GROUPS):
            qkv_move(act, g, 12 + 12 * g, DIL_QKV + 12 * g, 0)
        dil_attn_act(act)
        fence(act, "dil_attn")
        wo_act(act, 1)
        residual_act(act, DIL_WO + 4)
        fence(act, "dil_out")
        gain_load(act, g_row("norm_ffn_post", 1), 3)
        norm_act(act, x_tok, NT, "rms", aT, gains[:, 3, :], None)
        experts_act(act, "ff1", N_FF, FF1)
        residual_act(act, MOD)
        fence(act, "ffn1_out")

    def block1_dve(dve):
        dve.memset(rms_eps, RMS_EPS).then_inc(S("eps_set"), 1)
        dve.memset(ln_eps, LN_EPS).then_inc(S("eps_set"), 1)
        dve.memset(lnx_eps, RWKV_LNX_EPS).then_inc(S("eps_set"), 1)
        dve.wait_ge(S("consts"), 16 * 5)
        norm_dve(dve, x_tok, NT, "rms")
        qkv_move(dve, 0, 0, NA_QKV, 1)
        na_attn_dve(dve)
        fence(dve, "na_attn")
        residual_dve(dve)
        fence(dve, "na_out")
        norm_dve(dve, x_tok, NT, "rms")
        experts_dve(dve, "ff0", N_FF, FF0, False)
        residual_dve(dve)
        fence(dve, "ffn0_out")
        norm_dve(dve, x_tok, NT, "rms")
        for g in range(GROUPS):
            qkv_move(dve, g, 12 + 12 * g, DIL_QKV + 12 * g, 1)
        dil_attn_dve(dve)
        fence(dve, "dil_attn")
        residual_dve(dve)
        fence(dve, "dil_out")
        norm_dve(dve, x_tok, NT, "rms")
        experts_dve(dve, "ff1", N_FF, FF1, False)
        residual_dve(dve)
        fence(dve, "ffn1_out")

    def block1_pool(pool):
        pool.wait_ge(S("consts"), 16 * 5)
        pool.wait_ge(S("na_bias_in"), 16 * 12)
        b = na_bias.rearrange("p h j k -> p (h j) k")
        pool.tensor_tensor(b, b, bc(na_window, 1, 6 * HEADS), ALU.add).then_inc(S("na_bias_ready"), 1)
        for n in ("na_attn", "na_out", "ffn0_out", "dil_attn", "dil_out", "ffn1_out"):
            fence(pool, n)

    TILES = ALL // P
    KAPPA = float(np.exp(np.float32(-0.5)))
    top[0] = base_top
    vcol = alloc(VCOL_N)
    vrow = alloc(VROW_N)
    mats = alloc(4, 256)
    g1_b = alloc(D)
    g2_b = alloc(D)
    modT = alloc(4, 2, KC)
    z_tok = alloc(NT, 512)
    gqkT = alloc(2, ALL)
    gv_tok = alloc(TILES, 256)
    gdT = alloc(ALL)
    og_tok = alloc(NT, 256)
    dt_raw = alloc(TILES, 16)
    xbcT = alloc(8, ALL)
    rwT = alloc(9, ALL)
    stage_top = top[0]
    y_mix = xn

    def vc(name):
        o, n = VCOL[name]
        return vcol[:, o:o + n]

    def vr(name):
        o, n = VROW[name]
        return vrow[:, o:o + n]

    silu_c = hid.rearrange("p a b -> p (a b)")[:, 0:2 * KC].rearrange("p (k v) -> p k v", v=2)
    c_in = hid.rearrange("p a b -> p (a b)")[:, 64:64 + 2 * KC].rearrange("p (v k) -> p v k", v=2)
    ada_cols = hid.rearrange("p a b -> p (a b)")[:, 128:128 + 4 * KC].rearrange("p (j k) -> p j k", j=4)
    MOD_BANK = {0: 0, 1: 1, 3: 2, 4: 3, 2: 4, 5: 6}
    MOD_COL = (0, 1, 3, 4)

    def mod_sp(sp):
        W = d["ada_w_2"][0].rearrange("(p c) n -> p c n", p=P)
        for j in range(6):
            for s in range(4):
                load(sp, W[:, 2 * s:2 * s + 2, j * D:(j + 1) * D], 2, D)

    def mod_pe(pe):
        pe.wait_ge(S("mod_silu"), 1)
        for j in range(6):
            b = MOD_BANK[j]
            for s in range(4):
                w = take(pe, 2, D)
                for k in range(2):
                    first, last = s == 0 and k == 0, s == 3 and k == 1
                    if j in MOD_COL:
                        for c in range(KC):
                            ins = pe.matmul(bank(b, 2, 2 * c), w[:, k, c::KC], silu_c[:, 2 * s + k, :],
                                            start=first and c == 0, stop=last, skip_group_check=True)
                    else:
                        for h in range(2):
                            ins = pe.matmul(bank(b + h), silu_c[:, 2 * s + k, 0:1].to_broadcast([P, P]),
                                            w[:, k, 512 * h:512 * h + 512], start=first, stop=last)
                ins.then_inc(S("item_used"), 1)

    def mod_act(act):
        act.dma_start(c_in[:, 0, :], d["c_2"][0].rearrange("(p c) -> p c", p=P)).then_inc(S("mod_in"), 16)
        act.dma_start(c_in[:, 1, :], d["c_ctx_2"].rearrange("(p c) -> p c", p=P)).then_inc(S("mod_in"), 16)
        ada_b = d["ada_b_2"][0].rearrange("(j p c) -> j p c", j=6, p=P)
        for n, j in enumerate(MOD_COL):
            act.dma_start(ada_cols[:, n, :], ada_b[j]).then_inc(S("mod_in"), 16)
        for g, dst in ((2, g1_b), (5, g2_b)):
            act.dma_start(dst, d["ada_b_2"][:, g * D:(g + 1) * D].to_broadcast([P, D])).then_inc(S("mod_in"), 16)
        act.dma_start(vcol, d["vcol"]).then_inc(S("mod_in"), 16)
        act.dma_start(vrow, d["vrow"].to_broadcast([P, VROW_N])).then_inc(S("mod_in"), 16)
        act.dma_start(mats.rearrange("p a b -> p (a b)"), d["mats"]).then_inc(S("mod_in"), 16)
        act.wait_ge(S("mod_in"), 16 * 11)
        act.activation(silu_c.rearrange("p k v -> p v k"), c_in, ACT.Silu).then_inc(S("mod_silu"), 1)

    def mod_dve(dve):
        dve.wait_ge(S("mod_in"), 16 * 11)
        for j in range(6):
            b = MOD_BANK[j]
            dve.wait_ge(S("item_used"), MOD + 4 * (j + 1))
            if j in MOD_COL:
                n = MOD_COL.index(j)
                for v in range(2):
                    ins = dve.scalar_tensor_tensor(modT[:, n, v, :], bank(b, 2 * KC).rearrange("p (c v) -> p v c", v=2)[:, v, :],
                                                   1.0 if j in (1, 4) else 0.0, ada_cols[:, n, :], ALU.add, ALU.add)
                    ins.then_inc(S("mod_T"), 1)
            else:
                g = g1_b if j == 2 else g2_b
                dve.tensor_tensor(g, g, banks(b, 2), ALU.add).then_inc(S("mod_g"), 1)

    top[0] = stage_top
    uT = alloc(KC, ALL)
    ctx_tok = rwT.rearrange("p a b -> p (a b)")[:, 0:NT * D].rearrange("p (t c) -> p t c", t=NT)
    MIX = MOD + 24
    Z0, XBC0, DT0, RW0, GQ0, GV0, GD0, OG0 = 0, 512, 1536, 1552, 2704, 2960, 3216, 3248
    rw_in = alloc(9, ALL)

    mix_items = ([(Z0 + 256 * i, 256, "tok_x") for i in range(2)] + [(XBC0 + 256 * i, 256, "chan") for i in range(4)]
                 + [(DT0, 16, "dt")] + [(RW0 + 256 * i, 256, "chan") for i in range(4)] + [(RW0 + 1024, 128, "chan")]
                 + [(GQ0, 256, "chan"), (GV0, 256, "tok_all"), (GD0, 32, "chan"), (OG0, 256, "tok_x")])
    W_OUT = MIX + len(mix_items)

    def mix_jobs():
        for n, (c0, w, kind) in enumerate(mix_items):
            if kind == "tok_x":
                dst = z_tok[:, :, c0:c0 + 256] if c0 < XBC0 else og_tok
                yield n, 0, 1, dst, 1.0
            elif kind == "dt":
                yield n, 0, 1, dt_raw, 1.0
            elif kind == "tok_all":
                for k in range(2):
                    yield n, k, 2, gv_tok[:, 2 * k:2 * k + 2, :], 1.0
            else:
                for k in range(max(1, w // P)):
                    if c0 == GQ0:
                        yield n, k, 2, gqkT[:, k, :], 32 ** -0.5 if k == 0 else 1.0
                    elif c0 == GD0:
                        yield n, 0, 1, gdT[0:32, :], 1.0
                    elif c0 >= RW0:
                        yield n, k, w // P, rw_in[:, (c0 - RW0) // P + k, :], 1.0
                    else:
                        yield n, k, 2, xbcT[:, (c0 - XBC0) // P + k, :], 1.0

    def mix_in_sp(sp):
        for c0, w, _ in mix_items:
            load(sp, cols(d["w_in_2"][0], c0, w), KC, w)

    def mix_in_pe(pe):
        pe.wait_ge(S("norm_T"), KC * 6)
        w = None
        for m, (n, k, parts, dst, f) in enumerate(mix_jobs()):
            c0, width, kind = mix_items[n]
            if k == 0:
                w = take(pe, KC, width)
            if m >= 4:
                pe.wait_ge(S(f"mix_moved{m % 2}"), (m - 4) // 2 + 1)
            b = 4 + m % 4
            if kind == "chan":
                wd = min(P, width)
                for c in range(KC):
                    ins = pe.matmul(psum[0:wd, b, 0:ALL], w[:, c, k * P:k * P + wd], uT[:, c, :], start=c == 0,
                                    stop=c == KC - 1)
            else:
                tiles = {"tok_x": (2, 3), "tok_all": (2 * k, 2 * k + 1), "dt": range(TILES)}[kind]
                for a, t in enumerate(tiles):
                    for c in range(KC):
                        ins = pe.matmul(bank(b, width, a * width), uT[:, c, t * P:(t + 1) * P], w[:, c, :],
                                        start=c == 0, stop=c == KC - 1)
            ins.then_inc(S("item_used") if k == parts - 1 else S("mix_half"), 1)

    def mix_move(eng, parity):
        halves = 0
        for m, (n, k, parts, dst, f) in enumerate(mix_jobs()):
            if k < parts - 1:
                halves += 1
            if m % 2 != parity:
                continue
            if k == parts - 1:
                eng.wait_ge(S("item_used"), MIX + n + 1)
            else:
                eng.wait_ge(S("mix_half"), halves)
            b = 4 + m % 4
            if len(dst.shape) == 2:
                src = psum[0:dst.shape[0], b, 0:ALL]
            else:
                src = bank(b, dst.shape[1] * dst.shape[2]).rearrange("p (a b) -> p a b", a=dst.shape[1])
            if parity == 0:
                ins = nc.scalar.activation(dst, src, ACT.Copy, scale=f)
            else:
                ins = nc.vector.tensor_scalar(dst, src, f, None, ALU.mult)
            ins.then_inc(S(f"mix_moved{parity}"), 1)

    acc = [uT[:, j, :] for j in range(4)]

    def seg(ap, a, b):
        return ap.rearrange("p (s t) -> p s t", s=2)[:, :, a:b]

    def conv_act(act):
        cw, cb = vc("conv_w"), vc("conv_b")
        act.wait_ge(S("mix_moved1"), MIX_MOVED[1])
        for j in range(8):
            if j >= 4:
                act.wait_ge(S("conv_silu"), j - 3)
            act.activation(acc[j % 4], xbcT[:, j, :], ACT.Identity, scale=cw[:, 8 + j:9 + j], bias=cb[:, j:j + 1]
                           ).then_inc(S("conv_mid"), 1)
            if j >= 2:
                silu_act(act, j - 2)
        silu_act(act, 6)
        silu_act(act, 7)
        act.wait_ge(S("shift_coef"), 1)
        for j in range(9):
            for s in range(2):
                act.activation(rwT[:, j, s * 256:s * 256 + 256], rw_in[:, j, s * 256:s * 256 + 256], ACT.Copy,
                               scale=shift_c[:, s, j:j + 1]).then_inc(S("shift_mid"), 1)

    def silu_act(act, j):
        act.wait_ge(S("conv_taps"), j + 1)
        act.activation(xbcT[:, j, :], acc[j % 4], ACT.Silu).then_inc(S("conv_silu"), 1)

    shift_c = hid.rearrange("p a b -> p (a b)")[:, 0:18].rearrange("p (s j) -> p s j", s=2)

    def conv_dve(dve):
        cw, mu = vc("conv_w"), vc("mu").rearrange("p (m j) -> p m j", m=4)
        link(dve, "dve", dve.tensor_tensor(shift_c[:, 0, :], mu[:, 0, :], mu[:, 1, :], ALU.add))
        link(dve, "dve", dve.tensor_tensor(shift_c[:, 1, :], mu[:, 2, :], mu[:, 3, :], ALU.add))
        link(dve, "dve", dve.tensor_tensor(shift_c[:, 1, :], shift_c[:, 1, :], shift_c[:, 0, :], ALU.add))
        dve.tensor_scalar(hid[:, 0, 0:18], hid[:, 0, 0:18], -1.0, 1.0, ALU.mult, ALU.add).then_inc(S("shift_coef"), 1)
        for j in range(8):
            dve.wait_ge(S("conv_mid"), j + 1)
            a, x = acc[j % 4], xbcT[:, j, :]
            link(dve, "dve", dve.scalar_tensor_tensor(seg(a, 1, 256), seg(x, 0, 255), cw[:, j:j + 1], seg(a, 1, 256),
                                                      ALU.mult, ALU.add))
            dve.scalar_tensor_tensor(seg(a, 0, 255), seg(x, 1, 256), cw[:, 16 + j:17 + j], seg(a, 0, 255),
                                     ALU.mult, ALU.add).then_inc(S("conv_taps"), 1)
        for j in range(9):
            dve.wait_ge(S("shift_mid"), 2 * j + 2)
            o, x = rwT[:, j, :], rw_in[:, j, :]

            def add(dst, src, m):
                link(dve, "dve", dve.scalar_tensor_tensor(dst, src, mu[:, m, j:j + 1], dst, ALU.mult, ALU.add))

            add(o[:, 1:256], x[:, 0:255], 0)
            add(o[:, 0:255], x[:, 1:256], 1)
            og, xg = (v[:, 256:512].rearrange("p (r c) -> p r c", r=GRID_H) for v in (o, x))
            add(og[:, :, 1:GRID_W], xg[:, :, 0:GRID_W - 1], 0)
            add(og[:, :, 0:GRID_W - 1], xg[:, :, 1:GRID_W], 1)
            add(o[:, 256 + GRID_W:512], x[:, 256:512 - GRID_W], 2)
            add(o[:, 256:512 - GRID_W], x[:, 256 + GRID_W:512], 3)

    top[0] = stage_top
    lev_masks = alloc(15, P, dt=I32)
    la = alloc(TILES, 256)
    la_e = alloc(TILES, 256)
    gl_E = alloc(2, 256)
    gl_q = alloc(2, 256)
    gl_k = alloc(2, 256)
    gl_acc = alloc(4, NT, P)
    gl_cum = alloc(256)
    gl_rest = alloc(ALL)
    gl_tot = alloc(TILES)
    gl_kt = alloc(TILES, P)
    gl_S = alloc(3, 256)
    gl_y = alloc(NT, 256)
    gl_t = alloc(NT, 256)

    def gla_order(dr):
        return (0, 1, 2, 3) if dr == 0 else (1, 0, 3, 2)

    def gla_pe(pe):
        first_y = [True]

        def ymm(t, lo, n, lhs, rhs, last=False):
            ins = pe.matmul(bank(7, n, t * 256 + lo), lhs, rhs, start=first_y[0], stop=last, skip_group_check=True)
            first_y[0] = False
            return ins

        gu = mats[0:32, 3, :]
        for t in range(TILES):
            ins = pe.matmul(bank(t // 2, 256, (t % 2) * 256), gdT[0:32, t * P:(t + 1) * P], gu, start=True, stop=True)
        ins.then_inc(S("gl_z"), 1)
        pe.wait_ge(S("gl_la"), 1)
        for dr in range(2):
            if dr:
                pe.wait_ge(S("gl_decay"), 3 * dr)
                pe.wait_ge(S("gl_acc_n"), 8)
                pe.wait_ge(S("gl_S_n"), 3)
            for a, t in enumerate((2, 3)):
                pe.matmul(bank(2, P, a * P), la[:, t, dr * P:(dr + 1) * P], C(f"cum{dr}"), start=True, stop=True)
            for t in range(TILES):
                ins = pe.matmul(bank(3, P, t * P), la[:, t, dr * P:(dr + 1) * P], C(f"rest{dr}"), start=True, stop=True)
            for t in range(TILES):
                ins = pe.matmul(bank(2, 1, 256 + t), la[:, t, dr * P:(dr + 1) * P], C("ones")[:, 0:1], start=True, stop=True)
            ins.then_inc(S("gl_sums"), 1)
            pe.wait_ge(S("gl_kdec"), dr + 1)
            for t in range(TILES):
                ins = pe.transpose(bank(6, P, t * P), gl_rest[:, t * P:(t + 1) * P], ident)
            ins.then_inc(S("gl_kturn"), 1)
            pe.wait_ge(S("gl_kt"), dr + 1)
            order = gla_order(dr)
            for k in range(3):
                o = bank(6, 256, 0) if k == 0 else (bank(6, 256, 256) if k == 1 else bank(3, 256, 0))
                ins = pe.matmul(o, gl_kt[:, order[k], :], gv_tok[:, order[k], :], start=True, stop=True)
            ins.then_inc(S("gl_adds"), 1)
            for n in range(8):
                m = 8 * dr + n
                if n < 7:
                    if n >= 2:
                        pe.wait_ge(S("gl_E_n"), 7 * dr + n - 1)
                    for a, t in enumerate((2, 3)):
                        ins = pe.matmul(bank(n % 2, P, a * P), la[:, t, dr * P:(dr + 1) * P], C(f"lev{dr}_{n}"),
                                        start=True, stop=True)
                    ins.then_inc(S("gl_lev"), 1)
                if n >= 1:
                    gla_scores(pe, dr, n - 1)
            gla_scores(pe, dr, 7)
            for k in range(2):
                t = order[2 + k] - 2
                ymm(t, 0, 256, gl_cum[:, t * P:(t + 1) * P], gl_S[:, 1 + k, :])
            pe.wait_ge(S("gl_acc_n"), 8 * dr + 8)
            for t in range(NT):
                for h in range(4):
                    ins = ymm(t, h * 64, 64, gl_acc[:, h, t, :], gv_tok[:, 2 + t, h * 64:(h + 1) * 64], dr == 1)
            ins.then_inc(S("gl_pv"), 1)

    def gla_scores(pe, dr, n):
        m = 8 * dr + n
        if n < 7:
            pe.wait_ge(S("gl_q_n"), 7 * dr + n + 1)
            pe.wait_ge(S("gl_k_n"), 7 * dr + n + 1)
            q, k = gl_q[:, n % 2, :], gl_k[:, n % 2, :]
        else:
            q, k = gqkT[:, 0, CTX:ALL], gqkT[:, 1, CTX:ALL]
        if n == 0:
            pe.wait_ge(S("gl_S_n"), 3 * dr + 3)
        if m >= 1:
            pe.wait_ge(S("gl_acc_n"), m)
        for t in range(NT):
            for h in range(4):
                r = slice(32 * h, 32 * h + 32)
                ins = pe.matmul(bank(3 + h, P, t * P), k[r, t * P:(t + 1) * P], q[r, t * P:(t + 1) * P], start=True,
                                stop=True, tile_position=(32 * h, 0))
        ins.then_inc(S("gl_sc"), 1)

    def gla_act(act):
        act.dma_start(lev_masks.rearrange("p a b -> p (a b)"), d["lev_masks"]).then_inc(S("stage_in"), 16)
        act.wait_ge(S("gl_na"), 1)
        link(act, "act", act.activation(la_e, la_e, ACT.Exp))
        act.activation(la_e, la_e, ACT.Ln, bias=1.0).then_inc(S("gl_ln"), 1)
        act.wait_ge(S("gl_ln"), 1)
        for dr in range(2):
            act.wait_ge(S("gl_sums"), dr + 1)
            if dr:
                act.wait_ge(S("gl_pv"), dr)
            act.activation(gl_rest, bank(3), ACT.Exp, scale=1 / 16).then_inc(S("gl_decay"), 1)
            act.activation(gl_cum, bank(2, 256), ACT.Exp, scale=1 / 16).then_inc(S("gl_decay"), 1)
            act.activation(gl_tot, bank(2, TILES, 256), ACT.Exp, scale=1 / 16).then_inc(S("gl_decay"), 1)
            act.wait_ge(S("gl_kturn"), dr + 1)
            act.activation(gl_kt, bank(6).rearrange("p (t c) -> p t c", t=TILES), ACT.Copy).then_inc(S("gl_kt"), 1)
            for n in range(7):
                act.wait_ge(S("gl_lev"), 7 * dr + n + 1)
                if n >= 2 or dr:
                    used = 7 * dr + (n - 1 if n else 0)
                    act.wait_ge(S("gl_q_n"), used)
                    act.wait_ge(S("gl_k_n"), used)
                act.activation(gl_E[:, n % 2, :], bank(n % 2, 256), ACT.Exp, scale=1 / 16).then_inc(S("gl_E_n"), 1)
        act.wait_ge(S("gl_og"), 1)
        act.activation(og_tok, og_tok, ACT.Silu).then_inc(S("gl_silu"), 1)
        act.wait_ge(S("gl_ss"), 1)
        act.activation(stat[:, 1, 0:8], stat[:, 0, 0:8], ACT.Sqrt, scale=1 / 64, bias=ln_eps).then_inc(S("gl_root"), 1)

    def gla_dve(dve):
        dve.wait_ge(S("gl_z"), 1)
        gb = vr("gla_gb")
        link(dve, "dve", dve.tensor_tensor(la, psum[:, 0:2, :].rearrange("p b (t c) -> p (b t) c", t=2), bc(gb, 1, TILES),
                                           ALU.add))
        dve.scalar_tensor_tensor(la_e, la, -1.0, la, ALU.mult, ALU.min).then_inc(S("gl_na"), 1)
        dve.wait_ge(S("gl_ln"), 1)
        dve.scalar_tensor_tensor(la, la, 0.0, la_e, ALU.min, ALU.subtract).then_inc(S("gl_la"), 1)
        dve.wait_ge(S("stage_in"), 16 * 3)
        for dr in range(2):
            dve.wait_ge(S("gl_decay"), 3 * dr + 1)
            dve.tensor_tensor(gl_rest, gl_rest, gqkT[:, 1, :], ALU.mult).then_inc(S("gl_kdec"), 1)
            dve.wait_ge(S("gl_decay"), 3 * dr + 3)
            link(dve, "dve", dve.tensor_tensor(gl_cum, gl_cum, gqkT[:, 0, CTX:ALL], ALU.mult))
            link(dve, "dve", dve.memset(gl_acc, 0.0))
            dve.wait_ge(S("gl_adds"), dr + 1)
            order = gla_order(dr)
            diag = C("gla_diag")
            for k in range(3):
                src = bank(6, 256, 0) if k == 0 else (bank(6, 256, 256) if k == 1 else bank(3, 256, 0))
                if k == 0:
                    dve.tensor_tensor(gl_S[:, 0, :], src, diag, ALU.mult).then_inc(S("gl_S_n"), 1)
                else:
                    link(dve, "dve", dve.tensor_tensor(gl_t[:, 0, :], src, diag, ALU.mult))
                    tot = gl_tot[:, order[k]:order[k] + 1]
                    dve.scalar_tensor_tensor(gl_S[:, k, :], gl_S[:, k - 1, :], tot, gl_t[:, 0, :], ALU.mult, ALU.add
                                             ).then_inc(S("gl_S_n"), 1)
                dve.wait_ge(S("gl_S_n"), 3 * dr + k + 1)
            for n in range(8):
                if n < 7:
                    dve.wait_ge(S("gl_E_n"), 7 * dr + n + 1)
                    if 8 * dr + n >= 2:
                        dve.wait_ge(S("gl_sc"), 8 * dr + n - 1)
                    dve.tensor_tensor(gl_q[:, n % 2, :], gqkT[:, 0, CTX:ALL], gl_E[:, n % 2, :], ALU.mult
                                      ).then_inc(S("gl_q_n"), 1)
                if n >= 1:
                    gla_pick(dve, dr, n - 1)
            gla_pick(dve, dr, 7)
        dve.memset(gl_t, 0.0).then_inc(S("gl_og"), 1)
        dve.wait_ge(S("gl_pv"), 2)
        link(dve, "dve", dve.tensor_copy(gl_y, bank(7).rearrange("p (t c) -> p t c", t=NT)))
        link(dve, "dve", dve.tensor_tensor(gl_t, gl_y, gl_y, ALU.mult))
        dve.tensor_reduce(stat[:, 0, 0:8].rearrange("p (t h) -> p t h", t=2), gl_t.rearrange("p t (h e) -> p t h e", h=4),
                          X, ALU.add).then_inc(S("gl_ss"), 1)
        dve.wait_ge(S("gl_root"), 1)
        link(dve, "dve", dve.reciprocal(stat[:, 3, 0:8], stat[:, 1, 0:8]))
        dve.wait_ge(S("gl_silu"), 1)
        for t in range(NT):
            y3 = gl_y[:, t, :].rearrange("p (h e) -> p h e", h=4)
            link(dve, "dve", dve.tensor_tensor(y3, y3, bc(stat[:, 3, 4 * t:4 * t + 4], 2, 64), ALU.mult))
            link(dve, "dve", dve.tensor_tensor(gl_y[:, t, :], gl_y[:, t, :], vr("gla_norm_w"), ALU.mult))
            link(dve, "dve", dve.tensor_tensor(y_mix[:, t, 768:1024], gl_y[:, t, :], og_tok[:, t, :], ALU.mult))

    def gla_pick(dve, dr, n):
        dve.wait_ge(S("gl_sc"), 8 * dr + n + 1)
        mask = lev_masks[:, 7 * dr + n if n < 7 else 14, :]
        dve.copy_predicated(gl_acc, bc(bc(mask, 1, NT), 1, 4),
                            psum[:, 3:7, 0:SEQ].rearrange("p h (t i) -> p h t i", t=NT)
                            ).then_inc(S("gl_acc_n"), 1)

    def gla_pool(pool):
        for dr in range(2):
            for n in range(7):
                pool.wait_ge(S("gl_E_n"), 7 * dr + n + 1)
                if 8 * dr + n >= 2:
                    pool.wait_ge(S("gl_sc"), 8 * dr + n - 1)
                pool.tensor_tensor(gl_k[:, n % 2, :], gqkT[:, 1, CTX:ALL], gl_E[:, n % 2, :], ALU.mult
                                   ).then_inc(S("gl_k_n"), 1)

    MIX_MOVED = [sum(1 for m, _ in enumerate(mix_jobs()) if m % 2 == q) for q in range(2)]

    top[0] = stage_top
    tri = alloc(2, 9, P)
    gla_in = mem[:, stage_top - 9 * ALL - 8 * ALL - TILES * 16 - 3072:][:, 0:3072]
    xs_tok = gla_in[:, 0:2048].rearrange("p (t c) -> p t c", t=TILES)
    b_tok = gla_in[:, 2048:3072].rearrange("p (t c) -> p t c", t=TILES)
    dtv = alloc(TILES, 16)
    loga = alloc(TILES, 16)
    sp_t = alloc(4, 64)
    sums = alloc(2, 3, TILES, 8)
    esums = alloc(2, 3, TILES, 8)
    sd_sc = alloc(2, NT, 2, P)
    sd_L = alloc(8, P)
    sd_xdt = alloc(512)
    sd_xde = alloc(512)
    sd_h = alloc(3, 512)
    sd_y = alloc(NT, 512)
    sd_t = alloc(512)

    def ssd_pe(pe):
        for t in range(TILES):
            if t >= 2:
                pe.wait_ge(S("sd_turn_out"), 2 * (t - 1))
            for j in range(4):
                pe.transpose(bank(2 * (t % 2), P, j * P), xbcT[:, j, t * P:(t + 1) * P], ident)
            for j in range(2):
                ins = pe.transpose(bank(2 * (t % 2) + 1, P, j * P), xbcT[:, 4 + j, t * P:(t + 1) * P], ident)
            ins.then_inc(S("sd_turn"), 1)
        pe.wait_ge(S("sd_loga"), 1)
        for dr in range(2):
            for n, lhs in enumerate((C(f"cum{dr}"), C(f"rest{dr}"), C("ones"))):
                for t in range(TILES):
                    ins = pe.matmul(bank(4, 8, ((dr * 3 + n) * TILES + t) * 8), lhs, loga[:, t, dr * 8:dr * 8 + 8],
                                    start=True, stop=True)
        ins.then_inc(S("sd_sums"), 1)
        pe.wait_ge(S("sd_turn_out"), 2 * TILES)
        for t in range(NT):
            tok = slice(CTX + t * P, CTX + (t + 1) * P)
            for g in range(2):
                ins = pe.matmul(bank(2, P, (2 * t + g) * P), xbcT[:, 4 + g, tok], xbcT[:, 6 + g, tok], start=True,
                                stop=True)
        ins.then_inc(S("sd_scores"), 1)
        for dr in range(2):
            order = gla_order(dr)
            for k in range(3):
                m = 3 * dr + k
                pe.wait_ge(S("sd_xde_n"), m + 1)
                if m:
                    pe.wait_ge(S("sd_h_n"), m)
                for g in range(2):
                    ins = pe.matmul(bank(3, 256, g * 256), b_tok[:, order[k], g * P:(g + 1) * P],
                                    sd_xde[:, g * 256:(g + 1) * 256], start=True, stop=True)
                ins.then_inc(S("sd_adds"), 1)
            for k in range(2):
                t = order[2 + k] - 2
                m = 2 * dr + k
                tok = slice(CTX + t * P, CTX + (t + 1) * P)
                if m:
                    pe.wait_ge(S("sd_seg"), m)
                for h in range(8):
                    ins = pe.matmul(banks(0, 2)[:, h * P:(h + 1) * P],
                                    loga[:, 2 + t, dr * 8 + h:dr * 8 + h + 1].to_broadcast([P, P]), C(f"cum{dr}"),
                                    start=True, stop=True)
                ins.then_inc(S("sd_rows"), 1)
                if m:
                    pe.wait_ge(S("sd_off"), m)
                pe.wait_ge(S("sd_h_n"), 3 * dr + 2 + k)
                for g in range(2):
                    ins = pe.matmul(bank(7, 256, g * 256), xbcT[:, 6 + g, tok], sd_h[:, 1 + k, g * 256:(g + 1) * 256],
                                    start=True, stop=True)
                ins.then_inc(S("sd_inter"), 1)
                pe.wait_ge(S("sd_M"), m + 1)
                for h in range(8):
                    ins = pe.matmul(bank(5 + t, 64, h * 64), sd_L[:, h, :], sd_xdt[:, h * 64:(h + 1) * 64],
                                    start=dr == 0 and h == 0, stop=dr == 1, skip_group_check=True)
                ins.then_inc(S("sd_diag"), 1)

    def ssd_act(act):
        act.dma_start(tri.rearrange("p a b c -> p (a b c)"), d["tri_masks"]).then_inc(S("stage_in"), 16)
        act.activation(vr("a_log"), vr("a_log"), ACT.Exp).then_inc(S("sd_a"), 1)
        act.wait_ge(S("sd_na"), 1)
        act.activation(sp_t[:, 1, :], sp_t[:, 0, :], ACT.Exp).then_inc(S("sd_e"), 1)
        act.wait_ge(S("sd_u"), 1)
        act.activation(sp_t[:, 3, :], sp_t[:, 2, :], ACT.Ln).then_inc(S("sd_ln"), 1)
        for t in range(TILES):
            act.wait_ge(S("sd_turn"), t + 1)
            act.activation(xs_tok[:, t, :], bank(2 * (t % 2)), ACT.Copy).then_inc(S("sd_turn_out"), 1)
            act.activation(b_tok[:, t, :], bank(2 * (t % 2) + 1, 256), ACT.Copy).then_inc(S("sd_turn_out"), 1)
        act.wait_ge(S("sd_sums"), 1)
        act.activation(esums.rearrange("p a b c d -> p (a b c d)"), bank(4, 192), ACT.Exp).then_inc(S("sd_esums"), 1)
        for m in range(4):
            act.wait_ge(S("sd_seg"), m + 1)
            act.activation(sd_L, sd_L, ACT.Exp).then_inc(S("sd_L"), 1)
        act.activation(z_tok, z_tok, ACT.Silu).then_inc(S("sd_silu"), 1)
        act.wait_ge(S("sd_ss"), 1)
        act.activation(stat[:, 1, 0:4], stat[:, 0, 0:4], ACT.Sqrt, scale=1 / 256, bias=ln_eps).then_inc(S("sd_root"), 1)

    def ssd_dve(dve):
        def v(a):
            return a.rearrange("p a b -> p (a b)")

        link(dve, "dve", dve.tensor_tensor(dtv, dt_raw, bc(vr("dt_bias"), 1, TILES), ALU.add))
        dve.scalar_tensor_tensor(sp_t[:, 0, :], v(dtv), -1.0, v(dtv), ALU.mult, ALU.min).then_inc(S("sd_na"), 1)
        dve.wait_ge(S("sd_e"), 1)
        dve.tensor_scalar(sp_t[:, 2, :], sp_t[:, 1, :], 1.0, None, ALU.add).then_inc(S("sd_u"), 1)
        dve.wait_ge(S("sd_u"), 1)
        link(dve, "dve", dve.tensor_scalar(sp_t[:, 0, :], sp_t[:, 2, :], 1.0, None, ALU.is_equal))
        dve.wait_ge(S("sd_ln"), 1)
        link(dve, "dve", dve.tensor_tensor(sp_t[:, 3, :], sp_t[:, 3, :], sp_t[:, 0, :], ALU.add))
        link(dve, "dve", dve.scalar_tensor_tensor(sp_t[:, 2, :], sp_t[:, 2, :], 1.0, sp_t[:, 0, :], ALU.subtract, ALU.add))
        link(dve, "dve", dve.reciprocal(sp_t[:, 2, :], sp_t[:, 2, :]))
        link(dve, "dve", dve.tensor_tensor(sp_t[:, 3, :], sp_t[:, 3, :], sp_t[:, 2, :], ALU.mult))
        link(dve, "dve", dve.tensor_tensor(sp_t[:, 3, :], sp_t[:, 3, :], sp_t[:, 1, :], ALU.mult))
        link(dve, "dve", dve.scalar_tensor_tensor(v(dtv), v(dtv), 0.0, sp_t[:, 3, :], ALU.max, ALU.add))
        dve.wait_ge(S("sd_a"), 1)
        link(dve, "dve", dve.tensor_tensor(loga, dtv, bc(vr("a_log"), 1, TILES), ALU.mult))
        dve.tensor_scalar(v(loga), v(loga), -1.0, None, ALU.mult).then_inc(S("sd_loga"), 1)
        dve.wait_ge(S("sd_sums"), 1)
        dve.wait_ge(S("sd_esums"), 1)
        link(dve, "dve", dve.tensor_copy(sums.rearrange("p a b c d -> p (a b c d)"), bank(4, 192)))
        dve.wait_ge(S("stage_in"), 16 * 4)
        dve.wait_ge(S("sd_scores"), 1)
        for dr in range(2):
            for t in range(NT):
                link(dve, "dve", dve.tensor_tensor(sd_sc[:, dr, t, :, :], bank(2, 256, t * 256).rearrange("p (g i) -> p g i", g=2),
                                                   bc(tri[:, dr, 0, :], 1, 2), ALU.mult))
        dve.wait_ge(S("sd_turn_out"), 2 * TILES)
        off = gain_b.rearrange("p (t c) -> p t c", t=NT)
        for dr in range(2):
            order = gla_order(dr)

            def xdt(t, dst):
                link(dve, "dve", dve.tensor_tensor(dst.rearrange("p (h e) -> p h e", h=8),
                                                   xs_tok[:, t, :].rearrange("p (h e) -> p h e", h=8),
                                                   bc(dtv[:, t, dr * 8:dr * 8 + 8], 2, 64), ALU.mult))

            for k in range(3):
                m = 3 * dr + k
                t = order[k]
                if m:
                    dve.wait_ge(S("sd_adds"), m)
                xdt(t, sd_xde)
                dve.tensor_tensor(sd_xde.rearrange("p (h e) -> p h e", h=8), sd_xde.rearrange("p (h e) -> p h e", h=8),
                                  bc(esums[:, dr, 1, t, :], 2, 64), ALU.mult).then_inc(S("sd_xde_n"), 1)
                dve.wait_ge(S("sd_adds"), m + 1)
                if k == 0:
                    if dr:
                        dve.wait_ge(S("sd_inter"), 2)
                    dve.tensor_copy(sd_h[:, 0, :], bank(3)).then_inc(S("sd_h_n"), 1)
                else:
                    link(dve, "dve", dve.tensor_tensor(sd_t.rearrange("p (h e) -> p h e", h=8),
                                                       sd_h[:, k - 1, :].rearrange("p (h e) -> p h e", h=8),
                                                       bc(esums[:, dr, 2, t, :], 2, 64), ALU.mult))
                    dve.tensor_tensor(sd_h[:, k, :], sd_t, bank(3), ALU.add).then_inc(S("sd_h_n"), 1)
                dve.wait_ge(S("sd_h_n"), m + 1)
            for k in range(2):
                t = order[2 + k] - 2
                m = 2 * dr + k
                dve.wait_ge(S("sd_rows"), m + 1)
                if m:
                    dve.wait_ge(S("sd_diag"), m)
                link(dve, "dve", dve.tensor_tensor(sd_L, banks(0, 2).rearrange("p (h i) -> p h i", h=8),
                                                   bc(sums[:, dr, 0, 2 + t, :], 2, P), ALU.subtract))
                dve.tensor_scalar(sd_L, sd_L, 0.0, None, ALU.min).then_inc(S("sd_seg"), 1)
                xdt(2 + t, sd_xdt)
                dve.wait_ge(S("sd_inter"), m + 1)
                o3 = off[:, t, :].rearrange("p (h e) -> p h e", h=8)
                src = bank(7).rearrange("p (h e) -> p h e", h=8)
                e3 = bc(esums[:, dr, 0, 2 + t, :], 2, 64)
                if dr == 0:
                    dve.tensor_tensor(o3, src, e3, ALU.mult).then_inc(S("sd_off"), 1)
                    dve.wait_ge(S("sd_off"), m + 1)
                else:
                    dve.tensor_tensor(sd_t.rearrange("p (h e) -> p h e", h=8), src, e3, ALU.mult).then_inc(S("sd_off"), 1)
                    dve.wait_ge(S("sd_off"), m + 1)
                    link(dve, "dve", dve.tensor_tensor(off[:, t, :], off[:, t, :], sd_t, ALU.add))
                dve.wait_ge(S("sd_L"), m + 1)
                for g in range(2):
                    ins = dve.tensor_tensor(sd_L[:, 4 * g:4 * g + 4, :], sd_L[:, 4 * g:4 * g + 4, :],
                                            bc(sd_sc[:, dr, t, g, :], 1, 4), ALU.mult)
                ins.then_inc(S("sd_M"), 1)
        dve.wait_ge(S("sd_diag"), 4)
        dve.wait_ge(S("sd_silu"), 1)
        for t in range(NT):
            y, y3 = sd_y[:, t, :], sd_y[:, t, :].rearrange("p (h e) -> p h e", h=8)
            link(dve, "dve", dve.tensor_tensor(y3, xs_tok[:, 2 + t, :].rearrange("p (h e) -> p h e", h=8),
                                               bc(vr("ssd_d"), 2, 64), ALU.mult))
            link(dve, "dve", dve.tensor_tensor(y, y, bank(5 + t), ALU.add))
            link(dve, "dve", dve.tensor_tensor(y, y, off[:, t, :], ALU.add))
            link(dve, "dve", dve.tensor_tensor(y, y, z_tok[:, t, :], ALU.mult))
            link(dve, "dve", dve.tensor_tensor(sd_t, y, y, ALU.mult))
            ins = dve.tensor_reduce(stat[:, 0, 2 * t:2 * t + 2], sd_t.rearrange("p (g e) -> p g e", g=2), X, ALU.add)
            if t:
                ins.then_inc(S("sd_ss"), 1)
            else:
                link(dve, "dve", ins)
        dve.wait_ge(S("sd_root"), 1)
        link(dve, "dve", dve.reciprocal(stat[:, 3, 0:4], stat[:, 1, 0:4]))
        for t in range(NT):
            y2 = sd_y[:, t, :].rearrange("p (g e) -> p g e", g=2)
            link(dve, "dve", dve.tensor_tensor(y2, y2, bc(stat[:, 3, 2 * t:2 * t + 2], 2, 256), ALU.mult))
            link(dve, "dve", dve.tensor_tensor(y_mix[:, t, 0:512], sd_y[:, t, :], vr("ssd_norm_w"), ALU.mult))

    top[0] = stage_top - 8 * ALL - TILES * 16 - NT * 256 - ALL - TILES * 256 - 2 * ALL - NT * 512 - 9 * ALL
    rwkv_bottom = top[0]
    rk = rwT
    low_end = stage_top - 9 * ALL
    kkT = alloc(2, ALL)
    v_t = alloc(TILES, 256)
    khT = alloc(2, ALL)
    rhT = alloc(2, SEQ)
    btok = alloc(TILES, 256)
    ktok = alloc(TILES, 256)
    w1 = alloc(TILES, 256)
    arb = alloc(NT, 4, P)
    bonusT = alloc(2, SEQ)
    assert top[0] <= low_end, (top[0], low_end)
    top[0] = stage_top
    tt = alloc(TILES, 4, P)
    ab = alloc(TILES, 4, P)
    tf = alloc(TILES, 4, P)
    xf = alloc(2, 4, P)
    bT, kT2 = (tf.rearrange("p a b c -> p (a b c)")[:, n * 1024:(n + 1) * 1024].rearrange("p (a b) -> p a b", a=2)
               for n in range(2))
    lw = ab.rearrange("p a b c -> p (a b c)")[:, 0:1024].rearrange("p (t c) -> p t c", t=TILES)
    aTt = ab.rearrange("p a b c -> p (a b c)")[:, 1024:2048].rearrange("p (a b) -> p a b", a=2)
    spare = aT.rearrange("p a b -> p (a b)")
    ex = spare[:, 0:1024].rearrange("p (a b) -> p a b", a=2)
    uu = spare[:, 0:1024].rearrange("p (t c) -> p t c", t=TILES)
    akm = spare[:, 1024:1536].rearrange("p (h i) -> p h i", h=4)
    st = spare[:, 1536:1792].rearrange("p (a b) -> p a b", a=2)
    ur = spare[:, 1792:2048]
    lmask = alloc(2, 4, P)
    tri2 = alloc(9, P)
    dcol = alloc(2, TILES, 4)
    dec = alloc(2, 8)
    rk_g = gain_b[:, 0:512].rearrange("p (t c) -> p t c", t=NT)
    yk = gate_act.rearrange("p (t c) -> p t c", t=NT)
    yk2 = hid.rearrange("p a b -> p (a b)")[:, 0:512].rearrange("p (t c) -> p t c", t=NT)
    bon = alloc(NT, 4)

    def rwkv_once_pe(pe):
        pe.wait_ge(S("rk_sq"), 1)
        for p2 in range(2):
            ins = pe.matmul(bank(p2), C("head_sum"), khT[:, p2, :], start=True, stop=True)
        ins.then_inc(S("rk_ss"), 1)
        for t in range(TILES):
            for j in range(2):
                ins = pe.transpose(bank(2 + t // 2, P, (t % 2) * 256 + j * P), rk[:, 4 + j, t * P:(t + 1) * P], ident)
        ins.then_inc(S("rk_v"), 1)
        pe.wait_ge(S("rk_sig"), 1)
        for t in range(NT):
            ins = pe.matmul(bank(4, 256, t * 256), rk[:, 8, CTX + t * P:CTX + (t + 1) * P], mats[:, 2, :], start=True,
                            stop=True)
        ins.then_inc(S("rk_gate"), 1)

    def rwkv_once_act(act):
        act.activation(rk[:, 6, :], rk[:, 6, :], ACT.Tanh).then_inc(S("rk_tanh"), 1)
        act.activation(rk[:, 8, CTX:ALL], rk[:, 8, CTX:ALL], ACT.Sigmoid).then_inc(S("rk_sig"), 1)
        act.wait_ge(S("rk_v"), 1)
        act.activation(v_t, psum[:, 2:4, :].rearrange("p b (t c) -> p (b t) c", t=2), ACT.Copy).then_inc(S("rk_vt"), 1)
        act.wait_ge(S("rk_gate"), 1)
        act.activation(rk_g, bank(4).rearrange("p (t c) -> p t c", t=NT), ACT.Copy).then_inc(S("rk_vt"), 1)
        act.wait_ge(S("rk_ss"), 1)
        for p2 in range(2):
            ins = act.activation(khT[:, p2, :], bank(p2), ACT.Sqrt)
        ins.then_inc(S("rk_norm"), 1)

    def rwkv_once_dve(dve):
        for p2 in range(2):
            ins = dve.tensor_scalar(kkT[:, p2, :], rk[:, 2 + p2, :], vc("rwkv_kk")[:, p2:p2 + 1], None, ALU.mult)
            link(dve, "dve", ins)
        dve.tensor_tensor(khT, kkT, kkT, ALU.mult).then_inc(S("rk_sq"), 1)
        link(dve, "dve", dve.tensor_scalar(vc("one_less_ka"), vc("rwkv_ka"), -1.0, 1.0, ALU.mult, ALU.add))
        dve.wait_ge(S("rk_norm"), 1)
        link(dve, "dve", dve.tensor_scalar(khT, khT, 1e-12, None, ALU.max))
        link(dve, "dve", dve.reciprocal(khT, khT))
        link(dve, "dve", dve.tensor_tensor(kkT, kkT, khT, ALU.mult))

    def order8(dr):
        g = list(range(8)) if dr == 0 else [3, 2, 1, 0, 7, 6, 5, 4]
        return [divmod(c, 2) for c in g]

    def rwkv_pe(pe, dr):
        r64 = slice(64 * dr, 64 * dr + 64)
        if dr == 0:
            pe.wait_ge(S("rk_tanh"), 1)
        for t in range(TILES):
            ins = pe.matmul(bank(t // 2, 256, (t % 2) * 256), rk[r64, 6, t * P:(t + 1) * P], mats[r64, 0, :],
                            start=True, stop=True)
        ins.then_inc(S("rk_z"), 1)
        for p2 in range(2):
            ins = pe.matmul(bank(2 + p2), mats[r64, 1, p2 * P:(p2 + 1) * P], rk[r64, 7, :], start=True, stop=True)
        ins.then_inc(S("rk_za"), 1)
        pe.wait_ge(S("rk_lw"), dr + 1)
        lead, n_lead = names[f"rk_tail{dr}"][0], 4
        for p2 in range(2):
            for kind, b in (("inc", 4), ("exc", 0)):
                for t in range(TILES):
                    ins = pe.matmul(bank(b + p2, P, t * P), lw[:, t, p2 * P:(p2 + 1) * P], C(f"rk_{kind}{dr}"),
                                    start=True, stop=True)
            for t in range(TILES):
                ins = pe.matmul(bank(6, 4, (p2 * TILES + t) * 4), lw[:, t, p2 * P:(p2 + 1) * P],
                                cst[:, lead:lead + 4], start=True, stop=True)
        ins.then_inc(S("rk_c"), 1)
        pe.wait_ge(S("rk_bk"), dr + 1)
        for n, (src, b) in enumerate(((bT, 0), (kT2, 2))):
            for t in range(TILES):
                for j in range(2):
                    ins = pe.transpose(bank(b + t // 2, P, (t % 2) * 256 + j * P), src[:, j, t * P:(t + 1) * P], ident)
            ins.then_inc(S("rk_turn"), 1)
        pe.wait_ge(S("rk_turned"), 2 * dr + 2)
        q = 0
        for t in range(TILES):
            kinds = ("b", "k") + (("rb", "rk") if t >= 2 else ())
            for kind in kinds:
                m = 12 * dr + q
                if m % 12 >= 2 or dr:
                    pe.wait_ge(S("rk_A_out"), m - 1)
                for h in range(4):
                    r, p2 = slice(64 * (h % 2), 64 * (h % 2) + 64), h // 2
                    lhs = (bT if kind in ("b", "rb") else kT2)[r, p2, t * P:(t + 1) * P]
                    rhs = khT[r, p2, t * P:(t + 1) * P] if kind in ("b", "k") else rhT[r, p2, (t - 2) * P:(t - 1) * P]
                    ins = pe.matmul(bank((4, 0)[q % 2] + h % 2, P, (h // 2) * P), lhs, rhs, start=True, stop=True)
                ins.then_inc(S("rk_A"), 1)
                q += 1
                if kind in ("k", "rk"):
                    if kind == "k" and 4 * dr + t:
                        pe.wait_ge(S("rk_w1"), 4 * dr + t)
                    pe.wait_ge(S("rk_A_out"), m + 1)
                    for h in range(4):
                        if kind == "k":
                            o, start, stop = bank(6, 64, h * 64), True, True
                        else:
                            o = bank(7, 64, (t - 2) * 256 + h * 64)
                            start, stop = dr == 0 and t == 2 and h == 0, False
                        ins = pe.matmul(o, akm[:, h, :], v_t[:, t, h * 64:(h + 1) * 64], start=start, stop=stop,
                                        skip_group_check=True)
                    ins.then_inc(S("rk_AV"), 1)
        for n in range(6):
            for t in range(TILES):
                m = 24 * dr + 4 * n + t
                pe.wait_ge(S("rk_L"), m + 1)
                pe.wait_ge(S("rk_T"), 28 * dr + 4 * n + t + 1)
                if m % 24 >= 2 or dr:
                    pe.wait_ge(S("rk_X"), m - 1)
                for h in range(4):
                    ins = pe.matmul(bank(t % 2, P, h * P), lmask[:, t % 2, h, :], tf[:, t, h, :], start=True, stop=True)
                ins.then_inc(S("rk_Xp"), 1)
                if t >= 1:
                    rwkv_double(pe, dr, n, t - 1)
            rwkv_double(pe, dr, n, 3)
        for k, (t, c) in enumerate(order8(dr)):
            m = 8 * dr + k
            rows = slice(64 * c, 64 * c + 64)
            pe.wait_ge(S("rk_T"), 28 * dr + 28)
            pe.wait_ge(S("rk_state"), 9 * dr + k + 1)
            for p2 in range(2):
                ins = pe.matmul(bank(0, P, p2 * P), khT[:, p2, t * P:(t + 1) * P], st[:, p2, :], start=True, stop=True)
            ins.then_inc(S("rk_ks"), 1)
            if t >= 2:
                for p2 in range(2):
                    ins = pe.matmul(psum[rows, 7, (t - 2) * 256 + p2 * P:(t - 2) * 256 + (p2 + 1) * P],
                                    rhT[:, p2, (t - 2) * P + 64 * c:(t - 2) * P + 64 * c + 64], st[:, p2, :],
                                    start=False, stop=False, skip_group_check=True)
                ins.then_inc(S("rk_rs"), 1)
            last = k == 7
            if not last:
                for p2 in range(2):
                    pe.matmul(bank(2, P, p2 * P), ktok[rows, t, p2 * P:(p2 + 1) * P], v_t[rows, t, p2 * P:(p2 + 1) * P],
                              start=p2 == 0, stop=False, skip_group_check=True)
            pe.wait_ge(S("rk_r"), m + 1)
            for h in range(4):
                ins = pe.matmul(bank(1, 64, h * 64), tt[rows, t, h, :], ur[rows, h * 64:(h + 1) * 64], start=True,
                                stop=True)
            ins.then_inc(S("rk_u"), 1)
            pe.wait_ge(S("rk_uu"), m + 1)
            if not last:
                for p2 in range(2):
                    ins = pe.matmul(bank(2, P, p2 * P), btok[rows, t, p2 * P:(p2 + 1) * P],
                                    uu[rows, t, p2 * P:(p2 + 1) * P], start=False, stop=p2 == 1, skip_group_check=True)
                ins.then_inc(S("rk_add"), 1)
            if t >= 2 and k in (5, 7):
                for h in range(4):
                    ins = pe.matmul(bank(7, 64, (t - 2) * 256 + h * 64), arb[:, t - 2, h, :],
                                    uu[:, t, h * 64:(h + 1) * 64], start=False, stop=dr == 1 and k == 7,
                                    skip_group_check=True)
                ins.then_inc(S("rk_y"), 1)
        if dr == 1:
            for t in range(NT):
                for p2 in range(2):
                    ins = pe.matmul(bank(3, 2, t * 4 + p2 * 2), bonusT[:, p2, t * P:(t + 1) * P], C("head_cols"),
                                    start=True, stop=True)
            ins.then_inc(S("rk_bon"), 1)

    def rwkv_double(pe, dr, n, t):
        m = 24 * dr + 4 * n + t
        pe.wait_ge(S("rk_X"), m + 1)
        if m % 24 >= 2 or dr:
            pe.wait_ge(S("rk_T"), 28 * dr + (4 if m % 24 else 0) + max(m % 24 - 1, 0))
        for h in range(4):
            ins = pe.matmul(bank(2 + t % 2, P, h * P), xf[:, t % 2, h, :], tt[:, t, h, :], start=True, stop=True)
        if n < 5:
            for h in range(4):
                ins = pe.matmul(bank(4 + t % 2, P, h * P), tt[:, t, h, :], xf[:, t % 2, h, :], start=True, stop=True)
        ins.then_inc(S("rk_dT"), 1)

    def rwkv_act(act, dr):
        if dr == 0:
            act.wait_ge(S("rk_tri_free"), 1)
        act.dma_start(tri2.rearrange("p a b -> p (a b)"), d["tri_masks"][:, dr * 9 * P:(dr + 1) * 9 * P]
                      ).then_inc(S("rk_tri"), 16)
        act.wait_ge(S("rk_zb"), dr + 1)
        act.activation(lw, lw, ACT.Sigmoid).then_inc(S("rk_lw"), 1)
        act.wait_ge(S("rk_za"), dr + 1)
        for p2 in range(2):
            ins = act.activation(aTt[:, p2, :], bank(2 + p2), ACT.Sigmoid, bias=vc("rwkv_a0")[:, 2 * dr + p2:2 * dr + p2 + 1])
        ins.then_inc(S("rk_a"), 1)
        act.wait_ge(S("rk_c"), dr + 1)
        act.activation(dcol.rearrange("p a b c -> p (a b c)"), bank(6, 32), ACT.Exp, scale=-KAPPA).then_inc(S("rk_E"), 1)
        act.activation(khT, psum[:, 0:2, :], ACT.Exp, scale=-KAPPA).then_inc(S("rk_E"), 1)
        act.activation(rhT, psum[:, 4:6, CTX:ALL], ACT.Exp, scale=-KAPPA).then_inc(S("rk_E"), 1)
        act.activation(ex, psum[:, 4:6, :], ACT.Exp, scale=KAPPA).then_inc(S("rk_E"), 1)
        for n, (dst, b) in enumerate(((btok, 0), (ktok, 2))):
            act.wait_ge(S("rk_turn"), 2 * dr + n + 1)
            act.activation(dst, psum[:, b:b + 2, :].rearrange("p b (t c) -> p (b t) c", t=2), ACT.Copy
                           ).then_inc(S("rk_turned"), 1)
        done = 6 * dr
        for t in range(TILES):
            done += 1
            act.wait_ge(S("rk_AV"), done)
            act.activation(w1[:, t, :], bank(6, 256), ACT.Copy).then_inc(S("rk_w1"), 1)
            if t >= 2:
                done += 1
        for n in range(6):
            for t in range(TILES):
                m = 24 * dr + 4 * n + t
                act.wait_ge(S("rk_Xp"), m + 1)
                if m >= 2:
                    act.wait_ge(S("rk_dT"), m - 1)
                act.activation(xf[:, t % 2, :, :], bank(t % 2).rearrange("p (h i) -> p h i", h=4), ACT.Copy
                               ).then_inc(S("rk_X"), 1)

    def rwkv_pool(pool, dr):
        pool.wait_ge(S("rk_tri"), 16 * (dr + 1))
        for n in range(6):
            for t in range(TILES):
                m = 24 * dr + 4 * n + t
                pool.wait_ge(S("rk_ab"), 4 * dr + t + 1)
                if m >= 2:
                    pool.wait_ge(S("rk_Xp"), m - 1)
                pool.tensor_tensor(lmask[:, t % 2, :, :], ab[:, t, :, :], bc(tri2[:, 3 + n, :], 1, 4), ALU.mult
                                   ).then_inc(S("rk_L"), 1)

    def rwkv_dve(dve, dr):
        if dr == 0:
            dve.memset(bon, 0.0).then_inc(S("rk_tri_free"), 1)
        dve.wait_ge(S("rk_z"), dr + 1)
        dve.tensor_tensor(lw, psum[:, 0:2, :].rearrange("p b (t c) -> p (b t) c", t=2),
                          bc(vr("rwkv_w0")[:, dr * 256:dr * 256 + 256], 1, TILES), ALU.add).then_inc(S("rk_zb"), 1)
        dve.wait_ge(S("rk_a"), dr + 1)
        dve.wait_ge(S("rk_E"), 4 * dr + 4)
        link(dve, "dve", dve.tensor_tensor(khT, khT, kkT, ALU.mult))
        link(dve, "dve", dve.tensor_tensor(rhT, rhT, rk[:, 0:2, CTX:ALL], ALU.mult))
        for p2 in range(2):
            link(dve, "dve", dve.tensor_scalar(kT2[:, p2, :], aTt[:, p2, :], vc("rwkv_ka")[:, p2:p2 + 1],
                                               vc("one_less_ka")[:, p2:p2 + 1], ALU.mult, ALU.add))
        link(dve, "dve", dve.tensor_tensor(kT2, kT2, rk[:, 2:4, :], ALU.mult))
        if dr == 0:
            link(dve, "dve", dve.tensor_copy(bonusT, kT2[:, :, CTX:ALL]))
        else:
            link(dve, "dve", dve.tensor_tensor(bonusT, bonusT, kT2[:, :, CTX:ALL], ALU.add))
            for p2 in range(2):
                link(dve, "dve", dve.scalar_tensor_tensor(bonusT[:, p2, :], bonusT[:, p2, :], vc("rwkv_rk")[:, p2:p2 + 1],
                                                          rk[:, p2, CTX:ALL], ALU.mult, ALU.mult))
        link(dve, "dve", dve.tensor_tensor(bT, kkT, aTt, ALU.mult))
        link(dve, "dve", dve.tensor_tensor(kT2, kT2, ex, ALU.mult))
        dve.tensor_tensor(bT, bT, ex, ALU.mult).then_inc(S("rk_bk"), 1)
        for k, ((t, c), (t2, c2)) in enumerate(zip(order8(dr)[:-1], order8(dr)[1:])):
            ins = dve.tensor_tensor(dec[:, :, k:k + 1], dcol[:, :, t, c:c + 1], dcol[:, :, t2, 2 + c2:3 + c2], ALU.mult)
        link(dve, "dve", ins)
        link(dve, "dve", dve.memset(uu, 0.0))
        dve.wait_ge(S("rk_tri"), 16 * (dr + 1))
        q = 0
        av = 6 * dr
        for t in range(TILES):
            for kind in ("b", "k") + (("rb", "rk") if t >= 2 else ()):
                dve.wait_ge(S("rk_A"), 12 * dr + q + 1)
                b0 = (4, 0)[q % 2]
                src = psum[:, b0:b0 + 2, 0:SEQ].rearrange("p b (a i) -> p a b i", a=2)
                dst, mask = {"b": (ab[:, t, :, :], 2), "k": (akm, 2), "rb": (arb[:, max(t - 2, 0), :, :], 1),
                             "rk": (akm, 1)}[kind]
                if kind in ("k", "rk"):
                    if av:
                        dve.wait_ge(S("rk_AV"), av)
                    av += 1
                dve.tensor_tensor(dst.rearrange("p (a b) i -> p a b i", a=2), src,
                                  bc(bc(tri2[:, mask, :], 1, 2), 1, 2), ALU.mult).then_inc(S("rk_A_out"), 1)
                if kind == "b":
                    dve.wait_ge(S("rk_A_out"), 12 * dr + q + 1)
                    dve.tensor_copy(tt[:, t, :, :], bc(ident, 1, 4)).then_inc(S("rk_ab"), 1)
                q += 1
        dve.wait_ge(S("rk_A"), 12 * dr + 12)
        for t in range(TILES):
            dve.tensor_copy(tf[:, t, :, :], bc(ident, 1, 4)).then_inc(S("rk_T"), 1)
        for n in range(6):
            for t in range(TILES):
                m = 24 * dr + 4 * n + t
                dve.wait_ge(S("rk_dT"), m + 1)
                o = tt[:, t, :, :]
                if n == 5:
                    dve.tensor_tensor(o, o, bank(2 + t % 2).rearrange("p (h i) -> p h i", h=4), ALU.subtract
                                      ).then_inc(S("rk_T"), 1)
                else:
                    dve.tensor_tensor(o, o, bank(2 + t % 2).rearrange("p (h i) -> p h i", h=4), ALU.subtract)
                    o = tf[:, t, :, :]
                    dve.tensor_tensor(o, o, bank(4 + t % 2).rearrange("p (h i) -> p h i", h=4), ALU.subtract
                                      ).then_inc(S("rk_T"), 1)
        dve.wait_ge(S("rk_w1"), 4 * dr + 4)
        dve.memset(st, 0.0).then_inc(S("rk_state"), 1)
        for k, (t, c) in enumerate(order8(dr)):
            m = 8 * dr + k
            rows = slice(64 * c, 64 * c + 64)
            dve.wait_ge(S("rk_ks"), m + 1)
            dve.tensor_tensor(ur[rows, :], psum[rows, 0, 0:256], w1[rows, t, :], ALU.add).then_inc(S("rk_r"), 1)
            dve.wait_ge(S("rk_u"), m + 1)
            dve.tensor_scalar(uu[rows, t, :], psum[rows, 1, 0:256], -1.0, None, ALU.mult).then_inc(S("rk_uu"), 1)
            if k < 7:
                dve.wait_ge(S("rk_add"), 7 * dr + k + 1)
                if t >= 2:
                    dve.wait_ge(S("rk_rs"), 4 * dr + k - 3)
                for hf in range(2):
                    r = slice(64 * hf, 64 * hf + 64)
                    s3 = st[r, :, 64 * hf:64 * hf + 64]
                    link(dve, "dve", dve.tensor_tensor(s3, s3, psum[r, 2, 0:256].rearrange("p (a b) -> p a b", a=2)[
                        :, :, 64 * hf:64 * hf + 64], ALU.add))
                    ins = dve.tensor_tensor(s3, s3, bc(dec[r, :, k:k + 1].rearrange("p a k -> p (a k)"), 2, 64), ALU.mult)
                ins.then_inc(S("rk_state"), 1)
            else:
                dve.memset(ur[:, 0:1], 0.0).then_inc(S("rk_state"), 1)

    def rwkv_end_act(act):
        act.wait_ge(S("rk_var"), 1)
        act.activation(stat[:, 1, 0:8], stat[:, 2, 0:8], ACT.Sqrt, scale=1 / 64, bias=lnx_eps).then_inc(S("rk_root"), 1)

    def rwkv_end_dve(dve):
        dve.wait_ge(S("rk_y"), 4)
        dve.wait_ge(S("rk_bon"), 1)
        y4 = yk.rearrange("p t (h e) -> p (t h) e", h=4)
        link(dve, "dve", dve.tensor_copy(yk, bank(7).rearrange("p (t c) -> p t c", t=NT)))
        link(dve, "dve", dve.tensor_reduce(stat[:, 0, 0:8], y4, X, ALU.add))
        link(dve, "dve", dve.tensor_scalar(stat[:, 0, 0:8], stat[:, 0, 0:8], -1 / 64, None, ALU.mult))
        link(dve, "dve", dve.tensor_tensor(y4, y4, bc(stat[:, 0, 0:8], 2, 64), ALU.add))
        link(dve, "dve", dve.tensor_tensor(yk2, yk, yk, ALU.mult))
        dve.tensor_reduce(stat[:, 2, 0:8], yk2.rearrange("p t (h e) -> p (t h) e", h=4), X, ALU.add
                          ).then_inc(S("rk_var"), 1)
        dve.wait_ge(S("rk_root"), 1)
        link(dve, "dve", dve.reciprocal(stat[:, 3, 0:8], stat[:, 1, 0:8]))
        link(dve, "dve", dve.tensor_tensor(y4, y4, bc(stat[:, 3, 0:8], 2, 64), ALU.mult))
        link(dve, "dve", dve.tensor_tensor(yk, yk, bc(vr("lnx_w"), 1, NT), ALU.mult))
        link(dve, "dve", dve.tensor_tensor(yk, yk, bc(vr("lnx_b"), 1, NT), ALU.add))
        link(dve, "dve", dve.tensor_copy(bon, bank(3, 8).rearrange("p (t h) -> p t h", t=NT)))
        for t in range(NT):
            link(dve, "dve", dve.tensor_tensor(yk2[:, t, :].rearrange("p (h e) -> p h e", h=4),
                                               v_t[:, 2 + t, :].rearrange("p (h e) -> p h e", h=4),
                                               bc(bon[:, t, :], 2, 64), ALU.mult))
        link(dve, "dve", dve.tensor_tensor(yk, yk, yk2, ALU.add))
        link(dve, "dve", dve.tensor_tensor(y_mix[:, :, 512:768], yk, rk_g, ALU.mult))

    top[0] = stage_top - 9 * ALL
    ln_w = alloc(D)
    ln_b = alloc(D)
    router_w = alloc(KC, EXPERTS)
    scores = alloc(NT, EXPERTS)
    sel = alloc(NT, EXPERTS)
    picked = alloc(NT, EXPERTS)
    g8 = alloc(NT, EGROUPS, 8)
    gs = alloc(NT, EGROUPS)
    gr = alloc(NT, 64)
    g_eq = alloc(NT, 64)
    g_in = alloc(NT, EGROUPS)
    g_out = alloc(NT, EGROUPS)
    t8 = alloc(NT, 8)
    w_sum = alloc(NT)
    gate = alloc(NT, EXPERTS + 1)
    gate_diag = alloc(SEQ)

    MOE = W_OUT + 4

    def ln_load(act, k):
        for dst, n in ((ln_w, f"ln{k + 1}_w_2"), (ln_b, f"ln{k + 1}_b_2")):
            act.dma_start(dst, d[n].to_broadcast([P, D])).then_inc(S("ln_rows"), 16)

    def out_ln_act(act, k):
        act.wait_ge(S("row_var"), k + 1)
        act.activation(stat[:, 1, 0:NT], stat[:, 0, 0:2 * NT].rearrange("p (t s) -> p t s", s=2)[:, :, 1], ACT.Sqrt,
                       bias=ln_eps).then_inc(S("row_root"), 1)

    def out_ln_dve(dve, k, g_b):
        for t in range(NT):
            link(dve, "dve", dve.tensor_tensor(xn[:, t, :], banks(4 + 2 * t, 2), g_b, ALU.mult))
            link(dve, "dve", dve.scalar_tensor_tensor(xn[:, t, :], x_tok[:, t, :], DN_ALPHA, xn[:, t, :], ALU.mult,
                                                      ALU.add))
            for h in range(2):
                link(dve, "dve", dve.bn_stats(stat[:, 2, 12 * t + 6 * h:12 * t + 6 * h + 6],
                                              xn[:, t, 512 * h:512 * h + 512]))
        link(dve, "dve", dve.bn_aggr(stat[:, 0, 0:2], stat[:, 2, 0:12]))
        dve.bn_aggr(stat[:, 0, 2:4], stat[:, 2, 12:24]).then_inc(S("row_var"), 1)
        dve.wait_ge(S("row_root"), k + 1)
        link(dve, "dve", dve.reciprocal(stat[:, 3, 0:NT], stat[:, 1, 0:NT]))
        dve.wait_ge(S("ln_rows"), 32 * (k + 1))
        for t in range(NT):
            x = x_tok[:, t, :]
            link(dve, "dve", dve.tensor_scalar(x, xn[:, t, :], stat[:, 0, 2 * t:2 * t + 1], stat[:, 3, t:t + 1],
                                               ALU.subtract, ALU.mult))
            link(dve, "dve", dve.tensor_tensor(x, x, ln_w, ALU.mult))
            ins = dve.tensor_tensor(x, x, ln_b, ALU.add)
            link(dve, "dve", ins)

    def router_pe(pe):
        pe.wait_ge(S("norm_T"), KC * 7)
        pe.wait_ge(S("router_in"), 16)
        for t in range(NT):
            for c in range(KC):
                ins = pe.matmul(bank(3, EXPERTS, t * EXPERTS), aT[:, c, t * P:(t + 1) * P], router_w[:, c, :],
                                start=c == 0, stop=c == KC - 1)
        ins.then_inc(S("routed"), 1)

    def router_act(act):
        act.wait_ge(S("routed"), 1)
        act.activation(scores, bank(3, NT * EXPERTS).rearrange("p (t e) -> p t e", t=NT), ACT.Sigmoid
                       ).then_inc(S("router_scores"), 1)

    def router_dve(dve):
        link(dve, "dve", dve.memset(gate, 0.0))
        dve.wait_ge(S("router_scores"), 1)
        link(dve, "dve", dve.tensor_tensor(sel, scores, bc(vr("router_b"), 1, NT), ALU.add))
        for t in range(NT):
            for g in range(EGROUPS):
                ins = dve.max(g8[:, t, g, :], sel[:, t, 8 * g:8 * g + 8])
        link(dve, "dve", ins)
        link(dve, "dve", dve.tensor_tensor(gs, g8[:, :, :, 0], g8[:, :, :, 1], ALU.add))
        for t in range(NT):
            other, own = bc(gs[:, t, :], 1, 8), bc(gs[:, t, :], 2, 8)
            r3, e3 = (a[:, t, :].rearrange("p (g o) -> p g o", g=8) for a in (gr, g_eq))
            link(dve, "dve", dve.tensor_tensor(r3, other, own, ALU.is_gt))
            link(dve, "dve", dve.tensor_tensor(e3, other, own, ALU.is_equal))
            link(dve, "dve", dve.tensor_tensor(g_eq[:, t, :], g_eq[:, t, :], C("below8"), ALU.mult))
            link(dve, "dve", dve.tensor_tensor(gr[:, t, :], gr[:, t, :], g_eq[:, t, :], ALU.add))
            link(dve, "dve", dve.tensor_reduce(g_in[:, t, :], r3, X, ALU.add))
            link(dve, "dve", dve.tensor_scalar(g_in[:, t, :], g_in[:, t, :], TOP_GROUPS - 0.5, None, ALU.is_lt))
            link(dve, "dve", dve.tensor_scalar(g_out[:, t, :], g_in[:, t, :], -1.0, 1e30, ALU.add, ALU.mult))
            s3 = sel[:, t, :].rearrange("p (g o) -> p g o", g=8)
            link(dve, "dve", dve.tensor_tensor(s3, s3, bc(g_in[:, t, :], 2, 8), ALU.mult))
            link(dve, "dve", dve.tensor_tensor(s3, s3, bc(g_out[:, t, :], 2, 8), ALU.add))
            link(dve, "dve", dve.max(t8[:, t, :], sel[:, t, :]))
            link(dve, "dve", dve.match_replace(picked[:, t, :], t8[:, t, :], sel[:, t, :], -3e38))
            link(dve, "dve", dve.tensor_tensor(picked[:, t, :], picked[:, t, :], sel[:, t, :], ALU.not_equal))
            link(dve, "dve", dve.tensor_tensor(picked[:, t, :], picked[:, t, :], scores[:, t, :], ALU.mult))
            link(dve, "dve", dve.tensor_reduce(w_sum[:, t:t + 1], picked[:, t, :], X, ALU.add))
            link(dve, "dve", dve.reciprocal(w_sum[:, t:t + 1], w_sum[:, t:t + 1]))
            link(dve, "dve", dve.tensor_scalar(gate[:, t, 0:EXPERTS], picked[:, t, :], w_sum[:, t:t + 1], ROUTED_SCALE,
                                               ALU.mult, ALU.mult))

    def moe_sp(sp):
        def up(e):
            if isinstance(e, int) and e == 0:
                return [d[n][0].rearrange("(p c) n -> p c n", p=P) for n in ("sh_w1_2", "sh_w3_2")]
            return [d[n][0, bass.ds(e - 1, 1)].rearrange("e (p c) n -> (e p) c n", p=P) for n in ("exp_w1_2", "exp_w3_2")]

        def down(e):
            if isinstance(e, int) and e == 0:
                return d["sh_w2_2"][0].rearrange("(p c) n -> p c n", p=P)
            return d["exp_w2_2"][0, bass.ds(e - 1, 1)].rearrange("e (p c) n -> (e p) c n", p=P)

        experts_sp(sp, EXPERTS + 1, up, down)

    def block2_sp(sp):
        mod_sp(sp)
        mix_in_sp(sp)
        for i in range(4):
            load(sp, cols(d["w_out_2"][0], 256 * i), KC, 256)
        moe_sp(sp)

    def block2_pe(pe):
        mod_pe(pe)
        fence(pe, "mod")
        norm_pe(pe, NT)
        norm_pe(pe, NT)
        mix_in_pe(pe)
        fence(pe, "mix_in")
        fence(pe, "mix_conv")
        gla_pe(pe)
        fence(pe, "gla_done")
        ssd_pe(pe)
        fence(pe, "ssd_done")
        rwkv_once_pe(pe)
        fence(pe, "rwkv_once")
        rwkv_pe(pe, 0)
        fence(pe, "rwkv_fwd")
        rwkv_pe(pe, 1)
        fence(pe, "rwkv_bwd")
        wo_pe(pe, 2)
        fence(pe, "mix_out")
        norm_pe(pe, NT)
        router_pe(pe)
        experts_pe(pe, "moe", EXPERTS + 1, True)
        fence(pe, "moe_out")

    def block2_act(act):
        mod_act(act)
        fence(act, "mod")
        act.dma_start(ctx_tok, d["ctx_2"][0].rearrange("(t p) c -> p t c", p=P)).then_inc(S("stage_in"), 16)
        norm_act(act, ctx_tok, NT, "ln", uT[:, :, 0:CTX], modT[:, 1, 1, :], modT[:, 0, 1, :])
        norm_act(act, x_tok, NT, "ln", uT[:, :, CTX:ALL], modT[:, 1, 0, :], modT[:, 0, 0, :])
        mix_move(act, 0)
        fence(act, "mix_in")
        conv_act(act)
        fence(act, "mix_conv")
        gla_act(act)
        fence(act, "gla_done")
        ssd_act(act)
        fence(act, "ssd_done")
        rwkv_once_act(act)
        fence(act, "rwkv_once")
        rwkv_act(act, 0)
        fence(act, "rwkv_fwd")
        rwkv_act(act, 1)
        rwkv_end_act(act)
        fence(act, "rwkv_bwd")
        ln_load(act, 0)
        act.dma_start(router_w, d["router_w_2"][0].rearrange("(p c) e -> p c e", p=P)).then_inc(S("router_in"), 16)
        wo_act(act, 2)
        out_ln_act(act, 0)
        fence(act, "mix_out")
        ln_load(act, 1)
        norm_act(act, x_tok, NT, "ln", aT, modT[:, 3, 0, :], modT[:, 2, 0, :])
        router_act(act)
        experts_act(act, "moe", EXPERTS + 1, MOE)
        out_ln_act(act, 1)
        fence(act, "moe_out")

    def block2_dve(dve):
        mod_dve(dve)
        fence(dve, "mod")
        dve.wait_ge(S("stage_in"), 16 * 2)
        norm_dve(dve, ctx_tok, NT, "ln")
        norm_dve(dve, x_tok, NT, "ln")
        mix_move(dve, 1)
        fence(dve, "mix_in")
        conv_dve(dve)
        fence(dve, "mix_conv")
        gla_dve(dve)
        fence(dve, "gla_done")
        ssd_dve(dve)
        fence(dve, "ssd_done")
        rwkv_once_dve(dve)
        fence(dve, "rwkv_once")
        rwkv_dve(dve, 0)
        fence(dve, "rwkv_fwd")
        rwkv_dve(dve, 1)
        rwkv_end_dve(dve)
        fence(dve, "rwkv_bwd")
        dve.wait_ge(S("item_used"), MOE)
        out_ln_dve(dve, 0, g1_b)
        fence(dve, "mix_out")
        norm_dve(dve, x_tok, NT, "ln")
        router_dve(dve)
        experts_dve(dve, "moe", EXPERTS + 1, MOE, True)
        dve.wait_ge(S("item_used"), MOE + 3 * (EXPERTS + 1))
        out_ln_dve(dve, 1, g2_b)
        fence(dve, "moe_out")

    def block2_pool(pool):
        for n in FENCES[6:]:
            if n == "gla_done":
                gla_pool(pool)
            if n == "rwkv_fwd":
                rwkv_pool(pool, 0)
            if n == "rwkv_bwd":
                rwkv_pool(pool, 1)
            fence(pool, n)

    with ctx:
        block = ctx.enter_context(nc.Block())

        @block.sync
        def _(sp):
            block1_sp(sp)
            block2_sp(sp)
            sp.wait_ge(S("fence"), 4 * len(FENCES))
            sp.dma_start(out.rearrange("a (t p) c -> p (a t) c", p=P), x_tok).then_inc(S("stored"), 16)
            sp.wait_ge(S("stored"), 16)

        @block.tensor
        def _(pe):
            block1_pe(pe)
            block2_pe(pe)

        @block.scalar
        def _(act):
            block1_act(act)
            block2_act(act)

        @block.vector
        def _(dve):
            block1_dve(dve)
            block2_dve(dve)

        @block.gpsimd
        def _(pool):
            block1_pool(pool)
            block2_pool(pool)


_INS = """x norm_mix_pre norm_mix_post norm_ffn_pre norm_ffn_post na_w_qkv na_w_o na_rpb
dil_w_qkv dil_w_o ffn_w_gate ffn_w_up ffn_w_down c_2 ctx_2 c_ctx_2 ada_w_2 ada_b_2 w_in_2 w_out_2
ln1_w_2 ln1_b_2 ln2_w_2 ln2_b_2 router_w_2 exp_w1_2 exp_w3_2 exp_w2_2 sh_w1_2 sh_w3_2 sh_w2_2""".split()


def packed(v):
    def col(name):
        a = v[name + "_2"][0]
        return a.reshape(-1, a.shape[-1] // P, P).transpose(2, 0, 1).reshape(P, -1)

    cols_ = {"conv_w": col("ssd_conv_w"), "conv_b": col("ssd_conv_b"), "mu": col("rwkv_mu"), "rwkv_a0": col("rwkv_a0"),
             "rwkv_kk": col("rwkv_kk"), "rwkv_ka": col("rwkv_ka"),
             "rwkv_rk": v["rwkv_rk_2"][0].reshape(2, P).T, "one_less_ka": np.zeros((P, 2), np.float32)}
    rows_ = {"rwkv_w0": "rwkv_w0", "dt_bias": "ssd_dt_bias", "a_log": "ssd_a_log", "ssd_d": "ssd_d",
             "ssd_norm_w": "ssd_norm_w", "lnx_w": "rwkv_lnx_w", "lnx_b": "rwkv_lnx_b", "gla_gb": "gla_gb",
             "gla_norm_w": "gla_norm_w", "router_b": "router_b"}
    rows_ = {k: v[n + "_2"][0].reshape(1, -1) for k, n in rows_.items()}
    m = np.zeros((P, 4, 256), np.float32)
    m[:, 0] = v["rwkv_w2_2"][0].reshape(P, 256)
    m[:, 1] = v["rwkv_a2_2"][0].reshape(P, 256)
    m[:, 2] = v["rwkv_g2_2"][0]
    gu = v["gla_gu_2"][0]
    m[0:16, 3, 0:128], m[16:32, 3, 128:256] = gu[0], gu[1]
    for table, parts in ((VCOL, cols_), (VROW, rows_)):
        off = 0
        for k, a in parts.items():
            assert table[k] == (off, a.shape[1]), (k, off, a.shape)
            off += a.shape[1]
    return {"vcol": np.concatenate(list(cols_.values()), 1), "vrow": np.concatenate(list(rows_.values()), 1),
            "mats": m.reshape(P, -1)}


def kernel(**inputs):
    import numpy as _np
    import concourse.bacc as _bacc
    from concourse import mybir as _mybir
    from concourse.bass_utils import run_bass_kernel_spmd as _run

    nc = _bacc.Bacc("TRN2", target_bir_lowering=False, num_devices=1)
    names, consts = constants()
    given = {n: _np.asarray(a) for n, a in inputs.items()}
    arrays, aps = {}, {}
    for name, a in [(n, given[n]) for n in _INS] + list(packed(given).items()) + list(consts.items()):
        a = _np.ascontiguousarray(a)
        arrays[f"in_{name}_dram"] = a
        aps[name] = nc.dram_tensor(f"in_{name}_dram", a.shape, _mybir.dt.from_np(a.dtype), kind="ExternalInput").ap()
    out = nc.dram_tensor("out_0_dram", (1, SEQ, D), F32, kind="ExternalOutput").ap()
    program(nc, aps, out, names)
    r = _run(nc, [arrays], core_ids=[0])
    return r.results[0]["out_0_dram"]
```

```python
from contextlib import ExitStack

import numpy as np

import concourse.bass as bass
from concourse import mybir

F32 = mybir.dt.float32
F32R = mybir.dt.float32r
I32 = mybir.dt.int32
ALU = mybir.AluOpType
ACT = mybir.ActivationFunctionType
X = mybir.AxisListType.X

P = 128
D = 1024
KC = D // P
SEQ = 256
CTX = 256
NT = SEQ // P
ALL = CTX + SEQ
DEPTH = 2
HEADS = 16
HD = 64
GRID_W = 64
GRID_H = SEQ // GRID_W
NA_COLS = 16
RPB_R, RPB_C = 15, 31
GROUPS = 3
DFF = 2816
FF_TILE = 256
N_FF = DFF // FF_TILE
RMS_EPS = 1e-6
LN_EPS = 1e-5
RWKV_LNX_EPS = 64e-5
SLOTS = 6
SLOT = 2048
NEG_FILL = -1e33

EXPERTS = 64
TOP_K = 8
EGROUPS = 8
TOP_GROUPS = 4
ROUTED_SCALE = 2.5
DN_ALPHA = 2.0 ** 0.25


def slope(h):
    return float(np.float32(2.0) ** np.float32(-8.0 * (h + 1) / HEADS))


def offsets(widths):
    table, off = {}, 0
    for k, w in widths:
        table[k] = (off, w)
        off += w
    return table, off


VCOL, VCOL_N = offsets([("conv_w", 24), ("conv_b", 8), ("mu", 36), ("rwkv_a0", 4), ("rwkv_kk", 2), ("rwkv_ka", 2),
                        ("rwkv_rk", 2), ("one_less_ka", 2)])
VROW, VROW_N = offsets([("rwkv_w0", 512), ("dt_bias", 16), ("a_log", 16), ("ssd_d", 8), ("ssd_norm_w", 512),
                        ("lnx_w", 256), ("lnx_b", 256), ("gla_gb", 256), ("gla_norm_w", 256), ("router_b", 64)])

FENCES = ["na_attn", "na_out", "ffn0_out", "dil_attn", "dil_out", "ffn1_out", "mod", "mix_in", "mix_conv", "gla_done",
          "ssd_done", "rwkv_once", "rwkv_fwd", "rwkv_bwd", "mix_out", "moe_out"]


def constants():
    p = np.arange(P)[:, None]
    i = np.arange(P)[None, :]
    f = {}
    f["ident"] = (p == i)
    f["ones"] = np.ones((P, P))
    f["mirror"] = (p // 64 == i // 64) & (p % 64 == 63 - i % 64)
    f["head_sum"] = (p // HD == i // HD)
    f["below8"] = np.broadcast_to((np.arange(64) % 8 < np.arange(64) // 8)[None, :], (P, 64))
    f["head_cols"] = (p // HD == np.arange(2)[None, :])
    f["gla_diag"] = (p // 32 == np.arange(256)[None, :] // 64)
    same = p // 64 == i // 64
    col = np.arange(2)[None, :]
    for d in range(2):
        inc = (p <= i) if d == 0 else (p >= i)
        f[f"cum{d}"] = inc
        f[f"rest{d}"] = ~inc
        mid = (p % 64 <= 31) if d == 0 else (p % 64 >= 32)
        exc = (p < i) if d == 0 else (p > i)
        f[f"rk_inc{d}"] = (same & inc).astype(int) - (same & mid)
        f[f"rk_exc{d}"] = (same & exc).astype(int) - (same & mid)
        f[f"rk_tail{d}"] = (p // 64 == col) & ~mid
        f[f"rk_ref{d}"] = (p // 64 == col) & mid
        for n in range(7):
            s = 1 << n
            blk, u = i // (2 * s), i % (2 * s)
            m = blk * 2 * s + s - 1
            if d == 0:
                a = np.where(u >= s, (p > m) & (p <= i), (p > i) & (p <= m))
            else:
                a = np.where(u < s, (p >= i) & (p <= m), (p > m) & (p < i))
            f[f"lev{d}_{n}"] = a
    names, parts, off = {}, [], 0
    for k, v in f.items():
        names[k] = (off, v.shape[1])
        parts.append(v.astype(np.float32))
        off += v.shape[1]
    masks = []
    for d in range(2):
        for n in range(7):
            s = 1 << n
            same_blk = p // (2 * s) == i // (2 * s)
            first, second = p % (2 * s) < s, i % (2 * s) >= s
            masks.append(same_blk & (first & second if d == 0 else ~first & ~second))
    masks.append(p == i)
    masks = np.concatenate([m.astype(np.int32) for m in masks], 1)
    fm = []
    for d in range(2):
        inc = (p <= i) if d == 0 else (p >= i)
        fm += [inc, same & inc, same & inc & (p != i)]
        fm += [masks[:, (7 * d + n) * P:(7 * d + n + 1) * P] for n in range(6)]
    fm = np.concatenate([m.astype(np.float32) for m in fm], 1)
    tok = np.arange(SEQ)
    nd = np.zeros((P, NT, GROUPS, SEQ), np.float32)
    for t in range(NT):
        dist = np.abs(tok[None, :] - (t * P + np.arange(P))[:, None])
        for g, ok in enumerate((dist <= 64, dist % 4 == 0, dist % 16 == 0)):
            nd[:, t, g] = np.where(ok, -dist.astype(np.float32), NEG_FILL)
    c = 63 - np.arange(P)[:, None] % 64
    start = np.clip(c - NA_COLS // 2, 0, GRID_W - NA_COLS)
    k = np.arange(GRID_W)[None, :]
    win = np.where((k >= start) & (k < start + NA_COLS), 0.0, -1e30).astype(np.float32)
    return names, {"cst": np.concatenate(parts, 1), "lev_masks": masks, "tri_masks": fm,
                   "neg_dist": nd.reshape(P, -1), "na_window": win}


def program(nc, d, out, names):
    ctx = ExitStack()
    sems = {}

    def S(name):
        if name not in sems:
            sems[name] = ctx.enter_context(nc.semaphore(name))
        return sems[name]

    MEM = 53200
    mem_at = -(-nc.sbuf_base // 32) * 32
    mem = nc.alloc_sbuf_tensor_at("mem", [P, MEM], F32, offset=mem_at)
    psum = ctx.enter_context(nc.psum_tensor("psum", [P, 8, 512], F32))
    top = [0]
    high = [0]

    def alloc(*shape, dt=F32):
        n = int(np.prod(shape))
        a = mem[:, top[0]:top[0] + n]
        top[0] += -(-n // 8) * 8
        high[0] = max(high[0], top[0])
        assert top[0] <= MEM, (top[0], shape)
        if dt is not F32:
            a = a.bitcast(dt)
        names_ = "abcd"[:len(shape)]
        if len(shape) > 1:
            a = a.rearrange(f"p ({' '.join(names_)}) -> p {' '.join(names_)}",
                            **{k: v for k, v in zip(names_[1:], shape[1:])})
        return a

    def bc(ap, axis, n):
        a = ap.unsqueeze(axis)
        shape = list(a.shape)
        shape[axis] = n
        return a.to_broadcast(shape)

    def bank(b, n=512, off=0):
        return psum[:, b, off:off + n]

    def banks(b, n):
        return psum[:, b:b + n, :].rearrange("p b n -> p (b n)")

    ring_at = top[0]
    ring = alloc(SLOTS, SLOT)
    cst = alloc(sum(n for _, n in names.values()))
    x_tok = alloc(NT, D)

    def C(name):
        o, n = names[name]
        return cst[:, o:o + n]

    ident = C("ident")
    aT = alloc(KC, SEQ)
    xn_at = top[0]
    xn = alloc(NT, D)
    stat = alloc(4, 64)
    gains = alloc(8, KC)
    gain_b = alloc(D)
    rms_eps = alloc(1)
    ln_eps = alloc(1)
    lnx_eps = alloc(1)
    hid_at = top[0]
    hid = alloc(2, 2 * SEQ)
    gate_act = alloc(2 * SEQ)
    silu_c = alloc(KC, 2)
    c_in = alloc(2, KC)
    ada_cols = alloc(6, KC)
    base_top = top[0]

    HI = 3
    split_at = MEM - KC * SEQ - HI * SLOT - 4 * SEQ

    def both(name, at, a, b):
        r = nc.alloc_sbuf_tensor_at(name, [P, a, b], F32R, offset=mem_at + 4 * at)
        return r[:, :, :].bitcast(F32), r[:, :, :]

    x_hi_f, x_hi = both("x_hi", split_at, KC, SEQ)
    x_lo = both("x_lo", xn_at, KC, SEQ)[1]
    w_hi_f, w_hi = zip(*(both(f"w_hi{q}", split_at + KC * SEQ + q * SLOT, 1, SLOT) for q in range(HI)))
    w_lo = [both(f"w_lo{q}", ring_at + q * SLOT, 1, SLOT)[1] for q in range(SLOTS)]
    hid_hi_f, hid_hi = both("hid_hi", hid_at, 2, 2 * SEQ)
    hid_lo = both("hid_lo", split_at + KC * SEQ + HI * SLOT, 2, 2 * SEQ)[1]

    def hi_lo(n, c, w):
        return [r[:, 0, 0:c * w].rearrange("p (c w) -> p c w", c=c) for r in (w_hi[n % HI], w_lo[n % SLOTS])]

    def split_product(pe, out, lhs, rhs, start, stop, **kw):
        for k, (a, b) in enumerate(((0, 0), (0, 1), (1, 0))):
            ins = pe.matmul(out, lhs[a], rhs[b], start=start and k == 0, stop=stop and k == 2, **kw)
        return ins

    def cols(w, n0, n=256):
        return w.rearrange("(p c) n -> p c n", p=P)[:, :, n0:n0 + n]

    def slot(n, c, w):
        return ring[:, n % SLOTS, 0:c * w].rearrange("p (c w) -> p c w", c=c)

    sp_items, pe_items = [0], [0]

    def load(sp, src, c, w):
        n = sp_items[0]
        sp_items[0] += 1
        if n >= SLOTS:
            sp.wait_ge(S("item_used"), n - SLOTS + 1)
        sp.dma_start(slot(n, c, w), src).then_inc(S(f"slot_loaded{n % SLOTS}"), 16)

    def take(pe, c, w):
        n = pe_items[0]
        pe_items[0] += 1
        pe.wait_ge(S(f"slot_loaded{n % SLOTS}"), 16 * (n // SLOTS + 1))
        return slot(n, c, w)

    fences = {}

    def fence(eng, name):
        fences[name] = 1
        eng.drain().then_inc(S("fence"), 1)
        eng.wait_ge(S("fence"), 4 * fence_no[name])

    fence_no = {n: k + 1 for k, n in enumerate(FENCES)}

    links = {}

    def link(eng, key, ins):
        links[key] = links.get(key, 0) + 1
        ins.then_inc(S(f"{key}_chain"), 1)
        eng.wait_ge(S(f"{key}_chain"), links[key])

    X_NO = {k: n + 1 for n, k in enumerate(("na", "wo0", "ff0", "dil", "wo1", "ff1", "wo2", "moe"))}

    def split_no(n):
        return n + 1 if n < MOD else n + 1 - (W_OUT - MOD)

    EARLY = 2

    def x_hi_act(act, ready, k):
        act.wait_ge(S(ready), KC * k)
        act.activation(x_hi, aT, ACT.Copy).then_inc(S("x_hi"), 1)

    def x_lo_dve(dve, key):
        dve.wait_ge(S("x_hi"), X_NO[key])
        dve.tensor_tensor(x_lo, aT, x_hi_f, ALU.subtract).then_inc(S("x_split"), 1)

    def hi_act(act, n, i=None):
        load_no = 16 * (n // SLOTS + 1)
        act.wait_ge(S(f"slot_loaded{n % SLOTS}"), load_no if i is None else 16 * i + load_no)
        used = n - HI + 1
        if used > 0:
            act.wait_ge(S("item_used"), used if i is None else 6 * i + used)
        act.activation(w_hi[n % HI][:, 0, :], ring[:, n % SLOTS, :], ACT.Copy).then_inc(S("w_hi"), 1)

    def lo_dve(dve, n, i=None):
        no = split_no(n)
        dve.wait_ge(S("w_hi"), no if i is None else 6 * i + no)
        dve.tensor_tensor(w_lo[n % SLOTS][:, 0, :], ring[:, n % SLOTS, :], w_hi_f[n % HI][:, 0, :], ALU.subtract
                          ).then_inc(S("w_split"), 1)

    def take_split(pe, c, w):
        n = pe_items[0]
        pe_items[0] += 1
        pe.wait_ge(S("w_split"), split_no(n))
        return hi_lo(n, c, w)

    norm_n = {"act": 0, "dve": 0, "pe": 0}

    def norm_act(act, src, tiles, kind, dst, scale, shift, item=None):
        k = norm_n["act"]
        norm_n["act"] += 1
        if kind == "rms":
            for t in range(tiles):
                link(act, "act", nc.scalar.activation(xn[:, t % NT, :], src[:, t, :], ACT.Square,
                                                      accum_out=stat[:, 0, t:t + 1]))
            act.activation(stat[:, 1, 0:tiles], stat[:, 0, 0:tiles], ACT.Sqrt, bias=rms_eps,
                           scale=1.0 / D).then_inc(S("norm_root"), 1)
        else:
            act.wait_ge(S("norm_var"), norm_count["ln", k] + 1)
            act.activation(stat[:, 1, 0:tiles], stat[:, 0, 0:2 * tiles].rearrange("p (t s) -> p t s", s=2)[:, :, 1],
                           ACT.Sqrt, bias=ln_eps, scale=1.0).then_inc(S("norm_root"), 1)
        if item is not None:
            for n in range(EARLY):
                hi_act(act, item + n)
        for q in range(4):
            act.wait_ge(S("norm_turned"), 4 * k + q + 1)
            for c in (2 * q, 2 * q + 1):
                w = tiles * P
                o = dst[:, c, 0:w]
                i = bank(q, 2 * SEQ)[:, (c % 2) * w:(c % 2 + 1) * w]
                if shift is None:
                    ins = act.activation(o, i, ACT.Identity, scale=scale[:, c:c + 1])
                else:
                    ins = act.activation(o, i, ACT.Identity, scale=scale[:, c:c + 1], bias=shift[:, c:c + 1])
                ins.then_inc(S("norm_T"), 1)

    norm_count = {}
    norm_kinds = ["rms", "rms", "rms", "rms", "ln", "ln", "ln"]
    seen = 0
    for k, kind in enumerate(norm_kinds):
        norm_count["ln", k] = seen
        seen += kind == "ln"

    def norm_dve(dve, src, tiles, kind, item=None):
        k = norm_n["dve"]
        norm_n["dve"] += 1
        if kind == "ln":
            for t in range(tiles):
                for h in range(2):
                    link(dve, "dve", dve.bn_stats(stat[:, 2, 12 * t + 6 * h:12 * t + 6 * h + 6],
                                                  src[:, t, 512 * h:512 * h + 512]))
            for t in range(tiles):
                ins = dve.bn_aggr(stat[:, 0, 2 * t:2 * t + 2], stat[:, 2, 12 * t:12 * t + 12])
                if t < tiles - 1:
                    link(dve, "dve", ins)
            ins.then_inc(S("norm_var"), 1)
        dve.wait_ge(S("norm_root"), k + 1)
        link(dve, "dve", dve.reciprocal(stat[:, 3, 0:tiles], stat[:, 1, 0:tiles]))
        if k:
            dve.wait_ge(S("norm_turned"), 4 * k)
        for t in range(tiles):
            if kind == "rms":
                ins = dve.tensor_scalar(xn[:, t, :], src[:, t, :], stat[:, 3, t:t + 1], None, ALU.mult)
            else:
                ins = dve.tensor_scalar(xn[:, t, :], src[:, t, :], stat[:, 0, 2 * t:2 * t + 1],
                                        stat[:, 3, t:t + 1], ALU.subtract, ALU.mult)
            ins.then_inc(S("norm_rows"), 1)
        if item is not None:
            for n in range(EARLY):
                lo_dve(dve, item + n)

    def norm_pe(pe, tiles):
        k = norm_n["pe"]
        norm_n["pe"] += 1
        pe.wait_ge(S("norm_rows"), NT * (k + 1))
        if k:
            pe.wait_ge(S("norm_T"), KC * k)
        turn_pe(pe, xn, "norm_turned")

    def turn_pe(pe, rows, done):
        for q in range(4):
            for c in (2 * q, 2 * q + 1):
                for t in range(NT):
                    ins = pe.transpose(bank(q, P, (c % 2) * SEQ + t * P),
                                       rows[:, t, :].rearrange("p (i c) -> p c i", c=KC)[:, c, :], ident)
            ins.then_inc(S(done), 1)

    def rows_product(pe):
        for i in range(D // 256):
            w = take_split(pe, KC, 256)
            for t in range(NT):
                o = banks(4 + 2 * t, 2)[:, 256 * i:256 * i + 256]
                tok = slice(t * P, (t + 1) * P)
                for c in range(KC):
                    ins = split_product(pe, o, (x_hi[:, c, tok], x_lo[:, c, tok]), [a[:, c, :] for a in w], c == 0,
                                        c == KC - 1)
            ins.then_inc(S("item_used"), 1)

    res_n = {"act": 0, "dve": 0}

    def residual_act(act, item_count):
        k = res_n["act"]
        res_n["act"] += 1
        act.wait_ge(S("item_used"), item_count)
        for t in range(NT):
            link(act, "act", act.activation(xn[:, t, :], banks(4 + 2 * t, 2), ACT.Square,
                                            accum_out=stat[:, 0, t:t + 1]))
        act.activation(stat[:, 1, 0:NT], stat[:, 0, 0:NT], ACT.Sqrt, bias=rms_eps,
                       scale=1.0 / D).then_inc(S("post_root"), 1)

    def residual_dve(dve):
        k = res_n["dve"]
        res_n["dve"] += 1
        dve.wait_ge(S("post_root"), k + 1)
        dve.wait_ge(S("gain_b"), 16 * (k + 1))
        link(dve, "dve", dve.reciprocal(stat[:, 3, 0:NT], stat[:, 1, 0:NT]))
        for t in range(NT):
            link(dve, "dve", dve.scalar_tensor_tensor(xn[:, t, :], banks(4 + 2 * t, 2), stat[:, 3, t:t + 1], gain_b,
                                                      ALU.mult, ALU.mult))
            link(dve, "dve", dve.tensor_tensor(x_tok[:, t, :], x_tok[:, t, :], xn[:, t, :], ALU.add))

    def experts_sp(sp, n, up, down):
        for w in up(0):
            load(sp, w, KC, 256)
        n0 = sp_items[0]
        for e in range(2):
            for w in up(e + 1):
                load(sp, w, KC, 256)
            load(sp, down(e), 2, D)
        with sp.Fori(1, (n - 1) // 2) as i:
            for j in range(2):
                srcs = list(up(2 * i + 1 + j)) + [down(2 * i + j)]
                for m, w in enumerate(srcs):
                    q = n0 + 3 * j + m
                    sp.wait_ge(S("item_used"), 6 * i + (q - SLOTS + 1))
                    c, wd = (KC, 256) if m < 2 else (2, D)
                    sp.dma_start(slot(q, c, wd), w).then_inc(S(f"slot_loaded{q % SLOTS}"), 16)
        sp_items[0] = n0 + 6 * ((n - 1) // 2)
        load(sp, down(n - 1), 2, D)

    EX_BASE = {"ff0": 0, "ff1": N_FF, "moe": 2 * N_FF}

    def experts_pe(pe, tag, n, gated):
        eb = EX_BASE[tag]
        n0 = pe_items[0]
        pe.wait_ge(S("x_split"), X_NO[tag])

        def split_item(m, i, c, w):
            no = split_no(n0 + m)
            pe.wait_ge(S("w_split"), no if i is None else 6 * i + no)
            return hi_lo(n0 + m, c, w)

        def up(e, m, i, static):
            for k in range(2):
                if not static:
                    pe.wait_ge(S(("ex_silu", "ex_hid")[k]), e + eb)
                w = split_item(m + k, i, KC, 256)
                for f in range(2):
                    for c in range(KC):
                        ins = split_product(pe, bank(k, SEQ, f * SEQ), [a[:, c, f::2] for a in w],
                                            (x_hi[:, c, :], x_lo[:, c, :]), c == 0, c == KC - 1)
                ins.then_inc(S("item_used"), 1)
            if gated and not static:
                pe.wait_ge(S("gate_diag"), e)
                pe.matmul(bank(2, SEQ), C("ones"), gate_diag, start=True, stop=True
                          ).then_inc(S("gate_spread"), 1)

        def down(e, m, i, parity, first, last):
            w = split_item(m, i, 2, D)
            pe.wait_ge(S("ex_hid"), e + (eb + 1))
            for f in range(2):
                for t in range(NT):
                    tok = slice(f * SEQ + t * P, f * SEQ + (t + 1) * P)
                    for h in range(2):
                        ins = split_product(pe, bank(4 + 2 * t + h), (hid_hi[:, parity, tok], hid_lo[:, parity, tok]),
                                            [a[:, f, 512 * h:512 * h + 512] for a in w], first and f == 0,
                                            last and f == 1, skip_group_check=True)
            ins.then_inc(S("item_used"), 1)

        up(0, 0, None, True)
        up(1, 2, None, False)
        down(0, 4, None, 0, True, False)
        up(2, 5, None, False)
        down(1, 7, None, 1, False, False)
        with pe.Fori(1, (n - 1) // 2) as i:
            for j in range(2):
                up(2 * i + (1 + j), 2 + 3 * j, i, False)
                down(2 * i + j, 4 + 3 * j, i, j, False, False)
        pe_items[0] = n0 + 3 * n
        down(n - 1, 3 * n - 1, None, 0, False, True)

    def experts_act(act, tag, n, base):
        eb = EX_BASE[tag]

        def hi(m, i):
            hi_act(act, base + m, i)

        def silu(e, used, first):
            act.wait_ge(S("item_used"), used)
            if not first:
                act.wait_ge(S("ex_hid"), e + eb)
            act.activation(gate_act, bank(0), ACT.Silu).then_inc(S("ex_silu"), 1)

        x_hi_act(act, "norm_T", {"ff0": 2, "ff1": 4, "moe": 7}[tag])
        hi(2, None)
        silu(0, base + 1, True)
        for m in (3, 4):
            hi(m, None)

        def pair(i, last):
            for j in range(2):
                silu(2 * i + (1 + j), 6 * i + (base + 3 * (1 + j)), False)
                for m in range(1 if last and j else 3):
                    hi(5 + 3 * j + m, i)

        pairs = (n - 1) // 2
        with act.Fori(0, pairs - 1) as i:
            pair(i, False)
        pair(pairs - 1, True)

    def experts_dve(dve, tag, n, base, gated, beside=None, first_gates=None):
        eb = EX_BASE[tag]
        step = 3 if gated else 2
        cb = {"ff0": 0, "ff1": 2 * N_FF, "moe": 4 * N_FF - 1}[tag]

        def lo(m, i):
            lo_dve(dve, base + m, i)

        def one(e, used, parity, first):
            dve.wait_ge(S("ex_silu"), e + (eb + 1))
            done = step * e + cb
            if gated and first:
                done = done + 1
            if gated and not first:
                dve.wait_ge(S("gate_spread"), e)
                dve.tensor_tensor(gate_act.rearrange("p (f t) -> p f t", f=2), gate_act.rearrange("p (f t) -> p f t", f=2),
                                  bc(bank(2, SEQ), 1, 2), ALU.mult).then_inc(S("ex_chain"), 1)
                done = done + 1
                dve.wait_ge(S("ex_chain"), done)
            dve.wait_ge(S("item_used"), used)
            dve.tensor_tensor(gate_act, gate_act, bank(1), ALU.mult).then_inc(S("ex_chain"), 1)
            dve.wait_ge(S("ex_chain"), done + 1)
            dve.tensor_copy(hid_hi[:, parity, :], gate_act).then_inc(S("ex_chain"), 1)
            dve.wait_ge(S("ex_chain"), done + 2)
            dve.tensor_tensor(hid_lo[:, parity, :], gate_act, hid_hi_f[:, parity, :], ALU.subtract
                              ).then_inc(S("ex_hid"), 1)
            if gated and not first:
                diag(e, False)

        def diag(e, first):
            if not first:
                dve.wait_ge(S("gate_spread"), e)
            for t in range(NT):
                g = gate[:, t, e:e + 1] if isinstance(e, int) else gate[:, t, bass.ds(e, 1)]
                ins = dve.tensor_scalar(gate_diag[:, t * P:(t + 1) * P], ident, g, None, ALU.mult)
            ins.then_inc(S("gate_diag"), 1)

        x_lo_dve(dve, tag)
        lo(2, None)
        one(0, base + 2, 0, True)
        for m in (3, 4):
            lo(m, None)
        if gated:
            first_gates(dve)
            diag(0, True)

        def pair(i, last):
            for j in range(2):
                lo(5 + 3 * j, i)
                one(2 * i + (1 + j), 6 * i + (base + 3 * (1 + j) + 1), (1 + j) % 2, False)
                if not (last and j):
                    for m in (1, 2):
                        lo(5 + 3 * j + m, i)
                if beside and not last:
                    for m in range(2):
                        beside(dve, i, 2 * j + m)

        pairs = (n - 1) // 2
        with dve.Fori(0, pairs - 1) as i:
            pair(i, False)
        pair(pairs - 1, True)

    qT, kT, v_tok = [], [], []
    for g in range(GROUPS):
        if g == GROUPS - 1:
            na_bias = mem[:, top[0]:top[0] + HEADS * 6 * GRID_W].rearrange("p (a b c) -> p a b c", a=HEADS, b=6)
        qT.append(alloc(KC, SEQ))
        kT.append(alloc(KC, SEQ))
        v_tok.append(alloc(NT, D))
    s_buf_at = top[0]
    s_buf = alloc(2, GROUPS * SEQ)
    p_buf = alloc(2, GROUPS * SEQ)
    pT_buf = alloc(2, GROUPS * SEQ)
    neg_max = alloc(2 * HEADS)
    row_sum = alloc(NT, HEADS)
    inv_sum = alloc(NT, HEADS)
    o_tok = xn
    na_window = gate_act[:, 0:GRID_W]
    neg_dist = [mem[:, MEM - 4 * SEQ:][:, 0:GROUPS * SEQ], hid.rearrange("p a b -> p (a b)")[:, 0:GROUPS * SEQ]]
    assert split_at >= s_buf_at and top[0] <= MEM - 4 * SEQ
    attn_top = top[0]

    NA_QKV = 0
    NA_WO = 12
    FF0 = 16
    DIL_QKV = FF0 + 3 * N_FF
    DIL_WO = DIL_QKV + 12 * GROUPS
    FF1 = DIL_WO + 4
    MOD = FF1 + 3 * N_FF

    def qkv_pe(pe, g, n0):
        for i in range(12):
            m = n0 + i
            w = take_split(pe, KC, 256)
            if m >= 4:
                pe.wait_ge(S(f"qkv_moved{m % 2}"), (m - 4) // 2 + 1)
            for half in range(2):
                o = bank(4 + m % 4, SEQ, half * SEQ)
                hs = slice(half * P, (half + 1) * P)
                for c in range(KC):
                    if i < 8:
                        lhs, rhs = [a[:, c, hs] for a in w], (x_hi[:, c, :], x_lo[:, c, :])
                    else:
                        lhs, rhs = (x_hi[:, c, hs], x_lo[:, c, hs]), [a[:, c, :] for a in w]
                    ins = split_product(pe, o, lhs, rhs, c == 0, c == KC - 1)
            ins.then_inc(S("item_used"), 1)

    def qkv_place(g, i):
        if i < 8:
            return (qT if i < 4 else kT)[g][:, 2 * (i % 4):2 * (i % 4) + 2, :]
        return v_tok[g][:, :, 256 * (i - 8):256 * (i - 8) + 256]

    def qkv_move(eng, g, n0, item0, parity, last):
        split = (hi_act, lo_dve)[parity]
        for i in range(12):
            m = n0 + i
            if item0 + i + HI < last:
                split(eng, item0 + i + HI)
            if m % 2 != parity:
                continue
            eng.wait_ge(S("item_used"), item0 + i + 1)
            src = bank(4 + m % 4).rearrange("p (a b) -> p a b", a=2)
            f = HD ** -0.5 if i < 4 else 1.0
            if parity == 0:
                ins = nc.scalar.activation(qkv_place(g, i), src, ACT.Copy, scale=f)
            else:
                ins = nc.vector.tensor_scalar(qkv_place(g, i), src, f, None, ALU.mult)
            ins.then_inc(S(f"qkv_moved{parity}"), 1)

    def na_attn_pe(pe):
        pe.wait_ge(S("qkv_moved0"), 6)
        pe.wait_ge(S("qkv_moved1"), 6)
        pe.wait_ge(S("na_bias_ready"), 1)
        for h in range(HEADS + 2):
            if h < HEADS:
                if h >= 2:
                    pe.wait_ge(S("na_exp"), 2 * (h - 1))
                r = slice(HD * (h % 2), HD * (h % 2) + HD)
                for t in range(NT):
                    o = bank(h % 2, SEQ, t * SEQ)
                    pe.matmul(o, qT[0][r, h // 2, t * P:(t + 1) * P], kT[0][r, h // 2, :], start=True, stop=False)
                    ins = pe.matmul(o, C("mirror"), na_bias[:, h, 2 - 2 * t:6 - 2 * t, :].rearrange("p a b -> p (a b)"),
                                    start=False, stop=True)
                ins.then_inc(S("na_scores"), 1)
            if 1 <= h <= HEADS:
                g = h - 1
                pe.wait_ge(S("na_exp"), 2 * g + 2)
                if g >= 2:
                    pe.wait_ge(S("na_pT"), g - 1)
                for kc in range(2):
                    for t in range(NT):
                        ins = pe.transpose(bank(2 + g % 2, P, (2 * kc + t) * P), p_buf[:, g % 2, t * SEQ + kc * P:
                                           t * SEQ + kc * P + P], ident)
                ins.then_inc(S("na_turned"), 1)
            if h >= 2:
                g = h - 2
                pe.wait_ge(S("na_pT"), g + 1)
                if g % 4 == 0 and g >= 8:
                    pe.wait_ge(S("na_o"), g // 4 - 1)
                for t in range(NT):
                    for kc in range(2):
                        ins = pe.matmul(bank(4 + (g // 4) % 2, HD, t * SEQ + (g % 4) * HD),
                                        pT_buf[:, g % 2, (2 * kc + t) * P:(2 * kc + t + 1) * P],
                                        v_tok[0][:, kc, g * HD:(g + 1) * HD], start=kc == 0, stop=kc == 1)
                ins.then_inc(S("na_pv"), 1)

    def na_attn_act(act):
        for h in range(HEADS):
            act.wait_ge(S("na_max"), h + 1)
            if h >= 2:
                act.wait_ge(S("na_turned"), h - 1)
            for t in range(NT):
                act.activation(p_buf[:, h % 2, t * SEQ:(t + 1) * SEQ], bank(h % 2, SEQ, t * SEQ), ACT.Exp,
                               bias=neg_max[:, 2 * h + t:2 * h + t + 1], accum_out=row_sum[:, t, h:h + 1]
                               ).then_inc(S("na_exp"), 1)

    def na_attn_dve(dve):
        def rows(gq):
            dve.wait_ge(S("na_pv"), 4 * gq + 4)
            hs = slice(4 * gq, 4 * gq + 4)
            link(dve, "dve", dve.reciprocal(inv_sum[:, :, hs], row_sum[:, :, hs]))
            for t in range(NT):
                ins = dve.tensor_tensor(o_tok[:, t, 256 * gq:256 * gq + 256].rearrange("p (h e) -> p h e", h=4),
                                        bank(4 + gq % 2, SEQ, t * SEQ).rearrange("p (h e) -> p h e", h=4),
                                        bc(inv_sum[:, t, hs], 2, HD), ALU.mult)
            ins.then_inc(S("na_o"), 1)

        for h in range(HEADS + 1):
            if h < HEADS:
                dve.wait_ge(S("na_scores"), h + 1)
                dve.tensor_reduce(neg_max[:, 2 * h:2 * h + 2], bank(h % 2).rearrange("p (t k) -> p t k", t=2), X,
                                  ALU.max, negate=True).then_inc(S("na_max"), 1)
            if h >= 1:
                g = h - 1
                dve.wait_ge(S("na_turned"), g + 1)
                if g >= 2:
                    dve.wait_ge(S("na_pv"), g - 1)
                dve.tensor_copy(pT_buf[:, g % 2, 0:512], bank(2 + g % 2)).then_inc(S("na_pT"), 1)
                if g % 4 == 1 and g >= 5:
                    rows(g // 4 - 1)
        rows(3)

    def dil_attn_pe(pe):
        pe.wait_ge(S("qkv_moved0"), 6 + 18)
        pe.wait_ge(S("qkv_moved1"), 6 + 18)
        U = HEADS * NT
        for u in range(U + 2):
            if u < U:
                h, t = divmod(u, NT)
                r = slice(HD * (h % 2), HD * (h % 2) + HD)
                if u >= 2:
                    pe.wait_ge(S("dil_biased"), u - 1)
                for g in range(GROUPS):
                    ins = pe.matmul(banks(2 * (u % 2), 2)[:, g * SEQ:(g + 1) * SEQ],
                                    qT[g][r, h // 2, t * P:(t + 1) * P], kT[g][r, h // 2, :], start=True, stop=True)
                ins.then_inc(S("dil_scores"), 1)
            if 1 <= u <= U:
                w = u - 1
                pe.wait_ge(S("dil_exp"), w + 1)
                if w >= 1:
                    pe.wait_ge(S("dil_pT"), w)
                for k in range(2 * GROUPS):
                    ins = pe.transpose(banks(4, 2)[:, k * P:(k + 1) * P], p_buf[:, w % 2, k * P:(k + 1) * P], ident)
                ins.then_inc(S("dil_turned"), 1)
            if u >= 2:
                w = u - 2
                h, t = divmod(w, NT)
                pe.wait_ge(S("dil_pT"), w + 1)
                if w % 8 == 0 and w >= 16:
                    pe.wait_ge(S("dil_o"), w // 8 - 1)
                for k in range(2 * GROUPS):
                    ins = pe.matmul(bank(6 + (h // 4) % 2, HD, t * SEQ + (h % 4) * HD),
                                    pT_buf[:, w % 2, k * P:(k + 1) * P],
                                    v_tok[k // 2][:, k % 2, h * HD:(h + 1) * HD], start=k == 0,
                                    stop=k == 2 * GROUPS - 1)
                ins.then_inc(S("dil_pv"), 1)

    def dil_attn_act(act):
        for u in range(HEADS * NT + 1):
            if u < HEADS * NT:
                h, t = divmod(u, NT)
                act.wait_ge(S("dil_max"), u + 1)
                if u >= 2:
                    act.wait_ge(S("dil_turned"), u - 1)
                act.activation(p_buf[:, u % 2, :], s_buf[:, u % 2, :], ACT.Exp, bias=neg_max[:, u:u + 1],
                               accum_out=row_sum[:, t, h:h + 1]).then_inc(S("dil_exp"), 1)
            if u >= 1:
                w = u - 1
                act.wait_ge(S("dil_turned"), w + 1)
                if w >= 2:
                    act.wait_ge(S("dil_pv"), w - 1)
                act.activation(pT_buf[:, w % 2, :], banks(4, 2)[:, 0:GROUPS * SEQ], ACT.Copy
                               ).then_inc(S("dil_pT"), 1)

    def dil_attn_dve(dve):
        def rows(gq):
            dve.wait_ge(S("dil_pv"), 8 * gq + 8)
            hs = slice(4 * gq, 4 * gq + 4)
            link(dve, "dve", dve.reciprocal(inv_sum[:, :, hs], row_sum[:, :, hs]))
            for t in range(NT):
                ins = dve.tensor_tensor(o_tok[:, t, 256 * gq:256 * gq + 256].rearrange("p (h e) -> p h e", h=4),
                                        bank(6 + gq % 2, SEQ, t * SEQ).rearrange("p (h e) -> p h e", h=4),
                                        bc(inv_sum[:, t, hs], 2, HD), ALU.mult)
            ins.then_inc(S("dil_o"), 1)

        dve.wait_ge(S("stage_in"), 16 * 2)
        for u in range(HEADS * NT):
            h, t = divmod(u, NT)
            dve.wait_ge(S("dil_scores"), u + 1)
            if u >= 2:
                dve.wait_ge(S("dil_exp"), u - 1)
            dve.scalar_tensor_tensor(s_buf[:, u % 2, :], neg_dist[t], slope(h),
                                     banks(2 * (u % 2), 2)[:, 0:GROUPS * SEQ], ALU.mult, ALU.add
                                     ).then_inc(S("dil_biased"), 1)
            dve.wait_ge(S("dil_biased"), u + 1)
            dve.tensor_reduce(neg_max[:, u:u + 1], s_buf[:, u % 2, :], X, ALU.max, negate=True
                              ).then_inc(S("dil_max"), 1)
            if u % 8 == 4 and u >= 12:
                rows(u // 8 - 1)
        rows(3)

    def wo_pe(pe, k):
        turn_pe(pe, o_tok, "o_turned")
        pe.wait_ge(S("x_split"), X_NO[f"wo{k}"])
        rows_product(pe)

    def wo_act(act, k):
        item = (NA_WO, DIL_WO, W_OUT)[k]
        hi_act(act, item)
        for q in range(4):
            act.wait_ge(S("o_turned"), 4 * k + q + 1)
            for c in (2 * q, 2 * q + 1):
                act.activation(aT[:, c, :], bank(q, SEQ, (c % 2) * SEQ), ACT.Copy).then_inc(S("o_T"), 1)
        x_hi_act(act, "o_T", k + 1)
        for n in range(1, 4):
            hi_act(act, item + n)

    def wo_dve(dve, k):
        item = (NA_WO, DIL_WO, W_OUT)[k]
        lo_dve(dve, item)
        x_lo_dve(dve, f"wo{k}")
        for n in range(1, 4):
            lo_dve(dve, item + n)

    def gain_load(act, src, k):
        act.dma_start(gain_b, src.to_broadcast([P, D])).then_inc(S("gain_b"), 16)

    def g_row(name, layer):
        return d[name][layer:layer + 1, :]

    def block1_sp(sp):
        W = d["na_w_qkv"][0]
        for i in range(12):
            load(sp, cols(W, 256 * i), KC, 256)
        for i in range(4):
            load(sp, cols(d["na_w_o"][0], 256 * i), KC, 256)
        ffn_sp(sp, 0)
        W = d["dil_w_qkv"][0]
        for i in range(12 * GROUPS):
            load(sp, cols(W, 256 * i), KC, 256)
        for i in range(4):
            load(sp, cols(d["dil_w_o"][0], 256 * i), KC, 256)
        ffn_sp(sp, 1)

    def ffn_sp(sp, layer):
        def up(e):
            return [d[n][layer].rearrange("(p c) n -> p c n", p=P)[:, :, bass.ds(e * FF_TILE, FF_TILE)]
                    for n in ("ffn_w_gate", "ffn_w_up")]

        def down(e):
            return d["ffn_w_down"][layer].rearrange("(e p c) n -> e p c n", p=P, c=2)[bass.ds(e, 1)].rearrange(
                "e p c n -> (e p) c n")

        experts_sp(sp, N_FF, up, down)

    def block1_pe(pe):
        pe.wait_ge(S("consts"), 16 * 5)
        norm_pe(pe, NT)
        pe.wait_ge(S("x_split"), X_NO["na"])
        qkv_pe(pe, 0, 0)
        na_attn_pe(pe)
        fence(pe, "na_attn")
        wo_pe(pe, 0)
        fence(pe, "na_out")
        norm_pe(pe, NT)
        pe.wait_ge(S("norm_T"), KC * 2)
        experts_pe(pe, "ff0", N_FF, False)
        fence(pe, "ffn0_out")
        norm_pe(pe, NT)
        pe.wait_ge(S("x_split"), X_NO["dil"])
        for g in range(GROUPS):
            qkv_pe(pe, g, 12 + 12 * g)
        dil_attn_pe(pe)
        fence(pe, "dil_attn")
        wo_pe(pe, 1)
        fence(pe, "dil_out")
        norm_pe(pe, NT)
        pe.wait_ge(S("norm_T"), KC * 4)
        experts_pe(pe, "ff1", N_FF, False)
        fence(pe, "ffn1_out")

    def block1_act(act):
        act.dma_start(x_tok, d["x"][0].rearrange("(t p) c -> p t c", p=P)).then_inc(S("consts"), 16)
        for k, n in enumerate(("norm_mix_pre", "norm_ffn_pre")):
            act.dma_start(gains[:, 2 * k:2 * k + 2, :], d[n].rearrange("l (p c) -> p l c", p=P)).then_inc(S("consts"), 16)
        act.dma_start(cst, d["cst"]).then_inc(S("consts"), 16)
        act.dma_start(na_window, d["na_window"]).then_inc(S("consts"), 16)
        rpb = d["na_rpb"]
        for half in range(2):
            for j in range(6):
                src = bass.AP(tensor=rpb.tensor, offset=(5 - half + j) * RPB_C + NA_COLS - 1 - (GRID_W - 1),
                              ap=[[1, GRID_W], [RPB_R * RPB_C, HEADS], [1, GRID_W]])
                act.dma_start(na_bias[half * 64:half * 64 + 64, :, j, :], src).then_inc(S("na_bias_in"), 16)
        gain_load(act, g_row("norm_mix_post", 0), 0)
        mod_inputs(act)
        act.wait_ge(S("consts"), 16 * 5)
        act.wait_ge(S("eps_set"), 3)
        norm_act(act, x_tok, NT, "rms", aT, gains[:, 0, :], None, NA_QKV)
        x_hi_act(act, "norm_T", 1)
        hi_act(act, NA_QKV + EARLY)
        qkv_move(act, 0, 0, NA_QKV, 0, NA_WO)
        na_attn_act(act)
        fence(act, "na_attn")
        wo_act(act, 0)
        residual_act(act, NA_WO + 4)
        fence(act, "na_out")
        gain_load(act, g_row("norm_ffn_post", 0), 1)
        norm_act(act, x_tok, NT, "rms", aT, gains[:, 2, :], None, FF0)
        experts_act(act, "ff0", N_FF, FF0)
        residual_act(act, DIL_QKV)
        fence(act, "ffn0_out")
        for t in range(NT):
            src = d["neg_dist"][:, t * GROUPS * SEQ:(t + 1) * GROUPS * SEQ]
            act.dma_start(neg_dist[t], src).then_inc(S("stage_in"), 16)
        gain_load(act, g_row("norm_mix_post", 1), 2)
        norm_act(act, x_tok, NT, "rms", aT, gains[:, 1, :], None, DIL_QKV)
        x_hi_act(act, "norm_T", 3)
        hi_act(act, DIL_QKV + EARLY)
        for g in range(GROUPS):
            qkv_move(act, g, 12 + 12 * g, DIL_QKV + 12 * g, 0, DIL_WO)
        dil_attn_act(act)
        fence(act, "dil_attn")
        wo_act(act, 1)
        residual_act(act, DIL_WO + 4)
        fence(act, "dil_out")
        gain_load(act, g_row("norm_ffn_post", 1), 3)
        norm_act(act, x_tok, NT, "rms", aT, gains[:, 3, :], None, FF1)
        mod1_act(act)
        experts_act(act, "ff1", N_FF, FF1)
        residual_act(act, MOD)
        fence(act, "ffn1_out")

    def block1_dve(dve):
        dve.memset(rms_eps, RMS_EPS).then_inc(S("eps_set"), 1)
        dve.memset(ln_eps, LN_EPS).then_inc(S("eps_set"), 1)
        dve.memset(lnx_eps, RWKV_LNX_EPS).then_inc(S("eps_set"), 1)
        dve.wait_ge(S("consts"), 16 * 5)
        norm_dve(dve, x_tok, NT, "rms", NA_QKV)
        x_lo_dve(dve, "na")
        lo_dve(dve, NA_QKV + EARLY)
        qkv_move(dve, 0, 0, NA_QKV, 1, NA_WO)
        na_attn_dve(dve)
        fence(dve, "na_attn")
        wo_dve(dve, 0)
        residual_dve(dve)
        fence(dve, "na_out")
        norm_dve(dve, x_tok, NT, "rms", FF0)
        experts_dve(dve, "ff0", N_FF, FF0, False)
        residual_dve(dve)
        fence(dve, "ffn0_out")
        norm_dve(dve, x_tok, NT, "rms", DIL_QKV)
        x_lo_dve(dve, "dil")
        lo_dve(dve, DIL_QKV + EARLY)
        for g in range(GROUPS):
            qkv_move(dve, g, 12 + 12 * g, DIL_QKV + 12 * g, 1, DIL_WO)
        dil_attn_dve(dve)
        fence(dve, "dil_attn")
        wo_dve(dve, 1)
        residual_dve(dve)
        fence(dve, "dil_out")
        norm_dve(dve, x_tok, NT, "rms", FF1)
        experts_dve(dve, "ff1", N_FF, FF1, False, mod1_take)
        residual_dve(dve)
        fence(dve, "ffn1_out")

    def block1_pool(pool):
        pool.wait_ge(S("consts"), 16 * 5)
        pool.wait_ge(S("na_bias_in"), 16 * 12)
        b = na_bias.rearrange("p h j k -> p (h j) k")
        pool.tensor_tensor(b, b, bc(na_window, 1, 6 * HEADS), ALU.add).then_inc(S("na_bias_ready"), 1)
        for n in ("na_attn", "na_out", "ffn0_out", "dil_attn", "dil_out", "ffn1_out"):
            if n == "ffn1_out":
                mod1_pool(pool)
            fence(pool, n)

    TILES = ALL // P
    KAPPA = float(np.exp(np.float32(-0.5)))
    top[0] = base_top
    vcol = alloc(VCOL_N)
    vrow = alloc(VROW_N)
    mats = alloc(4, 256)
    g1_b = alloc(D)
    g2_b = alloc(D)
    modT = alloc(6, 2, KC)
    z_tok = alloc(NT, 512)
    gqkT = alloc(2, ALL)
    gv_tok = alloc(TILES, 256)
    gdT = alloc(ALL)
    og_tok = alloc(NT, 256)
    dt_raw = alloc(TILES, 16)
    xbcT = alloc(8, ALL)
    rwT = alloc(9, ALL)
    stage_top = top[0]
    y_mix = xn

    def vc(name):
        o, n = VCOL[name]
        return vcol[:, o:o + n]

    def vr(name):
        o, n = VROW[name]
        return vrow[:, o:o + n]

    MOD_1, MOD_2 = (0, 1), (2, 3, 4, 5)

    mod_at = base_top + 8192
    mod1_acc = mem[:, mod_at:mod_at + 4 * D].rearrange("p (j v n) -> p j v n", j=2, v=2)
    mod1_rows = mem[:, mod_at + 4 * D:mod_at + 6 * D].rearrange("p (q n) -> p q n", q=2)
    N_ROWS1 = len(MOD_1) * KC
    assert 4 * ((N_FF - 1) // 2 - 1) == N_ROWS1 and mod_at + 6 * D <= split_at

    def mod_inputs(act):
        act.dma_start(c_in[:, 0, :], d["c_2"][0].rearrange("(p c) -> p c", p=P)).then_inc(S("mod_in"), 16)
        act.dma_start(c_in[:, 1, :], d["c_ctx_2"].rearrange("(p c) -> p c", p=P)).then_inc(S("mod_in"), 16)
        act.dma_start(ada_cols, d["ada_b_2"][0].rearrange("(j p c) -> p j c", j=6, p=P)).then_inc(S("mod_in"), 16)

    def mod1_act(act):
        act.dma_start(vcol, d["vcol"]).then_inc(S("mod_in"), 16)
        act.dma_start(vrow, d["vrow"].to_broadcast([P, VROW_N])).then_inc(S("mod_in"), 16)
        act.dma_start(mats.rearrange("p a b -> p (a b)"), d["mats"]).then_inc(S("mod_in"), 16)
        for g, dst in ((2, g1_b), (5, g2_b)):
            act.dma_start(dst, d["ada_b_2"][:, g * D:(g + 1) * D].to_broadcast([P, D])).then_inc(S("mod_in"), 16)
        act.activation(silu_c.rearrange("p k v -> p v k"), c_in, ACT.Silu).then_inc(S("mod_silu"), 1)

    def mod1_pool(pool):
        W = d["ada_w_2"][0].rearrange("(p c) n -> p c n", p=P)
        link(pool, "pool", pool.memset(mod1_acc.rearrange("p j v n -> p (j v n)"), 0.0))
        pool.wait_ge(S("mod_silu"), 1)
        for h in range(N_ROWS1):
            i, m = divmod(h, 4)
            j = m // 2
            if h >= 2:
                pool.wait_ge(S("mod_used"), h - 1)
            pool.dma_start(mod1_rows[:, h % 2, :], W[:, 2 * i + m % 2, j * D:(j + 1) * D]
                           ).then_inc(S(f"mod_rows{h % 2}"), 16)

    def mod1_take(dve, i, m):
        dve.wait_ge(S(f"mod_rows{m % 2}"), 32 * i + 16 * (m // 2 + 1))
        for v in range(2):
            acc1 = mod1_acc[:, m // 2, v, :]
            s = silu_c[:, bass.ds(2 * i + m % 2, 1), v]
            ins = dve.scalar_tensor_tensor(acc1, mod1_rows[:, m % 2, :], s, acc1, ALU.mult, ALU.add)
        ins.then_inc(S("mod_used"), 1)
        dve.wait_ge(S("mod_used"), 4 * i + (m + 1))

    def mod_pe(pe):
        for j in MOD_1:
            for v in range(2):
                for c in range(KC):
                    ins = pe.matmul(bank(0, 1, (2 * j + v) * KC + c), mod1_acc[:, j, v, c::KC], C("ones")[:, 0:1],
                                    start=True, stop=True)
        ins.then_inc(S("mod_T"), 1)

    def mod_dve(dve):
        dve.wait_ge(S("mod_T"), 1)
        for j in MOD_1:
            dve.scalar_tensor_tensor(modT[:, j, :, :], bank(0, 2 * KC, 2 * j * KC).rearrange("p (v c) -> p v c", v=2),
                                     float(j), bc(ada_cols[:, j, :], 1, 2), ALU.add, ALU.add)

    mod_rows = [aT[:, 4 * q:4 * q + 4, :].rearrange("p c t -> p (c t)") for q in range(2)]
    mod_acc = {2: xn[:, 0, :], 5: xn[:, 1, :], 3: gain_b, 4: hid.rearrange("p a b -> p (a b)")}
    N_ROWS = len(MOD_2) * KC

    def mod2_pool(pool):
        W = d["ada_w_2"][0].rearrange("(p c) n -> p c n", p=P)
        for h in range(N_ROWS):
            j, c = MOD_2[h // KC], h % KC
            if h >= 2:
                pool.wait_ge(S("mod_used"), N_ROWS1 + h - 1)
            pool.dma_start(mod_rows[h % 2], W[:, c, j * D:(j + 1) * D]).then_inc(S(f"mod_rows{h % 2}"), 16)

    def mod2_take(dve, h):
        j, c = MOD_2[h // KC], h % KC
        if h == 0:
            dve.wait_ge(S("norm_turned"), 4 * 6)
        dve.wait_ge(S(f"mod_rows{h % 2}"), 16 * ((N_ROWS1 + h) // 2 + 1))
        if c == 0:
            ins = dve.tensor_scalar(mod_acc[j], mod_rows[h % 2], silu_c[:, c, 0:1], None, ALU.mult)
        else:
            ins = dve.scalar_tensor_tensor(mod_acc[j], mod_rows[h % 2], silu_c[:, c, 0:1], mod_acc[j], ALU.mult, ALU.add)
        ins.then_inc(S("mod_used"), 1)
        dve.wait_ge(S("mod_used"), N_ROWS1 + h + 1)

    def mod2_pe(pe):
        for j, b in ((2, 0), (5, 2)):
            for h in range(2):
                pe.matmul(bank(b + h), C("ones"), mod_acc[j][:, 512 * h:512 * h + 512], start=True, stop=True)
        for m, j in enumerate((3, 4)):
            for c in range(KC):
                ins = pe.matmul(bank(4, 1, 8 * m + c), mod_acc[j][:, c::KC], C("ones")[:, 0:1], start=True, stop=True)
        ins.then_inc(S("mod_sums"), 1)

    def mod2_dve(dve):
        dve.wait_ge(S("mod_sums"), 1)
        for g, b in ((g1_b, 0), (g2_b, 2)):
            dve.tensor_tensor(g, g, banks(b, 2), ALU.add)
        dve.tensor_tensor(modT[:, 3, 0, :], ada_cols[:, 3, :], bank(4, KC), ALU.add)
        dve.scalar_tensor_tensor(modT[:, 4, 0, :], bank(4, KC, 8), 1.0, ada_cols[:, 4, :], ALU.add, ALU.add)

    top[0] = stage_top
    uT = alloc(KC, ALL)
    ctx_tok = rwT.rearrange("p a b -> p (a b)")[:, 0:NT * D].rearrange("p (t c) -> p t c", t=NT)
    MIX = MOD
    Z0, XBC0, DT0, RW0, GQ0, GV0, GD0, OG0 = 0, 512, 1536, 1552, 2704, 2960, 3216, 3248
    rw_in = alloc(9, ALL)

    mix_items = ([(Z0 + 256 * i, 256, "tok_x") for i in range(2)] + [(XBC0 + 256 * i, 256, "chan") for i in range(4)]
                 + [(DT0, 16, "dt")] + [(RW0 + 256 * i, 256, "chan") for i in range(4)] + [(RW0 + 1024, 128, "chan")]
                 + [(GQ0, 256, "chan"), (GV0, 256, "tok_all"), (GD0, 32, "chan"), (OG0, 256, "tok_x")])
    W_OUT = MIX + len(mix_items)

    def mix_jobs():
        for n, (c0, w, kind) in enumerate(mix_items):
            if kind == "tok_x":
                dst = z_tok[:, :, c0:c0 + 256] if c0 < XBC0 else og_tok
                yield n, 0, 1, dst, 1.0
            elif kind == "dt":
                yield n, 0, 1, dt_raw, 1.0
            elif kind == "tok_all":
                for k in range(2):
                    yield n, k, 2, gv_tok[:, 2 * k:2 * k + 2, :], 1.0
            else:
                for k in range(max(1, w // P)):
                    if c0 == GQ0:
                        yield n, k, 2, gqkT[:, k, :], 32 ** -0.5 if k == 0 else 1.0
                    elif c0 == GD0:
                        yield n, 0, 1, gdT[0:32, :], 1.0
                    elif c0 >= RW0:
                        yield n, k, w // P, rw_in[:, (c0 - RW0) // P + k, :], 1.0
                    else:
                        yield n, k, 2, xbcT[:, (c0 - XBC0) // P + k, :], 1.0

    def mix_in_sp(sp):
        for c0, w, _ in mix_items:
            load(sp, cols(d["w_in_2"][0], c0, w), KC, w)

    def mix_in_pe(pe):
        pe.wait_ge(S("norm_T"), KC * 6)
        w = None
        for m, (n, k, parts, dst, f) in enumerate(mix_jobs()):
            c0, width, kind = mix_items[n]
            if k == 0:
                w = take(pe, KC, width)
            if m >= 4:
                pe.wait_ge(S(f"mix_moved{m % 2}"), (m - 4) // 2 + 1)
            b = 4 + m % 4
            if kind == "chan":
                wd = min(P, width)
                for c in range(KC):
                    ins = pe.matmul(psum[0:wd, b, 0:ALL], w[:, c, k * P:k * P + wd], uT[:, c, :], start=c == 0,
                                    stop=c == KC - 1)
            else:
                tiles = {"tok_x": (2, 3), "tok_all": (2 * k, 2 * k + 1), "dt": range(TILES)}[kind]
                for a, t in enumerate(tiles):
                    for c in range(KC):
                        ins = pe.matmul(bank(b, width, a * width), uT[:, c, t * P:(t + 1) * P], w[:, c, :],
                                        start=c == 0, stop=c == KC - 1)
            ins.then_inc(S("item_used") if k == parts - 1 else S("mix_half"), 1)

    def mix_move(eng, parity):
        halves = rows = 0
        for m, (n, k, parts, dst, f) in enumerate(mix_jobs()):
            if k < parts - 1:
                halves += 1
            if m % 2 != parity:
                continue
            if k == parts - 1:
                eng.wait_ge(S("item_used"), MIX + n + 1)
            else:
                eng.wait_ge(S("mix_half"), halves)
            b = 4 + m % 4
            if len(dst.shape) == 2:
                src = psum[0:dst.shape[0], b, 0:ALL]
            else:
                src = bank(b, dst.shape[1] * dst.shape[2]).rearrange("p (a b) -> p a b", a=dst.shape[1])
            if parity == 0:
                ins = nc.scalar.activation(dst, src, ACT.Copy, scale=f)
            else:
                ins = nc.vector.tensor_scalar(dst, src, f, None, ALU.mult)
            ins.then_inc(S(f"mix_moved{parity}"), 1)
            if parity == 1:
                for _ in range(2):
                    if rows < N_ROWS:
                        mod2_take(eng, rows)
                        rows += 1
        if parity == 1:
            while rows < N_ROWS:
                mod2_take(eng, rows)
                rows += 1

    acc = [uT[:, j, :] for j in range(4)]

    def seg(ap, a, b):
        return ap.rearrange("p (s t) -> p s t", s=2)[:, :, a:b]

    def conv_act(act):
        cw, cb = vc("conv_w"), vc("conv_b")
        act.wait_ge(S("mix_moved1"), MIX_MOVED[1])
        for j in range(8):
            if j >= 4:
                act.wait_ge(S("conv_silu"), j - 3)
            act.activation(acc[j % 4], xbcT[:, j, :], ACT.Identity, scale=cw[:, 8 + j:9 + j], bias=cb[:, j:j + 1]
                           ).then_inc(S("conv_mid"), 1)
            if j >= 2:
                silu_act(act, j - 2)
        silu_act(act, 6)
        silu_act(act, 7)
        act.wait_ge(S("shift_coef"), 1)
        for j in range(9):
            for s in range(2):
                act.activation(rwT[:, j, s * 256:s * 256 + 256], rw_in[:, j, s * 256:s * 256 + 256], ACT.Copy,
                               scale=shift_c[:, s, j:j + 1]).then_inc(S("shift_mid"), 1)

    def silu_act(act, j):
        act.wait_ge(S("conv_taps"), j + 1)
        act.activation(xbcT[:, j, :], acc[j % 4], ACT.Silu).then_inc(S("conv_silu"), 1)

    shift_c = gate_act[:, 0:18].rearrange("p (s j) -> p s j", s=2)

    def conv_dve(dve):
        cw, mu = vc("conv_w"), vc("mu").rearrange("p (m j) -> p m j", m=4)
        link(dve, "dve", dve.tensor_tensor(shift_c[:, 0, :], mu[:, 0, :], mu[:, 1, :], ALU.add))
        link(dve, "dve", dve.tensor_tensor(shift_c[:, 1, :], mu[:, 2, :], mu[:, 3, :], ALU.add))
        link(dve, "dve", dve.tensor_tensor(shift_c[:, 1, :], shift_c[:, 1, :], shift_c[:, 0, :], ALU.add))
        dve.tensor_scalar(gate_act[:, 0:18], gate_act[:, 0:18], -1.0, 1.0, ALU.mult, ALU.add).then_inc(S("shift_coef"), 1)
        for j in range(8):
            dve.wait_ge(S("conv_mid"), j + 1)
            a, x = acc[j % 4], xbcT[:, j, :]
            link(dve, "dve", dve.scalar_tensor_tensor(seg(a, 1, 256), seg(x, 0, 255), cw[:, j:j + 1], seg(a, 1, 256),
                                                      ALU.mult, ALU.add))
            dve.scalar_tensor_tensor(seg(a, 0, 255), seg(x, 1, 256), cw[:, 16 + j:17 + j], seg(a, 0, 255),
                                     ALU.mult, ALU.add).then_inc(S("conv_taps"), 1)
        for j in range(9):
            dve.wait_ge(S("shift_mid"), 2 * j + 2)
            o, x = rwT[:, j, :], rw_in[:, j, :]

            def add(dst, src, m):
                link(dve, "dve", dve.scalar_tensor_tensor(dst, src, mu[:, m, j:j + 1], dst, ALU.mult, ALU.add))

            add(o[:, 1:256], x[:, 0:255], 0)
            add(o[:, 0:255], x[:, 1:256], 1)
            og, xg = (v[:, 256:512].rearrange("p (r c) -> p r c", r=GRID_H) for v in (o, x))
            add(og[:, :, 1:GRID_W], xg[:, :, 0:GRID_W - 1], 0)
            add(og[:, :, 0:GRID_W - 1], xg[:, :, 1:GRID_W], 1)
            add(o[:, 256 + GRID_W:512], x[:, 256:512 - GRID_W], 2)
            add(o[:, 256:512 - GRID_W], x[:, 256 + GRID_W:512], 3)

    top[0] = stage_top
    lev_masks = alloc(15, P, dt=I32)
    la = alloc(TILES, 256)
    la_e = alloc(TILES, 256)
    gl_E = alloc(2, 256)
    gl_q = alloc(2, 256)
    gl_k = alloc(2, 256)
    gl_acc = alloc(4, NT, P)
    gl_cum = alloc(256)
    gl_rest = alloc(ALL)
    gl_tot = alloc(TILES)
    gl_kt = alloc(TILES, P)
    gl_S = alloc(3, 256)
    gl_y = alloc(NT, 256)
    gl_t = alloc(NT, 256)

    def gla_order(dr):
        return (0, 1, 2, 3) if dr == 0 else (1, 0, 3, 2)

    def gla_pe(pe):
        first_y = [True]

        def ymm(t, lo, n, lhs, rhs, last=False):
            ins = pe.matmul(bank(7, n, t * 256 + lo), lhs, rhs, start=first_y[0], stop=last, skip_group_check=True)
            first_y[0] = False
            return ins

        gu = mats[0:32, 3, :]
        for t in range(TILES):
            ins = pe.matmul(bank(t // 2, 256, (t % 2) * 256), gdT[0:32, t * P:(t + 1) * P], gu, start=True, stop=True)
        ins.then_inc(S("gl_z"), 1)
        pe.wait_ge(S("gl_la"), 1)
        for dr in range(2):
            if dr:
                pe.wait_ge(S("gl_decay"), 3 * dr)
                pe.wait_ge(S("gl_acc_n"), 8)
                pe.wait_ge(S("gl_S_n"), 3)
            for a, t in enumerate((2, 3)):
                pe.matmul(bank(2, P, a * P), la[:, t, dr * P:(dr + 1) * P], C(f"cum{dr}"), start=True, stop=True)
            for t in range(TILES):
                ins = pe.matmul(bank(3, P, t * P), la[:, t, dr * P:(dr + 1) * P], C(f"rest{dr}"), start=True, stop=True)
            for t in range(TILES):
                ins = pe.matmul(bank(2, 1, 256 + t), la[:, t, dr * P:(dr + 1) * P], C("ones")[:, 0:1], start=True, stop=True)
            ins.then_inc(S("gl_sums"), 1)
            pe.wait_ge(S("gl_kdec"), dr + 1)
            for t in range(TILES):
                ins = pe.transpose(bank(6, P, t * P), gl_rest[:, t * P:(t + 1) * P], ident)
            ins.then_inc(S("gl_kturn"), 1)
            pe.wait_ge(S("gl_kt"), dr + 1)
            order = gla_order(dr)
            for k in range(3):
                o = bank(6, 256, 0) if k == 0 else (bank(6, 256, 256) if k == 1 else bank(3, 256, 0))
                ins = pe.matmul(o, gl_kt[:, order[k], :], gv_tok[:, order[k], :], start=True, stop=True)
            ins.then_inc(S("gl_adds"), 1)
            for n in range(8):
                m = 8 * dr + n
                if n < 7:
                    if n >= 2:
                        pe.wait_ge(S("gl_E_n"), 7 * dr + n - 1)
                    for a, t in enumerate((2, 3)):
                        ins = pe.matmul(bank(n % 2, P, a * P), la[:, t, dr * P:(dr + 1) * P], C(f"lev{dr}_{n}"),
                                        start=True, stop=True)
                    ins.then_inc(S("gl_lev"), 1)
                if n >= 1:
                    gla_scores(pe, dr, n - 1)
            gla_scores(pe, dr, 7)
            for k in range(2):
                t = order[2 + k] - 2
                ymm(t, 0, 256, gl_cum[:, t * P:(t + 1) * P], gl_S[:, 1 + k, :])
            pe.wait_ge(S("gl_acc_n"), 8 * dr + 8)
            for t in range(NT):
                for h in range(4):
                    ins = ymm(t, h * 64, 64, gl_acc[:, h, t, :], gv_tok[:, 2 + t, h * 64:(h + 1) * 64], dr == 1)
            ins.then_inc(S("gl_pv"), 1)

    def gla_scores(pe, dr, n):
        m = 8 * dr + n
        if n < 7:
            pe.wait_ge(S("gl_q_n"), 7 * dr + n + 1)
            pe.wait_ge(S("gl_k_n"), 7 * dr + n + 1)
            q, k = gl_q[:, n % 2, :], gl_k[:, n % 2, :]
        else:
            q, k = gqkT[:, 0, CTX:ALL], gqkT[:, 1, CTX:ALL]
        if n == 0:
            pe.wait_ge(S("gl_S_n"), 3 * dr + 3)
        if m >= 1:
            pe.wait_ge(S("gl_acc_n"), m)
        for t in range(NT):
            for h in range(4):
                r = slice(32 * h, 32 * h + 32)
                ins = pe.matmul(bank(3 + h, P, t * P), k[r, t * P:(t + 1) * P], q[r, t * P:(t + 1) * P], start=True,
                                stop=True, tile_position=(32 * h, 0))
        ins.then_inc(S("gl_sc"), 1)

    def gla_act(act):
        act.dma_start(lev_masks.rearrange("p a b -> p (a b)"), d["lev_masks"]).then_inc(S("stage_in"), 16)
        act.wait_ge(S("gl_na"), 1)
        link(act, "act", act.activation(la_e, la_e, ACT.Exp))
        act.activation(la_e, la_e, ACT.Ln, bias=1.0).then_inc(S("gl_ln"), 1)
        act.wait_ge(S("gl_ln"), 1)
        for dr in range(2):
            act.wait_ge(S("gl_sums"), dr + 1)
            if dr:
                act.wait_ge(S("gl_pv"), dr)
            act.activation(gl_rest, bank(3), ACT.Exp, scale=1 / 16).then_inc(S("gl_decay"), 1)
            act.activation(gl_cum, bank(2, 256), ACT.Exp, scale=1 / 16).then_inc(S("gl_decay"), 1)
            act.activation(gl_tot, bank(2, TILES, 256), ACT.Exp, scale=1 / 16).then_inc(S("gl_decay"), 1)
            act.wait_ge(S("gl_kturn"), dr + 1)
            act.activation(gl_kt, bank(6).rearrange("p (t c) -> p t c", t=TILES), ACT.Copy).then_inc(S("gl_kt"), 1)
            for n in range(7):
                act.wait_ge(S("gl_lev"), 7 * dr + n + 1)
                if n >= 2 or dr:
                    used = 7 * dr + (n - 1 if n else 0)
                    act.wait_ge(S("gl_q_n"), used)
                    act.wait_ge(S("gl_k_n"), used)
                act.activation(gl_E[:, n % 2, :], bank(n % 2, 256), ACT.Exp, scale=1 / 16).then_inc(S("gl_E_n"), 1)
        act.wait_ge(S("gl_og"), 1)
        act.activation(og_tok, og_tok, ACT.Silu).then_inc(S("gate_silu"), 1)
        act.wait_ge(S("group_sums"), 1)
        act.activation(stat[:, 1, 0:8], stat[:, 0, 0:8], ACT.Sqrt, scale=1 / 64, bias=ln_eps).then_inc(S("group_root"), 1)

    def gla_dve(dve):
        dve.wait_ge(S("gl_z"), 1)
        gb = vr("gla_gb")
        link(dve, "dve", dve.tensor_tensor(la, psum[:, 0:2, :].rearrange("p b (t c) -> p (b t) c", t=2), bc(gb, 1, TILES),
                                           ALU.add))
        dve.scalar_tensor_tensor(la_e, la, -1.0, la, ALU.mult, ALU.min).then_inc(S("gl_na"), 1)
        dve.wait_ge(S("gl_ln"), 1)
        dve.scalar_tensor_tensor(la, la, 0.0, la_e, ALU.min, ALU.subtract).then_inc(S("gl_la"), 1)
        dve.wait_ge(S("stage_in"), 16 * 4)
        for dr in range(2):
            dve.wait_ge(S("gl_decay"), 3 * dr + 1)
            dve.tensor_tensor(gl_rest, gl_rest, gqkT[:, 1, :], ALU.mult).then_inc(S("gl_kdec"), 1)
            dve.wait_ge(S("gl_decay"), 3 * dr + 3)
            link(dve, "dve", dve.tensor_tensor(gl_cum, gl_cum, gqkT[:, 0, CTX:ALL], ALU.mult))
            link(dve, "dve", dve.memset(gl_acc, 0.0))
            dve.wait_ge(S("gl_adds"), dr + 1)
            order = gla_order(dr)
            diag = C("gla_diag")
            for k in range(3):
                src = bank(6, 256, 0) if k == 0 else (bank(6, 256, 256) if k == 1 else bank(3, 256, 0))
                if k == 0:
                    dve.tensor_tensor(gl_S[:, 0, :], src, diag, ALU.mult).then_inc(S("gl_S_n"), 1)
                else:
                    link(dve, "dve", dve.tensor_tensor(gl_t[:, 0, :], src, diag, ALU.mult))
                    tot = gl_tot[:, order[k]:order[k] + 1]
                    dve.scalar_tensor_tensor(gl_S[:, k, :], gl_S[:, k - 1, :], tot, gl_t[:, 0, :], ALU.mult, ALU.add
                                             ).then_inc(S("gl_S_n"), 1)
                dve.wait_ge(S("gl_S_n"), 3 * dr + k + 1)
            for n in range(8):
                if n < 7:
                    dve.wait_ge(S("gl_E_n"), 7 * dr + n + 1)
                    if 8 * dr + n >= 2:
                        dve.wait_ge(S("gl_sc"), 8 * dr + n - 1)
                    dve.tensor_tensor(gl_q[:, n % 2, :], gqkT[:, 0, CTX:ALL], gl_E[:, n % 2, :], ALU.mult
                                      ).then_inc(S("gl_q_n"), 1)
                if n >= 1:
                    gla_pick(dve, dr, n - 1)
            gla_pick(dve, dr, 7)
        dve.memset(gl_t, 0.0).then_inc(S("gl_og"), 1)
        dve.wait_ge(S("gl_pv"), 2)
        link(dve, "dve", dve.tensor_copy(gl_y, bank(7).rearrange("p (t c) -> p t c", t=NT)))
        link(dve, "dve", dve.tensor_tensor(gl_t, gl_y, gl_y, ALU.mult))
        dve.tensor_reduce(stat[:, 0, 0:8].rearrange("p (t h) -> p t h", t=2), gl_t.rearrange("p t (h e) -> p t h e", h=4),
                          X, ALU.add).then_inc(S("group_sums"), 1)
        dve.wait_ge(S("group_root"), 1)
        link(dve, "dve", dve.reciprocal(stat[:, 3, 0:8], stat[:, 1, 0:8]))
        dve.wait_ge(S("gate_silu"), 1)
        for t in range(NT):
            y3 = gl_y[:, t, :].rearrange("p (h e) -> p h e", h=4)
            link(dve, "dve", dve.tensor_tensor(y3, y3, bc(stat[:, 3, 4 * t:4 * t + 4], 2, 64), ALU.mult))
            link(dve, "dve", dve.tensor_tensor(gl_y[:, t, :], gl_y[:, t, :], vr("gla_norm_w"), ALU.mult))
            link(dve, "dve", dve.tensor_tensor(y_mix[:, t, 768:1024], gl_y[:, t, :], og_tok[:, t, :], ALU.mult))

    def gla_pick(dve, dr, n):
        dve.wait_ge(S("gl_sc"), 8 * dr + n + 1)
        mask = lev_masks[:, 7 * dr + n if n < 7 else 14, :]
        dve.copy_predicated(gl_acc, bc(bc(mask, 1, NT), 1, 4),
                            psum[:, 3:7, 0:SEQ].rearrange("p h (t i) -> p h t i", t=NT)
                            ).then_inc(S("gl_acc_n"), 1)

    def gla_pool(pool):
        for dr in range(2):
            for n in range(7):
                pool.wait_ge(S("gl_E_n"), 7 * dr + n + 1)
                if 8 * dr + n >= 2:
                    pool.wait_ge(S("gl_sc"), 8 * dr + n - 1)
                pool.tensor_tensor(gl_k[:, n % 2, :], gqkT[:, 1, CTX:ALL], gl_E[:, n % 2, :], ALU.mult
                                   ).then_inc(S("gl_k_n"), 1)

    MIX_MOVED = [sum(1 for m, _ in enumerate(mix_jobs()) if m % 2 == q) for q in range(2)]

    top[0] = stage_top
    tri = alloc(2, 9, P)
    gla_in = mem[:, stage_top - 9 * ALL - 8 * ALL - TILES * 16 - 3072:][:, 0:3072]
    xs_tok = gla_in[:, 0:2048].rearrange("p (t c) -> p t c", t=TILES)
    b_tok = gla_in[:, 2048:3072].rearrange("p (t c) -> p t c", t=TILES)
    dtv = alloc(TILES, 16)
    loga = alloc(TILES, 16)
    sp_t = alloc(4, 64)
    sums = alloc(2, 3, TILES, 8)
    esums = alloc(2, 3, TILES, 8)
    sd_sc = alloc(2, NT, 2, P)
    sd_L = alloc(8, P)
    sd_xdt = alloc(512)
    sd_xde = alloc(512)
    sd_h = alloc(3, 512)
    sd_y = alloc(NT, 512)
    sd_t = alloc(512)

    def ssd_pe(pe):
        for t in range(TILES):
            if t >= 2:
                pe.wait_ge(S("sd_turn_out"), 2 * (t - 1))
            for j in range(4):
                pe.transpose(bank(2 * (t % 2), P, j * P), xbcT[:, j, t * P:(t + 1) * P], ident)
            for j in range(2):
                ins = pe.transpose(bank(2 * (t % 2) + 1, P, j * P), xbcT[:, 4 + j, t * P:(t + 1) * P], ident)
            ins.then_inc(S("sd_turn"), 1)
        pe.wait_ge(S("sd_loga"), 1)
        for dr in range(2):
            for n, lhs in enumerate((C(f"cum{dr}"), C(f"rest{dr}"), C("ones"))):
                for t in range(TILES):
                    ins = pe.matmul(bank(4, 8, ((dr * 3 + n) * TILES + t) * 8), lhs, loga[:, t, dr * 8:dr * 8 + 8],
                                    start=True, stop=True)
        ins.then_inc(S("sd_sums"), 1)
        pe.wait_ge(S("sd_turn_out"), 2 * TILES)
        for t in range(NT):
            tok = slice(CTX + t * P, CTX + (t + 1) * P)
            for g in range(2):
                ins = pe.matmul(bank(2, P, (2 * t + g) * P), xbcT[:, 4 + g, tok], xbcT[:, 6 + g, tok], start=True,
                                stop=True)
        ins.then_inc(S("sd_scores"), 1)
        for dr in range(2):
            order = gla_order(dr)
            for k in range(3):
                m = 3 * dr + k
                pe.wait_ge(S("sd_xde_n"), m + 1)
                if m:
                    pe.wait_ge(S("sd_h_n"), m)
                for g in range(2):
                    ins = pe.matmul(bank(3, 256, g * 256), b_tok[:, order[k], g * P:(g + 1) * P],
                                    sd_xde[:, g * 256:(g + 1) * 256], start=True, stop=True)
                ins.then_inc(S("sd_adds"), 1)
            for k in range(2):
                t = order[2 + k] - 2
                m = 2 * dr + k
                tok = slice(CTX + t * P, CTX + (t + 1) * P)
                if m:
                    pe.wait_ge(S("sd_seg"), m)
                for h in range(8):
                    ins = pe.matmul(banks(0, 2)[:, h * P:(h + 1) * P],
                                    loga[:, 2 + t, dr * 8 + h:dr * 8 + h + 1].to_broadcast([P, P]), C(f"cum{dr}"),
                                    start=True, stop=True)
                ins.then_inc(S("sd_rows"), 1)
                if m:
                    pe.wait_ge(S("sd_off"), m)
                pe.wait_ge(S("sd_h_n"), 3 * dr + 2 + k)
                for g in range(2):
                    ins = pe.matmul(bank(7, 256, g * 256), xbcT[:, 6 + g, tok], sd_h[:, 1 + k, g * 256:(g + 1) * 256],
                                    start=True, stop=True)
                ins.then_inc(S("sd_inter"), 1)
                pe.wait_ge(S("sd_M"), m + 1)
                for h in range(8):
                    ins = pe.matmul(bank(5 + t, 64, h * 64), sd_L[:, h, :], sd_xdt[:, h * 64:(h + 1) * 64],
                                    start=dr == 0 and h == 0, stop=dr == 1, skip_group_check=True)
                ins.then_inc(S("sd_diag"), 1)

    def ssd_act(act):
        act.dma_start(tri.rearrange("p a b c -> p (a b c)"), d["tri_masks"]).then_inc(S("stage_in"), 16)
        act.activation(vr("a_log"), vr("a_log"), ACT.Exp).then_inc(S("sd_a"), 1)
        act.wait_ge(S("sd_na"), 1)
        act.activation(sp_t[:, 1, :], sp_t[:, 0, :], ACT.Exp).then_inc(S("sd_e"), 1)
        act.wait_ge(S("sd_u"), 1)
        act.activation(sp_t[:, 3, :], sp_t[:, 2, :], ACT.Ln).then_inc(S("sd_ln"), 1)
        for t in range(TILES):
            act.wait_ge(S("sd_turn"), t + 1)
            act.activation(xs_tok[:, t, :], bank(2 * (t % 2)), ACT.Copy).then_inc(S("sd_turn_out"), 1)
            act.activation(b_tok[:, t, :], bank(2 * (t % 2) + 1, 256), ACT.Copy).then_inc(S("sd_turn_out"), 1)
        act.wait_ge(S("sd_sums"), 1)
        act.activation(esums.rearrange("p a b c d -> p (a b c d)"), bank(4, 192), ACT.Exp).then_inc(S("sd_esums"), 1)
        for m in range(4):
            act.wait_ge(S("sd_seg"), m + 1)
            act.activation(sd_L, sd_L, ACT.Exp).then_inc(S("sd_L"), 1)
        act.activation(z_tok, z_tok, ACT.Silu).then_inc(S("gate_silu"), 1)
        act.wait_ge(S("group_sums"), 2)
        act.activation(stat[:, 1, 0:4], stat[:, 0, 0:4], ACT.Sqrt, scale=1 / 256, bias=ln_eps).then_inc(S("group_root"), 1)

    def ssd_dve(dve):
        def v(a):
            return a.rearrange("p a b -> p (a b)")

        link(dve, "dve", dve.tensor_tensor(dtv, dt_raw, bc(vr("dt_bias"), 1, TILES), ALU.add))
        dve.scalar_tensor_tensor(sp_t[:, 0, :], v(dtv), -1.0, v(dtv), ALU.mult, ALU.min).then_inc(S("sd_na"), 1)
        dve.wait_ge(S("sd_e"), 1)
        dve.tensor_scalar(sp_t[:, 2, :], sp_t[:, 1, :], 1.0, None, ALU.add).then_inc(S("sd_u"), 1)
        dve.wait_ge(S("sd_u"), 1)
        link(dve, "dve", dve.tensor_scalar(sp_t[:, 0, :], sp_t[:, 2, :], 1.0, None, ALU.is_equal))
        dve.wait_ge(S("sd_ln"), 1)
        link(dve, "dve", dve.tensor_tensor(sp_t[:, 3, :], sp_t[:, 3, :], sp_t[:, 0, :], ALU.add))
        link(dve, "dve", dve.scalar_tensor_tensor(sp_t[:, 2, :], sp_t[:, 2, :], 1.0, sp_t[:, 0, :], ALU.subtract, ALU.add))
        link(dve, "dve", dve.reciprocal(sp_t[:, 2, :], sp_t[:, 2, :]))
        link(dve, "dve", dve.tensor_tensor(sp_t[:, 3, :], sp_t[:, 3, :], sp_t[:, 2, :], ALU.mult))
        link(dve, "dve", dve.tensor_tensor(sp_t[:, 3, :], sp_t[:, 3, :], sp_t[:, 1, :], ALU.mult))
        link(dve, "dve", dve.scalar_tensor_tensor(v(dtv), v(dtv), 0.0, sp_t[:, 3, :], ALU.max, ALU.add))
        dve.wait_ge(S("sd_a"), 1)
        link(dve, "dve", dve.tensor_tensor(loga, dtv, bc(vr("a_log"), 1, TILES), ALU.mult))
        dve.tensor_scalar(v(loga), v(loga), -1.0, None, ALU.mult).then_inc(S("sd_loga"), 1)
        dve.wait_ge(S("sd_sums"), 1)
        dve.wait_ge(S("sd_esums"), 1)
        link(dve, "dve", dve.tensor_copy(sums.rearrange("p a b c d -> p (a b c d)"), bank(4, 192)))
        dve.wait_ge(S("stage_in"), 16 * 5)
        dve.wait_ge(S("sd_scores"), 1)
        for dr in range(2):
            for t in range(NT):
                link(dve, "dve", dve.tensor_tensor(sd_sc[:, dr, t, :, :], bank(2, 256, t * 256).rearrange("p (g i) -> p g i", g=2),
                                                   bc(tri[:, dr, 0, :], 1, 2), ALU.mult))
        dve.wait_ge(S("sd_turn_out"), 2 * TILES)
        off = gain_b.rearrange("p (t c) -> p t c", t=NT)
        for dr in range(2):
            order = gla_order(dr)

            def xdt(t, dst):
                link(dve, "dve", dve.tensor_tensor(dst.rearrange("p (h e) -> p h e", h=8),
                                                   xs_tok[:, t, :].rearrange("p (h e) -> p h e", h=8),
                                                   bc(dtv[:, t, dr * 8:dr * 8 + 8], 2, 64), ALU.mult))

            for k in range(3):
                m = 3 * dr + k
                t = order[k]
                if m:
                    dve.wait_ge(S("sd_adds"), m)
                xdt(t, sd_xde)
                dve.tensor_tensor(sd_xde.rearrange("p (h e) -> p h e", h=8), sd_xde.rearrange("p (h e) -> p h e", h=8),
                                  bc(esums[:, dr, 1, t, :], 2, 64), ALU.mult).then_inc(S("sd_xde_n"), 1)
                dve.wait_ge(S("sd_adds"), m + 1)
                if k == 0:
                    if dr:
                        dve.wait_ge(S("sd_inter"), 2)
                    dve.tensor_copy(sd_h[:, 0, :], bank(3)).then_inc(S("sd_h_n"), 1)
                else:
                    link(dve, "dve", dve.tensor_tensor(sd_t.rearrange("p (h e) -> p h e", h=8),
                                                       sd_h[:, k - 1, :].rearrange("p (h e) -> p h e", h=8),
                                                       bc(esums[:, dr, 2, t, :], 2, 64), ALU.mult))
                    dve.tensor_tensor(sd_h[:, k, :], sd_t, bank(3), ALU.add).then_inc(S("sd_h_n"), 1)
                dve.wait_ge(S("sd_h_n"), m + 1)
            for k in range(2):
                t = order[2 + k] - 2
                m = 2 * dr + k
                dve.wait_ge(S("sd_rows"), m + 1)
                if m:
                    dve.wait_ge(S("sd_diag"), m)
                link(dve, "dve", dve.tensor_tensor(sd_L, banks(0, 2).rearrange("p (h i) -> p h i", h=8),
                                                   bc(sums[:, dr, 0, 2 + t, :], 2, P), ALU.subtract))
                dve.tensor_scalar(sd_L, sd_L, 0.0, None, ALU.min).then_inc(S("sd_seg"), 1)
                xdt(2 + t, sd_xdt)
                dve.wait_ge(S("sd_inter"), m + 1)
                o3 = off[:, t, :].rearrange("p (h e) -> p h e", h=8)
                src = bank(7).rearrange("p (h e) -> p h e", h=8)
                e3 = bc(esums[:, dr, 0, 2 + t, :], 2, 64)
                if dr == 0:
                    dve.tensor_tensor(o3, src, e3, ALU.mult).then_inc(S("sd_off"), 1)
                    dve.wait_ge(S("sd_off"), m + 1)
                else:
                    dve.tensor_tensor(sd_t.rearrange("p (h e) -> p h e", h=8), src, e3, ALU.mult).then_inc(S("sd_off"), 1)
                    dve.wait_ge(S("sd_off"), m + 1)
                    link(dve, "dve", dve.tensor_tensor(off[:, t, :], off[:, t, :], sd_t, ALU.add))
                dve.wait_ge(S("sd_L"), m + 1)
                for g in range(2):
                    ins = dve.tensor_tensor(sd_L[:, 4 * g:4 * g + 4, :], sd_L[:, 4 * g:4 * g + 4, :],
                                            bc(sd_sc[:, dr, t, g, :], 1, 4), ALU.mult)
                ins.then_inc(S("sd_M"), 1)
        dve.wait_ge(S("sd_diag"), 4)
        dve.wait_ge(S("gate_silu"), 2)
        for t in range(NT):
            y, y3 = sd_y[:, t, :], sd_y[:, t, :].rearrange("p (h e) -> p h e", h=8)
            link(dve, "dve", dve.tensor_tensor(y3, xs_tok[:, 2 + t, :].rearrange("p (h e) -> p h e", h=8),
                                               bc(vr("ssd_d"), 2, 64), ALU.mult))
            link(dve, "dve", dve.tensor_tensor(y, y, bank(5 + t), ALU.add))
            link(dve, "dve", dve.tensor_tensor(y, y, off[:, t, :], ALU.add))
            link(dve, "dve", dve.tensor_tensor(y, y, z_tok[:, t, :], ALU.mult))
            link(dve, "dve", dve.tensor_tensor(sd_t, y, y, ALU.mult))
            ins = dve.tensor_reduce(stat[:, 0, 2 * t:2 * t + 2], sd_t.rearrange("p (g e) -> p g e", g=2), X, ALU.add)
            if t:
                ins.then_inc(S("group_sums"), 1)
            else:
                link(dve, "dve", ins)
        dve.wait_ge(S("group_root"), 2)
        link(dve, "dve", dve.reciprocal(stat[:, 3, 0:4], stat[:, 1, 0:4]))
        for t in range(NT):
            y2 = sd_y[:, t, :].rearrange("p (g e) -> p g e", g=2)
            link(dve, "dve", dve.tensor_tensor(y2, y2, bc(stat[:, 3, 2 * t:2 * t + 2], 2, 256), ALU.mult))
            link(dve, "dve", dve.tensor_tensor(y_mix[:, t, 0:512], sd_y[:, t, :], vr("ssd_norm_w"), ALU.mult))

    top[0] = stage_top - 8 * ALL - TILES * 16 - NT * 256 - ALL - TILES * 256 - 2 * ALL - NT * 512 - 9 * ALL
    rwkv_bottom = top[0]
    rk = rwT
    low_end = stage_top - 9 * ALL
    kkT = alloc(2, ALL)
    v_t = alloc(TILES, 256)
    khT = alloc(2, ALL)
    rhT = alloc(2, SEQ)
    btok = alloc(TILES, 256)
    ktok = alloc(TILES, 256)
    w1 = alloc(TILES, 256)
    arb = alloc(NT, 4, P)
    bonusT = alloc(2, SEQ)
    assert top[0] <= low_end, (top[0], low_end)
    top[0] = stage_top
    tt = alloc(TILES, 4, P)
    ab = alloc(TILES, 4, P)
    tf = alloc(TILES, 4, P)
    xf = alloc(2, 4, P)
    bT, kT2 = (tf.rearrange("p a b c -> p (a b c)")[:, n * 1024:(n + 1) * 1024].rearrange("p (a b) -> p a b", a=2)
               for n in range(2))
    lw = ab.rearrange("p a b c -> p (a b c)")[:, 0:1024].rearrange("p (t c) -> p t c", t=TILES)
    aTt = ab.rearrange("p a b c -> p (a b c)")[:, 1024:2048].rearrange("p (a b) -> p a b", a=2)
    spare = aT.rearrange("p a b -> p (a b)")
    ex = spare[:, 0:1024].rearrange("p (a b) -> p a b", a=2)
    uu = spare[:, 0:1024].rearrange("p (t c) -> p t c", t=TILES)
    akm = spare[:, 1024:1536].rearrange("p (h i) -> p h i", h=4)
    st = spare[:, 1536:1792].rearrange("p (a b) -> p a b", a=2)
    ur = spare[:, 1792:2048]
    lmask = alloc(2, 4, P)
    tri2 = alloc(9, P)
    dcol = alloc(2, TILES, 4)
    dec = alloc(2, 8)
    rk_g = gain_b[:, 0:512].rearrange("p (t c) -> p t c", t=NT)
    yk = gate_act.rearrange("p (t c) -> p t c", t=NT)
    yk2 = hid.rearrange("p a b -> p (a b)")[:, 0:512].rearrange("p (t c) -> p t c", t=NT)
    bon = alloc(NT, 4)

    def rwkv_once_pe(pe):
        pe.wait_ge(S("rk_sq"), 1)
        for p2 in range(2):
            ins = pe.matmul(bank(p2), C("head_sum"), khT[:, p2, :], start=True, stop=True)
        ins.then_inc(S("rk_ss"), 1)
        for t in range(TILES):
            for j in range(2):
                ins = pe.transpose(bank(2 + t // 2, P, (t % 2) * 256 + j * P), rk[:, 4 + j, t * P:(t + 1) * P], ident)
        ins.then_inc(S("rk_v"), 1)
        pe.wait_ge(S("rk_sig"), 1)
        for t in range(NT):
            ins = pe.matmul(bank(4, 256, t * 256), rk[:, 8, CTX + t * P:CTX + (t + 1) * P], mats[:, 2, :], start=True,
                            stop=True)
        ins.then_inc(S("rk_gate"), 1)

    def rwkv_once_act(act):
        act.activation(rk[:, 6, :], rk[:, 6, :], ACT.Tanh).then_inc(S("rk_tanh"), 1)
        act.activation(rk[:, 8, CTX:ALL], rk[:, 8, CTX:ALL], ACT.Sigmoid).then_inc(S("rk_sig"), 1)
        act.wait_ge(S("rk_v"), 1)
        act.activation(v_t, psum[:, 2:4, :].rearrange("p b (t c) -> p (b t) c", t=2), ACT.Copy).then_inc(S("rk_vt"), 1)
        act.wait_ge(S("rk_gate"), 1)
        act.activation(rk_g, bank(4).rearrange("p (t c) -> p t c", t=NT), ACT.Copy).then_inc(S("rk_vt"), 1)
        act.wait_ge(S("rk_ss"), 1)
        for p2 in range(2):
            ins = act.activation(khT[:, p2, :], bank(p2), ACT.Sqrt)
        ins.then_inc(S("rk_norm"), 1)

    def rwkv_once_dve(dve):
        for p2 in range(2):
            ins = dve.tensor_scalar(kkT[:, p2, :], rk[:, 2 + p2, :], vc("rwkv_kk")[:, p2:p2 + 1], None, ALU.mult)
            link(dve, "dve", ins)
        dve.tensor_tensor(khT, kkT, kkT, ALU.mult).then_inc(S("rk_sq"), 1)
        link(dve, "dve", dve.tensor_scalar(vc("one_less_ka"), vc("rwkv_ka"), -1.0, 1.0, ALU.mult, ALU.add))
        dve.wait_ge(S("rk_norm"), 1)
        link(dve, "dve", dve.tensor_scalar(khT, khT, 1e-12, None, ALU.max))
        link(dve, "dve", dve.reciprocal(khT, khT))
        link(dve, "dve", dve.tensor_tensor(kkT, kkT, khT, ALU.mult))

    def order8(dr):
        g = list(range(8)) if dr == 0 else [3, 2, 1, 0, 7, 6, 5, 4]
        return [divmod(c, 2) for c in g]

    def rwkv_pe(pe, dr):
        r64 = slice(64 * dr, 64 * dr + 64)
        if dr == 0:
            pe.wait_ge(S("rk_tanh"), 1)
        for t in range(TILES):
            ins = pe.matmul(bank(t // 2, 256, (t % 2) * 256), rk[r64, 6, t * P:(t + 1) * P], mats[r64, 0, :],
                            start=True, stop=True)
        ins.then_inc(S("rk_z"), 1)
        for p2 in range(2):
            ins = pe.matmul(bank(2 + p2), mats[r64, 1, p2 * P:(p2 + 1) * P], rk[r64, 7, :], start=True, stop=True)
        ins.then_inc(S("rk_za"), 1)
        pe.wait_ge(S("rk_lw"), dr + 1)
        lead, n_lead = names[f"rk_tail{dr}"][0], 4
        for p2 in range(2):
            for kind, b in (("inc", 4), ("exc", 0)):
                for t in range(TILES):
                    ins = pe.matmul(bank(b + p2, P, t * P), lw[:, t, p2 * P:(p2 + 1) * P], C(f"rk_{kind}{dr}"),
                                    start=True, stop=True)
            for t in range(TILES):
                ins = pe.matmul(bank(6, 4, (p2 * TILES + t) * 4), lw[:, t, p2 * P:(p2 + 1) * P],
                                cst[:, lead:lead + 4], start=True, stop=True)
        ins.then_inc(S("rk_c"), 1)
        pe.wait_ge(S("rk_bk"), dr + 1)
        for n, (src, b) in enumerate(((bT, 0), (kT2, 2))):
            for t in range(TILES):
                for j in range(2):
                    ins = pe.transpose(bank(b + t // 2, P, (t % 2) * 256 + j * P), src[:, j, t * P:(t + 1) * P], ident)
            ins.then_inc(S("rk_turn"), 1)
        pe.wait_ge(S("rk_turned"), 2 * dr + 2)
        q = 0
        for t in range(TILES):
            kinds = ("b", "k") + (("rb", "rk") if t >= 2 else ())
            for kind in kinds:
                m = 12 * dr + q
                if m % 12 >= 2 or dr:
                    pe.wait_ge(S("rk_A_out"), m - 1)
                for h in range(4):
                    r, p2 = slice(64 * (h % 2), 64 * (h % 2) + 64), h // 2
                    lhs = (bT if kind in ("b", "rb") else kT2)[r, p2, t * P:(t + 1) * P]
                    rhs = khT[r, p2, t * P:(t + 1) * P] if kind in ("b", "k") else rhT[r, p2, (t - 2) * P:(t - 1) * P]
                    ins = pe.matmul(bank((4, 0)[q % 2] + h % 2, P, (h // 2) * P), lhs, rhs, start=True, stop=True)
                ins.then_inc(S("rk_A"), 1)
                q += 1
                if kind in ("k", "rk"):
                    if kind == "k" and 4 * dr + t:
                        pe.wait_ge(S("rk_w1"), 4 * dr + t)
                    pe.wait_ge(S("rk_A_out"), m + 1)
                    for h in range(4):
                        if kind == "k":
                            o, start, stop = bank(6, 64, h * 64), True, True
                        else:
                            o = bank(7, 64, (t - 2) * 256 + h * 64)
                            start, stop = dr == 0 and t == 2 and h == 0, False
                        ins = pe.matmul(o, akm[:, h, :], v_t[:, t, h * 64:(h + 1) * 64], start=start, stop=stop,
                                        skip_group_check=True)
                    ins.then_inc(S("rk_AV"), 1)
        for n in range(6):
            for t in range(TILES):
                m = 24 * dr + 4 * n + t
                pe.wait_ge(S("rk_L"), m + 1)
                pe.wait_ge(S("rk_T"), 28 * dr + 4 * n + t + 1)
                if m % 24 >= 2 or dr:
                    pe.wait_ge(S("rk_X"), m - 1)
                for h in range(4):
                    ins = pe.matmul(bank(t % 2, P, h * P), lmask[:, t % 2, h, :], tf[:, t, h, :], start=True, stop=True)
                ins.then_inc(S("rk_Xp"), 1)
                if t >= 1:
                    rwkv_double(pe, dr, n, t - 1)
            rwkv_double(pe, dr, n, 3)
        for k, (t, c) in enumerate(order8(dr)):
            m = 8 * dr + k
            rows = slice(64 * c, 64 * c + 64)
            pe.wait_ge(S("rk_T"), 28 * dr + 28)
            pe.wait_ge(S("rk_state"), 9 * dr + k + 1)
            for p2 in range(2):
                ins = pe.matmul(bank(0, P, p2 * P), khT[:, p2, t * P:(t + 1) * P], st[:, p2, :], start=True, stop=True)
            ins.then_inc(S("rk_ks"), 1)
            if t >= 2:
                for p2 in range(2):
                    ins = pe.matmul(psum[rows, 7, (t - 2) * 256 + p2 * P:(t - 2) * 256 + (p2 + 1) * P],
                                    rhT[:, p2, (t - 2) * P + 64 * c:(t - 2) * P + 64 * c + 64], st[:, p2, :],
                                    start=False, stop=False, skip_group_check=True)
                ins.then_inc(S("rk_rs"), 1)
            last = k == 7
            if not last:
                for p2 in range(2):
                    pe.matmul(bank(2, P, p2 * P), ktok[rows, t, p2 * P:(p2 + 1) * P], v_t[rows, t, p2 * P:(p2 + 1) * P],
                              start=p2 == 0, stop=False, skip_group_check=True)
            pe.wait_ge(S("rk_r"), m + 1)
            for h in range(4):
                ins = pe.matmul(bank(1, 64, h * 64), tt[rows, t, h, :], ur[rows, h * 64:(h + 1) * 64], start=True,
                                stop=True)
            ins.then_inc(S("rk_u"), 1)
            pe.wait_ge(S("rk_uu"), m + 1)
            if not last:
                for p2 in range(2):
                    ins = pe.matmul(bank(2, P, p2 * P), btok[rows, t, p2 * P:(p2 + 1) * P],
                                    uu[rows, t, p2 * P:(p2 + 1) * P], start=False, stop=p2 == 1, skip_group_check=True)
                ins.then_inc(S("rk_add"), 1)
            if t >= 2 and k in (5, 7):
                for h in range(4):
                    ins = pe.matmul(bank(7, 64, (t - 2) * 256 + h * 64), arb[:, t - 2, h, :],
                                    uu[:, t, h * 64:(h + 1) * 64], start=False, stop=dr == 1 and k == 7,
                                    skip_group_check=True)
                ins.then_inc(S("rk_y"), 1)
        if dr == 1:
            for t in range(NT):
                for p2 in range(2):
                    ins = pe.matmul(bank(3, 2, t * 4 + p2 * 2), bonusT[:, p2, t * P:(t + 1) * P], C("head_cols"),
                                    start=True, stop=True)
            ins.then_inc(S("rk_bon"), 1)

    def rwkv_double(pe, dr, n, t):
        m = 24 * dr + 4 * n + t
        pe.wait_ge(S("rk_X"), m + 1)
        if m % 24 >= 2 or dr:
            pe.wait_ge(S("rk_T"), 28 * dr + (4 if m % 24 else 0) + max(m % 24 - 1, 0))
        for h in range(4):
            ins = pe.matmul(bank(2 + t % 2, P, h * P), xf[:, t % 2, h, :], tt[:, t, h, :], start=True, stop=True)
        if n < 5:
            for h in range(4):
                ins = pe.matmul(bank(4 + t % 2, P, h * P), tt[:, t, h, :], xf[:, t % 2, h, :], start=True, stop=True)
        ins.then_inc(S("rk_dT"), 1)

    def rwkv_act(act, dr):
        if dr == 0:
            act.wait_ge(S("rk_tri_free"), 1)
        act.dma_start(tri2.rearrange("p a b -> p (a b)"), d["tri_masks"][:, dr * 9 * P:(dr + 1) * 9 * P]
                      ).then_inc(S("rk_tri"), 16)
        act.wait_ge(S("rk_zb"), dr + 1)
        act.activation(lw, lw, ACT.Sigmoid).then_inc(S("rk_lw"), 1)
        act.wait_ge(S("rk_za"), dr + 1)
        for p2 in range(2):
            ins = act.activation(aTt[:, p2, :], bank(2 + p2), ACT.Sigmoid, bias=vc("rwkv_a0")[:, 2 * dr + p2:2 * dr + p2 + 1])
        ins.then_inc(S("rk_a"), 1)
        act.wait_ge(S("rk_c"), dr + 1)
        act.activation(dcol.rearrange("p a b c -> p (a b c)"), bank(6, 32), ACT.Exp, scale=-KAPPA).then_inc(S("rk_E"), 1)
        act.activation(khT, psum[:, 0:2, :], ACT.Exp, scale=-KAPPA).then_inc(S("rk_E"), 1)
        act.activation(rhT, psum[:, 4:6, CTX:ALL], ACT.Exp, scale=-KAPPA).then_inc(S("rk_E"), 1)
        act.activation(ex, psum[:, 4:6, :], ACT.Exp, scale=KAPPA).then_inc(S("rk_E"), 1)
        for n, (dst, b) in enumerate(((btok, 0), (ktok, 2))):
            act.wait_ge(S("rk_turn"), 2 * dr + n + 1)
            act.activation(dst, psum[:, b:b + 2, :].rearrange("p b (t c) -> p (b t) c", t=2), ACT.Copy
                           ).then_inc(S("rk_turned"), 1)
        done = 6 * dr
        for t in range(TILES):
            done += 1
            act.wait_ge(S("rk_AV"), done)
            act.activation(w1[:, t, :], bank(6, 256), ACT.Copy).then_inc(S("rk_w1"), 1)
            if t >= 2:
                done += 1
        for n in range(6):
            for t in range(TILES):
                m = 24 * dr + 4 * n + t
                act.wait_ge(S("rk_Xp"), m + 1)
                if m >= 2:
                    act.wait_ge(S("rk_dT"), m - 1)
                act.activation(xf[:, t % 2, :, :], bank(t % 2).rearrange("p (h i) -> p h i", h=4), ACT.Copy
                               ).then_inc(S("rk_X"), 1)

    def rwkv_pool(pool, dr):
        pool.wait_ge(S("rk_tri"), 16 * (dr + 1))
        for n in range(6):
            for t in range(TILES):
                m = 24 * dr + 4 * n + t
                pool.wait_ge(S("rk_ab"), 4 * dr + t + 1)
                if m >= 2:
                    pool.wait_ge(S("rk_Xp"), m - 1)
                pool.tensor_tensor(lmask[:, t % 2, :, :], ab[:, t, :, :], bc(tri2[:, 3 + n, :], 1, 4), ALU.mult
                                   ).then_inc(S("rk_L"), 1)

    def rwkv_dve(dve, dr):
        if dr == 0:
            dve.memset(bon, 0.0).then_inc(S("rk_tri_free"), 1)
        dve.wait_ge(S("rk_z"), dr + 1)
        dve.tensor_tensor(lw, psum[:, 0:2, :].rearrange("p b (t c) -> p (b t) c", t=2),
                          bc(vr("rwkv_w0")[:, dr * 256:dr * 256 + 256], 1, TILES), ALU.add).then_inc(S("rk_zb"), 1)
        dve.wait_ge(S("rk_a"), dr + 1)
        dve.wait_ge(S("rk_E"), 4 * dr + 4)
        link(dve, "dve", dve.tensor_tensor(khT, khT, kkT, ALU.mult))
        link(dve, "dve", dve.tensor_tensor(rhT, rhT, rk[:, 0:2, CTX:ALL], ALU.mult))
        for p2 in range(2):
            link(dve, "dve", dve.tensor_scalar(kT2[:, p2, :], aTt[:, p2, :], vc("rwkv_ka")[:, p2:p2 + 1],
                                               vc("one_less_ka")[:, p2:p2 + 1], ALU.mult, ALU.add))
        link(dve, "dve", dve.tensor_tensor(kT2, kT2, rk[:, 2:4, :], ALU.mult))
        if dr == 0:
            link(dve, "dve", dve.tensor_copy(bonusT, kT2[:, :, CTX:ALL]))
        else:
            link(dve, "dve", dve.tensor_tensor(bonusT, bonusT, kT2[:, :, CTX:ALL], ALU.add))
            for p2 in range(2):
                link(dve, "dve", dve.scalar_tensor_tensor(bonusT[:, p2, :], bonusT[:, p2, :], vc("rwkv_rk")[:, p2:p2 + 1],
                                                          rk[:, p2, CTX:ALL], ALU.mult, ALU.mult))
        link(dve, "dve", dve.tensor_tensor(bT, kkT, aTt, ALU.mult))
        link(dve, "dve", dve.tensor_tensor(kT2, kT2, ex, ALU.mult))
        dve.tensor_tensor(bT, bT, ex, ALU.mult).then_inc(S("rk_bk"), 1)
        for k, ((t, c), (t2, c2)) in enumerate(zip(order8(dr)[:-1], order8(dr)[1:])):
            ins = dve.tensor_tensor(dec[:, :, k:k + 1], dcol[:, :, t, c:c + 1], dcol[:, :, t2, 2 + c2:3 + c2], ALU.mult)
        link(dve, "dve", ins)
        link(dve, "dve", dve.memset(uu, 0.0))
        dve.wait_ge(S("rk_tri"), 16 * (dr + 1))
        q = 0
        av = 6 * dr
        for t in range(TILES):
            for kind in ("b", "k") + (("rb", "rk") if t >= 2 else ()):
                dve.wait_ge(S("rk_A"), 12 * dr + q + 1)
                b0 = (4, 0)[q % 2]
                src = psum[:, b0:b0 + 2, 0:SEQ].rearrange("p b (a i) -> p a b i", a=2)
                dst, mask = {"b": (ab[:, t, :, :], 2), "k": (akm, 2), "rb": (arb[:, max(t - 2, 0), :, :], 1),
                             "rk": (akm, 1)}[kind]
                if kind in ("k", "rk"):
                    if av:
                        dve.wait_ge(S("rk_AV"), av)
                    av += 1
                dve.tensor_tensor(dst.rearrange("p (a b) i -> p a b i", a=2), src,
                                  bc(bc(tri2[:, mask, :], 1, 2), 1, 2), ALU.mult).then_inc(S("rk_A_out"), 1)
                if kind == "b":
                    dve.wait_ge(S("rk_A_out"), 12 * dr + q + 1)
                    dve.tensor_copy(tt[:, t, :, :], bc(ident, 1, 4)).then_inc(S("rk_ab"), 1)
                q += 1
        dve.wait_ge(S("rk_A"), 12 * dr + 12)
        for t in range(TILES):
            dve.tensor_copy(tf[:, t, :, :], bc(ident, 1, 4)).then_inc(S("rk_T"), 1)
        for n in range(6):
            for t in range(TILES):
                m = 24 * dr + 4 * n + t
                dve.wait_ge(S("rk_dT"), m + 1)
                o = tt[:, t, :, :]
                if n == 5:
                    dve.tensor_tensor(o, o, bank(2 + t % 2).rearrange("p (h i) -> p h i", h=4), ALU.subtract
                                      ).then_inc(S("rk_T"), 1)
                else:
                    dve.tensor_tensor(o, o, bank(2 + t % 2).rearrange("p (h i) -> p h i", h=4), ALU.subtract)
                    o = tf[:, t, :, :]
                    dve.tensor_tensor(o, o, bank(4 + t % 2).rearrange("p (h i) -> p h i", h=4), ALU.subtract
                                      ).then_inc(S("rk_T"), 1)
        dve.wait_ge(S("rk_w1"), 4 * dr + 4)
        dve.memset(st, 0.0).then_inc(S("rk_state"), 1)
        for k, (t, c) in enumerate(order8(dr)):
            m = 8 * dr + k
            rows = slice(64 * c, 64 * c + 64)
            dve.wait_ge(S("rk_ks"), m + 1)
            dve.tensor_tensor(ur[rows, :], psum[rows, 0, 0:256], w1[rows, t, :], ALU.add).then_inc(S("rk_r"), 1)
            dve.wait_ge(S("rk_u"), m + 1)
            dve.tensor_scalar(uu[rows, t, :], psum[rows, 1, 0:256], -1.0, None, ALU.mult).then_inc(S("rk_uu"), 1)
            if k < 7:
                dve.wait_ge(S("rk_add"), 7 * dr + k + 1)
                if t >= 2:
                    dve.wait_ge(S("rk_rs"), 4 * dr + k - 3)
                for hf in range(2):
                    r = slice(64 * hf, 64 * hf + 64)
                    s3 = st[r, :, 64 * hf:64 * hf + 64]
                    link(dve, "dve", dve.tensor_tensor(s3, s3, psum[r, 2, 0:256].rearrange("p (a b) -> p a b", a=2)[
                        :, :, 64 * hf:64 * hf + 64], ALU.add))
                    ins = dve.tensor_tensor(s3, s3, bc(dec[r, :, k:k + 1].rearrange("p a k -> p (a k)"), 2, 64), ALU.mult)
                ins.then_inc(S("rk_state"), 1)
            else:
                dve.memset(ur[:, 0:1], 0.0).then_inc(S("rk_state"), 1)

    def rwkv_end_act(act):
        act.wait_ge(S("group_sums"), 3)
        act.activation(stat[:, 1, 0:8], stat[:, 2, 0:8], ACT.Sqrt, scale=1 / 64, bias=lnx_eps).then_inc(S("group_root"), 1)

    def rwkv_end_dve(dve):
        dve.wait_ge(S("rk_y"), 4)
        dve.wait_ge(S("rk_bon"), 1)
        y4 = yk.rearrange("p t (h e) -> p (t h) e", h=4)
        link(dve, "dve", dve.tensor_copy(yk, bank(7).rearrange("p (t c) -> p t c", t=NT)))
        link(dve, "dve", dve.tensor_reduce(stat[:, 0, 0:8], y4, X, ALU.add))
        link(dve, "dve", dve.tensor_scalar(stat[:, 0, 0:8], stat[:, 0, 0:8], -1 / 64, None, ALU.mult))
        link(dve, "dve", dve.tensor_tensor(y4, y4, bc(stat[:, 0, 0:8], 2, 64), ALU.add))
        link(dve, "dve", dve.tensor_tensor(yk2, yk, yk, ALU.mult))
        dve.tensor_reduce(stat[:, 2, 0:8], yk2.rearrange("p t (h e) -> p (t h) e", h=4), X, ALU.add
                          ).then_inc(S("group_sums"), 1)
        dve.wait_ge(S("group_root"), 3)
        link(dve, "dve", dve.reciprocal(stat[:, 3, 0:8], stat[:, 1, 0:8]))
        link(dve, "dve", dve.tensor_tensor(y4, y4, bc(stat[:, 3, 0:8], 2, 64), ALU.mult))
        link(dve, "dve", dve.tensor_tensor(yk, yk, bc(vr("lnx_w"), 1, NT), ALU.mult))
        link(dve, "dve", dve.tensor_tensor(yk, yk, bc(vr("lnx_b"), 1, NT), ALU.add))
        link(dve, "dve", dve.tensor_copy(bon, bank(3, 8).rearrange("p (t h) -> p t h", t=NT)))
        for t in range(NT):
            link(dve, "dve", dve.tensor_tensor(yk2[:, t, :].rearrange("p (h e) -> p h e", h=4),
                                               v_t[:, 2 + t, :].rearrange("p (h e) -> p h e", h=4),
                                               bc(bon[:, t, :], 2, 64), ALU.mult))
        link(dve, "dve", dve.tensor_tensor(yk, yk, yk2, ALU.add))
        link(dve, "dve", dve.tensor_tensor(y_mix[:, :, 512:768], yk, rk_g, ALU.mult))

    top[0] = stage_top - 9 * ALL
    ln_w = alloc(D)
    ln_b = alloc(D)
    router_w = alloc(KC, EXPERTS)
    scores = alloc(NT, EXPERTS)
    sel = alloc(NT, EXPERTS)
    picked = alloc(NT, EXPERTS)
    g8 = alloc(NT, EGROUPS, 8)
    gs = alloc(NT, EGROUPS)
    gr = alloc(NT, 64)
    g_eq = alloc(NT, 64)
    g_in = alloc(NT, EGROUPS)
    g_out = alloc(NT, EGROUPS)
    t8 = alloc(NT, 8)
    w_sum = alloc(NT)
    gate = alloc(NT, EXPERTS + 1)
    gate_diag = alloc(SEQ)

    MOE = W_OUT + 4

    def ln_load(act, k):
        for dst, n in ((ln_w, f"ln{k + 1}_w_2"), (ln_b, f"ln{k + 1}_b_2")):
            act.dma_start(dst, d[n].to_broadcast([P, D])).then_inc(S("ln_rows"), 16)

    def out_ln_act(act, k):
        act.wait_ge(S("row_var"), k + 1)
        act.activation(stat[:, 1, 0:NT], stat[:, 0, 0:2 * NT].rearrange("p (t s) -> p t s", s=2)[:, :, 1], ACT.Sqrt,
                       bias=ln_eps).then_inc(S("row_root"), 1)

    def out_ln_dve(dve, k, g_b):
        for t in range(NT):
            link(dve, "dve", dve.tensor_tensor(xn[:, t, :], banks(4 + 2 * t, 2), g_b, ALU.mult))
            link(dve, "dve", dve.scalar_tensor_tensor(xn[:, t, :], x_tok[:, t, :], DN_ALPHA, xn[:, t, :], ALU.mult,
                                                      ALU.add))
            for h in range(2):
                link(dve, "dve", dve.bn_stats(stat[:, 2, 12 * t + 6 * h:12 * t + 6 * h + 6],
                                              xn[:, t, 512 * h:512 * h + 512]))
        link(dve, "dve", dve.bn_aggr(stat[:, 0, 0:2], stat[:, 2, 0:12]))
        dve.bn_aggr(stat[:, 0, 2:4], stat[:, 2, 12:24]).then_inc(S("row_var"), 1)
        dve.wait_ge(S("row_root"), k + 1)
        link(dve, "dve", dve.reciprocal(stat[:, 3, 0:NT], stat[:, 1, 0:NT]))
        dve.wait_ge(S("ln_rows"), 32 * (k + 1))
        for t in range(NT):
            x = x_tok[:, t, :]
            link(dve, "dve", dve.tensor_scalar(x, xn[:, t, :], stat[:, 0, 2 * t:2 * t + 1], stat[:, 3, t:t + 1],
                                               ALU.subtract, ALU.mult))
            link(dve, "dve", dve.tensor_tensor(x, x, ln_w, ALU.mult))
            ins = dve.tensor_tensor(x, x, ln_b, ALU.add)
            link(dve, "dve", ins)

    def router_pe(pe):
        pe.wait_ge(S("norm_T"), KC * 7)
        pe.wait_ge(S("router_in"), 16)
        for t in range(NT):
            for c in range(KC):
                ins = pe.matmul(bank(3, EXPERTS, t * EXPERTS), aT[:, c, t * P:(t + 1) * P], router_w[:, c, :],
                                start=c == 0, stop=c == KC - 1)
        ins.then_inc(S("routed"), 1)

    def router_act(act):
        act.wait_ge(S("routed"), 1)
        act.activation(scores, bank(3, NT * EXPERTS).rearrange("p (t e) -> p t e", t=NT), ACT.Sigmoid
                       ).then_inc(S("router_scores"), 1)

    def router_dve(dve):
        link(dve, "dve", dve.memset(gate, 0.0))
        dve.wait_ge(S("router_scores"), 1)
        link(dve, "dve", dve.tensor_tensor(sel, scores, bc(vr("router_b"), 1, NT), ALU.add))
        for t in range(NT):
            for g in range(EGROUPS):
                ins = dve.max(g8[:, t, g, :], sel[:, t, 8 * g:8 * g + 8])
        link(dve, "dve", ins)
        link(dve, "dve", dve.tensor_tensor(gs, g8[:, :, :, 0], g8[:, :, :, 1], ALU.add))
        for t in range(NT):
            other, own = bc(gs[:, t, :], 1, 8), bc(gs[:, t, :], 2, 8)
            r3, e3 = (a[:, t, :].rearrange("p (g o) -> p g o", g=8) for a in (gr, g_eq))
            link(dve, "dve", dve.tensor_tensor(r3, other, own, ALU.is_gt))
            link(dve, "dve", dve.tensor_tensor(e3, other, own, ALU.is_equal))
            link(dve, "dve", dve.tensor_tensor(g_eq[:, t, :], g_eq[:, t, :], C("below8"), ALU.mult))
            link(dve, "dve", dve.tensor_tensor(gr[:, t, :], gr[:, t, :], g_eq[:, t, :], ALU.add))
            link(dve, "dve", dve.tensor_reduce(g_in[:, t, :], r3, X, ALU.add))
            link(dve, "dve", dve.tensor_scalar(g_in[:, t, :], g_in[:, t, :], TOP_GROUPS - 0.5, None, ALU.is_lt))
            link(dve, "dve", dve.tensor_scalar(g_out[:, t, :], g_in[:, t, :], -1.0, 1e30, ALU.add, ALU.mult))
            s3 = sel[:, t, :].rearrange("p (g o) -> p g o", g=8)
            link(dve, "dve", dve.tensor_tensor(s3, s3, bc(g_in[:, t, :], 2, 8), ALU.mult))
            link(dve, "dve", dve.tensor_tensor(s3, s3, bc(g_out[:, t, :], 2, 8), ALU.add))
            link(dve, "dve", dve.max(t8[:, t, :], sel[:, t, :]))
            link(dve, "dve", dve.match_replace(picked[:, t, :], t8[:, t, :], sel[:, t, :], -3e38))
            link(dve, "dve", dve.tensor_tensor(picked[:, t, :], picked[:, t, :], sel[:, t, :], ALU.not_equal))
            link(dve, "dve", dve.tensor_tensor(picked[:, t, :], picked[:, t, :], scores[:, t, :], ALU.mult))
            link(dve, "dve", dve.tensor_reduce(w_sum[:, t:t + 1], picked[:, t, :], X, ALU.add))
            link(dve, "dve", dve.reciprocal(w_sum[:, t:t + 1], w_sum[:, t:t + 1]))
            link(dve, "dve", dve.tensor_scalar(gate[:, t, 0:EXPERTS], picked[:, t, :], w_sum[:, t:t + 1], ROUTED_SCALE,
                                               ALU.mult, ALU.mult))

    def moe_sp(sp):
        def up(e):
            if isinstance(e, int) and e == 0:
                return [d[n][0].rearrange("(p c) n -> p c n", p=P) for n in ("sh_w1_2", "sh_w3_2")]
            return [d[n][0, bass.ds(e - 1, 1)].rearrange("e (p c) n -> (e p) c n", p=P) for n in ("exp_w1_2", "exp_w3_2")]

        def down(e):
            if isinstance(e, int) and e == 0:
                return d["sh_w2_2"][0].rearrange("(p c) n -> p c n", p=P)
            return d["exp_w2_2"][0, bass.ds(e - 1, 1)].rearrange("e (p c) n -> (e p) c n", p=P)

        experts_sp(sp, EXPERTS + 1, up, down)

    def block2_sp(sp):
        mix_in_sp(sp)
        for i in range(4):
            load(sp, cols(d["w_out_2"][0], 256 * i), KC, 256)
        moe_sp(sp)

    def block2_pe(pe):
        mod_pe(pe)
        fence(pe, "mod")
        norm_pe(pe, NT)
        norm_pe(pe, NT)
        mix_in_pe(pe)
        fence(pe, "mix_in")
        mod2_pe(pe)
        fence(pe, "mix_conv")
        gla_pe(pe)
        fence(pe, "gla_done")
        ssd_pe(pe)
        fence(pe, "ssd_done")
        rwkv_once_pe(pe)
        fence(pe, "rwkv_once")
        rwkv_pe(pe, 0)
        fence(pe, "rwkv_fwd")
        rwkv_pe(pe, 1)
        fence(pe, "rwkv_bwd")
        wo_pe(pe, 2)
        fence(pe, "mix_out")
        norm_pe(pe, NT)
        router_pe(pe)
        experts_pe(pe, "moe", EXPERTS + 1, True)
        fence(pe, "moe_out")

    def block2_act(act):
        act.wait_ge(S("mod_in"), 16 * 8)
        fence(act, "mod")
        act.dma_start(ctx_tok, d["ctx_2"][0].rearrange("(t p) c -> p t c", p=P)).then_inc(S("stage_in"), 16)
        norm_act(act, ctx_tok, NT, "ln", uT[:, :, 0:CTX], modT[:, 1, 1, :], modT[:, 0, 1, :])
        norm_act(act, x_tok, NT, "ln", uT[:, :, CTX:ALL], modT[:, 1, 0, :], modT[:, 0, 0, :])
        mix_move(act, 0)
        fence(act, "mix_in")
        conv_act(act)
        fence(act, "mix_conv")
        gla_act(act)
        fence(act, "gla_done")
        ssd_act(act)
        fence(act, "ssd_done")
        rwkv_once_act(act)
        fence(act, "rwkv_once")
        rwkv_act(act, 0)
        fence(act, "rwkv_fwd")
        rwkv_act(act, 1)
        rwkv_end_act(act)
        fence(act, "rwkv_bwd")
        ln_load(act, 0)
        act.dma_start(router_w, d["router_w_2"][0].rearrange("(p c) e -> p c e", p=P)).then_inc(S("router_in"), 16)
        wo_act(act, 2)
        out_ln_act(act, 0)
        fence(act, "mix_out")
        ln_load(act, 1)
        norm_act(act, x_tok, NT, "ln", aT, modT[:, 4, 0, :], modT[:, 3, 0, :], MOE)
        router_act(act)
        experts_act(act, "moe", EXPERTS + 1, MOE)
        out_ln_act(act, 1)
        fence(act, "moe_out")

    def block2_dve(dve):
        mod_dve(dve)
        fence(dve, "mod")
        dve.wait_ge(S("stage_in"), 16 * 3)
        norm_dve(dve, ctx_tok, NT, "ln")
        norm_dve(dve, x_tok, NT, "ln")
        mix_move(dve, 1)
        fence(dve, "mix_in")
        conv_dve(dve)
        mod2_dve(dve)
        fence(dve, "mix_conv")
        gla_dve(dve)
        fence(dve, "gla_done")
        ssd_dve(dve)
        fence(dve, "ssd_done")
        rwkv_once_dve(dve)
        fence(dve, "rwkv_once")
        rwkv_dve(dve, 0)
        fence(dve, "rwkv_fwd")
        rwkv_dve(dve, 1)
        rwkv_end_dve(dve)
        fence(dve, "rwkv_bwd")
        wo_dve(dve, 2)
        dve.wait_ge(S("item_used"), MOE)
        out_ln_dve(dve, 0, g1_b)
        fence(dve, "mix_out")
        norm_dve(dve, x_tok, NT, "ln", MOE)
        experts_dve(dve, "moe", EXPERTS + 1, MOE, True, first_gates=router_dve)
        dve.wait_ge(S("item_used"), MOE + 3 * (EXPERTS + 1))
        out_ln_dve(dve, 1, g2_b)
        fence(dve, "moe_out")

    def block2_pool(pool):
        for n in FENCES[6:]:
            if n == "mix_in":
                mod2_pool(pool)
            if n == "gla_done":
                gla_pool(pool)
            if n == "rwkv_fwd":
                rwkv_pool(pool, 0)
            if n == "rwkv_bwd":
                rwkv_pool(pool, 1)
            fence(pool, n)

    with ctx:
        block = ctx.enter_context(nc.Block())

        @block.sync
        def _(sp):
            block1_sp(sp)
            block2_sp(sp)
            sp.wait_ge(S("fence"), 4 * len(FENCES))
            sp.dma_start(out.rearrange("a (t p) c -> p (a t) c", p=P), x_tok).then_inc(S("stored"), 16)
            sp.wait_ge(S("stored"), 16)

        @block.tensor
        def _(pe):
            block1_pe(pe)
            block2_pe(pe)

        @block.scalar
        def _(act):
            block1_act(act)
            block2_act(act)

        @block.vector
        def _(dve):
            block1_dve(dve)
            block2_dve(dve)

        @block.gpsimd
        def _(pool):
            block1_pool(pool)
            block2_pool(pool)


_INS = """x norm_mix_pre norm_mix_post norm_ffn_pre norm_ffn_post na_w_qkv na_w_o na_rpb
dil_w_qkv dil_w_o ffn_w_gate ffn_w_up ffn_w_down c_2 ctx_2 c_ctx_2 ada_w_2 ada_b_2 w_in_2 w_out_2
ln1_w_2 ln1_b_2 ln2_w_2 ln2_b_2 router_w_2 exp_w1_2 exp_w3_2 exp_w2_2 sh_w1_2 sh_w3_2 sh_w2_2""".split()


def packed(v):
    def col(name):
        a = v[name + "_2"][0]
        return a.reshape(-1, a.shape[-1] // P, P).transpose(2, 0, 1).reshape(P, -1)

    cols_ = {"conv_w": col("ssd_conv_w"), "conv_b": col("ssd_conv_b"), "mu": col("rwkv_mu"), "rwkv_a0": col("rwkv_a0"),
             "rwkv_kk": col("rwkv_kk"), "rwkv_ka": col("rwkv_ka"),
             "rwkv_rk": v["rwkv_rk_2"][0].reshape(2, P).T, "one_less_ka": np.zeros((P, 2), np.float32)}
    rows_ = {"rwkv_w0": "rwkv_w0", "dt_bias": "ssd_dt_bias", "a_log": "ssd_a_log", "ssd_d": "ssd_d",
             "ssd_norm_w": "ssd_norm_w", "lnx_w": "rwkv_lnx_w", "lnx_b": "rwkv_lnx_b", "gla_gb": "gla_gb",
             "gla_norm_w": "gla_norm_w", "router_b": "router_b"}
    rows_ = {k: v[n + "_2"][0].reshape(1, -1) for k, n in rows_.items()}
    m = np.zeros((P, 4, 256), np.float32)
    m[:, 0] = v["rwkv_w2_2"][0].reshape(P, 256)
    m[:, 1] = v["rwkv_a2_2"][0].reshape(P, 256)
    m[:, 2] = v["rwkv_g2_2"][0]
    gu = v["gla_gu_2"][0]
    m[0:16, 3, 0:128], m[16:32, 3, 128:256] = gu[0], gu[1]
    for table, parts in ((VCOL, cols_), (VROW, rows_)):
        off = 0
        for k, a in parts.items():
            assert table[k] == (off, a.shape[1]), (k, off, a.shape)
            off += a.shape[1]
    return {"vcol": np.concatenate(list(cols_.values()), 1), "vrow": np.concatenate(list(rows_.values()), 1),
            "mats": m.reshape(P, -1)}


def kernel(**inputs):
    import numpy as _np
    import concourse.bacc as _bacc
    from concourse import mybir as _mybir
    from concourse.bass_utils import run_bass_kernel_spmd as _run

    nc = _bacc.Bacc("TRN2", target_bir_lowering=False, num_devices=1)
    names, consts = constants()
    given = {n: _np.asarray(a) for n, a in inputs.items()}
    arrays, aps = {}, {}
    for name, a in [(n, given[n]) for n in _INS] + list(packed(given).items()) + list(consts.items()):
        a = _np.ascontiguousarray(a)
        arrays[f"in_{name}_dram"] = a
        aps[name] = nc.dram_tensor(f"in_{name}_dram", a.shape, _mybir.dt.from_np(a.dtype), kind="ExternalInput").ap()
    out = nc.dram_tensor("out_0_dram", (1, SEQ, D), F32, kind="ExternalOutput").ap()
    program(nc, aps, out, names)
    r = _run(nc, [arrays], core_ids=[0])
    return r.results[0]["out_0_dram"]
```
